# Optimizing a Trainium2 kernel written in Bass

```python
import jax, jax.numpy as jnp
from jax import lax
import numpy as np

D_MODEL = 1024
BATCH = 1
SEQ = 1024
DEPTH = 1

GRID_W = 64
MIX_WIDTH = D_MODEL
NA_HEADS = 8
NA_HEAD_DIM = 64
NA_WIDTH = NA_HEADS * NA_HEAD_DIM
NA_WIN_R = 8
NA_WIN_C = 16
NA_QCB = 16
NA_KCB = 32
NA_NCB = GRID_W // NA_QCB
HG_HEADS = 4
HG_DK = 128
HG_DV = 128
HG_FDIM = HG_HEADS * HG_DK
HG_WIDTH = HG_HEADS * HG_DV
HG_CHUNK = 64
D_FF = 4 * D_MODEL
RMS_EPS = 1e-6
SPLIT_SIZES = (NA_WIDTH, NA_WIDTH, NA_WIDTH, HG_FDIM, HG_FDIM, HG_FDIM, HG_WIDTH, HG_WIDTH)
D_IN_PROJ = 3 * NA_WIDTH + 3 * HG_FDIM + 2 * HG_WIDTH

kernel_name = "hybrid_natten_hgrn2_encoder_block"

def _rmsnorm(x, w):
    xf = x.astype(jnp.float32)
    y = xf * lax.rsqrt(jnp.mean(xf * xf, axis=-1, keepdims=True) + RMS_EPS)
    return (y * w.astype(jnp.float32)).astype(x.dtype)

def _neighbourhood_attention(qa, ka, va, qn_w, kn_w, rpb, rows):
    B, S, _ = qa.shape
    wr = min(NA_WIN_R, rows)

    def to_grid(t, w):
        t = _rmsnorm(t.reshape(B, S, NA_HEADS, NA_HEAD_DIM).astype(jnp.float32), w) if w is not None \
            else t.reshape(B, S, NA_HEADS, NA_HEAD_DIM).astype(jnp.float32)
        return t.reshape(B, rows, GRID_W, NA_HEADS, NA_HEAD_DIM).transpose(0, 3, 1, 2, 4)

    q = to_grid(qa, qn_w)
    k = to_grid(ka, kn_w)
    v = to_grid(va, None)

    qcol = np.arange(GRID_W).reshape(NA_NCB, NA_QCB)
    band_start = np.clip(np.arange(NA_NCB) * NA_QCB - NA_WIN_C // 2, 0, GRID_W - NA_KCB)
    band_cols = band_start[:, None] + np.arange(NA_KCB)[None, :]
    col_start = np.clip(qcol - NA_WIN_C // 2, 0, GRID_W - NA_WIN_C)
    kc = band_cols[:, None, :]
    col_mask = (kc >= col_start[..., None]) & (kc < col_start[..., None] + NA_WIN_C)
    col_idx = np.clip(kc - qcol[..., None] + NA_WIN_C - 1, 0, 2 * NA_WIN_C - 2)

    k_band = k[:, :, :, band_cols]
    v_band = v[:, :, :, band_cols]
    q_blk = jnp.moveaxis(q.reshape(B, NA_HEADS, rows, NA_NCB, NA_QCB, NA_HEAD_DIM), 2, 0)
    rpb_cols = rpb.astype(jnp.float32)[:, :, col_idx]
    mask = jnp.asarray(col_mask)[:, :, None, :]
    scale = NA_HEAD_DIM ** -0.5

    def row_block(inp):
        r, q_r = inp
        start = jnp.clip(r - wr // 2, 0, rows - wr)
        k_r = lax.dynamic_slice_in_dim(k_band, start, wr, axis=2)
        v_r = lax.dynamic_slice_in_dim(v_band, start, wr, axis=2)
        s = jnp.einsum('bhnqd,bhrnkd->bhnqrk', q_r, k_r) * scale
        ridx = start + jnp.arange(wr, dtype=jnp.int32) - r + NA_WIN_R - 1
        bias = jnp.transpose(rpb_cols[:, ridx], (0, 2, 3, 1, 4))
        s = jnp.where(mask, s + bias, -jnp.inf)
        p = jax.nn.softmax(s, axis=(-2, -1))
        return jnp.einsum('bhnqrk,bhrnkd->bhnqd', p, v_r)

    o = lax.map(row_block, (jnp.arange(rows, dtype=jnp.int32), q_blk))
    o = jnp.moveaxis(o, 0, 2).reshape(B, NA_HEADS, S, NA_HEAD_DIM)
    return o.transpose(0, 2, 1, 3).reshape(B, S, NA_WIDTH)

def _gla_chunk_scan(q, k, log_f, v):
    B, H, S, dk = q.shape
    dv = v.shape[-1]
    n = S // HG_CHUNK

    def chunks(t):
        return jnp.moveaxis(t.reshape(B, H, n, HG_CHUNK, t.shape[-1]), 2, 0)

    qc, kc, vc = chunks(q), chunks(k), chunks(v)
    bc = jnp.cumsum(chunks(log_f), axis=3)
    incl = jnp.tril(jnp.ones((HG_CHUNK, HG_CHUNK), dtype=bool))

    def step(state, inp):
        qi, ki, bi, vi = inp
        o_inter = jnp.einsum('bhid,bhdv->bhiv', qi * jnp.exp(bi), state)
        diff = bi[:, :, :, None, :] - bi[:, :, None, :, :]
        decay = jnp.exp(jnp.where(incl[:, :, None], diff, -jnp.inf))
        a = jnp.einsum('bhid,bhjd,bhijd->bhij', qi, ki, decay)
        o = o_inter + jnp.einsum('bhij,bhjv->bhiv', a, vi)
        b_last = bi[:, :, -1:, :]
        state = jnp.exp(b_last[:, :, 0, :])[..., None] * state + \
            jnp.einsum('bhjd,bhjv->bhdv', ki * jnp.exp(b_last - bi), vi)
        return state, o

    s0 = jnp.zeros((B, H, dk, dv), jnp.float32)
    _, o = lax.scan(step, s0, (qc, kc, bc, vc))
    return jnp.moveaxis(o, 0, 2).reshape(B, H, S, dv)

def _hgrn2_bidirectional(hq, hf_fwd, hf_bwd, hi, hg, lb_f, lb_b, gnorm_w):
    B, S, _ = hq.shape

    def heads(t, d):
        return t.reshape(B, S, HG_HEADS, d).transpose(0, 2, 1, 3)

    q = heads(hq.astype(jnp.float32), HG_DK)
    v = heads(hi.astype(jnp.float32), HG_DV)

    def gate(hf, lb):
        f = lb + (1.0 - lb) * jax.nn.sigmoid(hf.astype(jnp.float32))
        return heads(1.0 - f, HG_DK), heads(jnp.log(f), HG_DK)

    k_f, lf_f = gate(hf_fwd, lb_f)
    k_b, lf_b = gate(hf_bwd, lb_b)
    o_fwd = _gla_chunk_scan(q, k_f, lf_f, v)
    flip = lambda t: jnp.flip(t, axis=2)
    o_bwd = flip(_gla_chunk_scan(flip(q), flip(k_b), flip(lf_b), flip(v)))
    o = (o_fwd + o_bwd).transpose(0, 2, 1, 3)
    g = hg.astype(jnp.float32).reshape(B, S, HG_HEADS, HG_DV)
    o = _rmsnorm(o, gnorm_w) * jax.nn.silu(g)
    return o.reshape(B, S, HG_WIDTH)

def setup_inputs(seed: int = 0) -> dict:
    key = jax.random.key(seed)
    ks = jax.random.split(key, 14)
    f32 = jnp.float32
    nrm = lambda k, shape, s: jax.random.normal(k, shape, f32) * s
    return {
        "x": jax.random.normal(ks[0], (BATCH, SEQ, D_MODEL), f32),
        "w_in": nrm(ks[1], (DEPTH, D_MODEL, D_IN_PROJ), D_MODEL ** -0.5),
        "w_out": nrm(ks[2], (DEPTH, MIX_WIDTH, D_MODEL), MIX_WIDTH ** -0.5),
        "attn_norm_w": 1.0 + nrm(ks[3], (DEPTH, D_MODEL), 0.02),
        "mlp_norm_w": 1.0 + nrm(ks[4], (DEPTH, D_MODEL), 0.02),
        "q_norm_w": 1.0 + nrm(ks[5], (DEPTH, NA_HEAD_DIM), 0.02),
        "k_norm_w": 1.0 + nrm(ks[6], (DEPTH, NA_HEAD_DIM), 0.02),
        "rpb": nrm(ks[7], (DEPTH, NA_HEADS, 2 * NA_WIN_R - 1, 2 * NA_WIN_C - 1), 0.02),
        "hg_norm_w": 1.0 + nrm(ks[8], (DEPTH, HG_DV), 0.02),
        "lb_fwd": 1.0 + nrm(ks[9], (DEPTH + 1, HG_FDIM), 0.1),
        "lb_bwd": 1.0 + nrm(ks[10], (DEPTH + 1, HG_FDIM), 0.1),
        "w_up": nrm(ks[11], (DEPTH, D_MODEL, D_FF), D_MODEL ** -0.5),
        "w_down": nrm(ks[12], (DEPTH, D_FF, D_MODEL), D_FF ** -0.5),
    }

def reference(x, w_in, w_out, attn_norm_w, mlp_norm_w, q_norm_w, k_norm_w, rpb,
              hg_norm_w, lb_fwd, lb_bwd, w_up, w_down):
    B, S, D = x.shape
    rows = S // GRID_W
    split_idx = [int(i) for i in np.cumsum(SPLIT_SIZES)[:-1]]
    lbf_all = jnp.cumsum(jax.nn.softmax(lb_fwd.astype(jnp.float32), axis=0), axis=0)
    lbb_all = jnp.cumsum(jax.nn.softmax(lb_bwd.astype(jnp.float32), axis=0), axis=0)
    h = x
    for layer in range(DEPTH):
        u = _rmsnorm(h, attn_norm_w[layer])
        proj = jnp.einsum('bsd,de->bse', u, w_in[layer])
        qa, ka, va, hq, hff, hfb, hi, hg = jnp.split(proj, split_idx, axis=-1)
        y_na = _neighbourhood_attention(qa, ka, va, q_norm_w[layer], k_norm_w[layer], rpb[layer], rows)
        y_hg = _hgrn2_bidirectional(hq, hff, hfb, hi, hg, lbf_all[layer], lbb_all[layer], hg_norm_w[layer])
        mix = jnp.concatenate([y_na, y_hg], axis=-1).astype(h.dtype)
        h = h + jnp.einsum('bse,ed->bsd', mix, w_out[layer])
        u = _rmsnorm(h, mlp_norm_w[layer])
        a = jnp.square(jax.nn.relu(jnp.einsum('bsd,df->bsf', u, w_up[layer])))
        h = h + jnp.einsum('bsf,fd->bsd', a, w_down[layer])
    return h


_drawn_inputs = setup_inputs


def setup_inputs(seed=0):
    import zlib

    import numpy as np

    out = dict(_drawn_inputs(seed))
    spreads = {}
    factors = {'attn_norm_w': 3.204,
     'mlp_norm_w': 10.432,
     'q_norm_w': 8.0,
     'k_norm_w': 8.0,
     'rpb': 64.0,
     'hg_norm_w': 6.439}
    for name, (base, spread) in spreads.items():
        noise = np.random.default_rng([zlib.crc32(name.encode()), seed]).standard_normal(out[name].shape)
        drawn = base * np.exp(spread * noise) if base else spread * noise
        out[name] = __import__('jax').numpy.asarray(drawn.astype(out[name].dtype))
    for name, factor in factors.items():
        out[name] = (out[name] * factor).astype(out[name].dtype)
    return out
```

```python
from contextlib import ExitStack

import numpy as np
import concourse.bass as bass
from concourse import mybir

F32 = mybir.dt.float32
F32R = mybir.dt.float32r
U8 = mybir.dt.uint8
I32 = mybir.dt.int32
ALU = mybir.AluOpType
ACT = mybir.ActivationFunctionType

P = 128
D = 1024
S = 1024
KT = D // P
TT = S // P
HALF = 512
NA_HEADS, NA_DIM = 8, 64
PAIRS = NA_HEADS // 2
GRID = 64
NG, NB = 4, 4
BAND = 32
BAND_START = [0, 8, 24, 32]
BAND_CLASS = [0, 1, 1, 2]
CLASS_SHIFT = [0, -8, -16]
KEY_ROW0 = [0, 0, 4, 8]
KEY_ROWS = [8, 12, 12, 8]
MASK_ROW0 = [4, 0, 0, 0]
TILE_W = [r * BAND for r in KEY_ROWS]
TILE_OFF = [0, 256, 640, 1024]
STEP_W = 1280
KG_GROUPS = [(0, 1), (0, 1, 2), (1, 2, 3), (2, 3)]
KG0 = [0, 0, 1, 2]
STEPS = PAIRS * NB
BIAS_ROWS = 28
BIAS_OFF = [0, 8 * BAND, 8 * BAND, 20 * BAND]
RPB_PITCH = 64
HG_HEADS = 4
CHUNK = 128
NCH = S // CHUNK
LEVELS = [128, 64, 32, 16]
NLEV = 7
EPS = 1e-6
BIG = 1e30
LOG_F_MIN = -18.0
SIG_MAX = 1e18
RING, STAGE = 4, 2
FBLK = 2
MLP_BLOCKS = 4 * D // P // FBLK
OUT_BLOCKS = KT // FBLK
C_Q, C_K, C_V, C_HQ, C_FF, C_FB, C_HV, C_HG = [512 * i for i in range(8)]
M_HG, M_NA, M_SCAN = 0, NLEV * P, NLEV * P + 3 * BIAS_ROWS * BAND
M_END = M_SCAN + S + 4


def shape_tables():
    f = np.zeros((P, 3 * P), np.float32)
    f[:, 0:P] = np.eye(P)
    for h in range(2):
        f[64 * h:64 * h + 64, P + 64 * h:P + 64 * h + 64] = 1.0 / 64
    f[:, 2 * P:] = 1.0 / P
    m = np.zeros((P, M_END), np.uint8)
    j, i = np.arange(P)[:, None], np.arange(P)[None, :]
    for n, b in enumerate(LEVELS):
        m[:, n * P:(n + 1) * P] = (j // b == i // b) & (j // (b // 2) != i // (b // 2))
    m[:, 4 * P:5 * P] = (j // 8 == i // 8) & (j < i)
    m[:, 5 * P:6 * P] = (j // 8 == i // 8) & (j > i)
    m[:, 6 * P:7 * P] = j == i
    p = np.arange(P)
    rr, c = (p % 64 // 16)[:, None, None], (p % 16)[:, None, None]
    col = np.arange(BAND)[None, None, :]
    for k, n in enumerate([0, 1, 3]):
        first = np.clip(16 * n + c - 8, 0, GRID - 16) - BAND_START[n]
        out_col = (col < first) | (col >= first + 16)
        u = np.arange(12)[None, :, None]
        row_in = (u - rr >= 0) & (u - rr <= 7)
        parts = [np.broadcast_to(out_col, (P, 8, BAND)), out_col | ~row_in,
                 np.broadcast_to(out_col, (P, 8, BAND))]
        at = M_NA + k * BIAS_ROWS * BAND
        m[:, at:at + BIAS_ROWS * BAND] = np.concatenate(parts, axis=1).reshape(P, -1)
    m[:, M_SCAN:] = (np.arange(S + 4) % CHUNK != 0)[None, :]
    return f, m.view(np.int32)


def weight_tiles():
    order = [("in", C_V + P * c) for c in range(4)]
    for p in range(PAIRS):
        order += [("in", C_Q + P * p), ("in", C_K + P * p)]
    order += [("in", C_HV + P * c) for c in range(4)]
    order += [("in", C_FF), ("in", C_FB), ("in", C_HQ)]
    for h in range(HG_HEADS):
        order += [("in", C_HG + P * h)]
        if h + 1 < HG_HEADS:
            order += [("in", c + P * (h + 1)) for c in (C_FF, C_FB, C_HQ)]
    order += [("out", k) for k in range(KT)]
    return order


TILES = weight_tiles()
N_IN = 32
N_TILES = len(TILES) + 2 * 4 * D // P


def proj_units():
    u = [("v", c, t) for c in range(2) for t in range(TT)]
    for p in range(PAIRS):
        u += [("q", p, 0), ("q", p, 1), ("k", p, 0), ("k", p, 1)]
    u += [("hv", c, t) for c in range(2) for t in range(TT)]
    for h in range(HG_HEADS):
        if h == 0:
            u += [(k, 0, i) for k in ("ff", "fb", "hq") for i in range(2)]
        u += [("hg", h, i) for i in range(2)]
        if h + 1 < HG_HEADS:
            u += [(k, h + 1, i) for k in ("ff", "fb", "hq") for i in range(2)]
    return u


UNITS = proj_units()
UNIT = {u: n for n, u in enumerate(UNITS)}
TILE_OF = {("in", c): n for n, (k, c) in enumerate(TILES) if k == "in"}
COL = {"q": C_Q, "k": C_K, "ff": C_FF, "fb": C_FB, "hq": C_HQ, "hg": C_HG}

BEFORE = 16 + 6
STEP_UNITS = {s: [BEFORE + 1 + s] for s in range(-1, 9)}
STEP_UNITS.update({s: [] for s in range(9, STEPS)})
FIRST_HEAD = list(range(BEFORE + 10, UNIT[("hg", 0, 0)]))
PIECES = 9
HEAD_UNITS = []
for _h in range(HG_HEADS):
    _units = [UNIT[("hg", _h, i)] for i in range(2)]
    if _h + 1 < HG_HEADS:
        _units += [UNIT[(k, _h + 1, i)] for k in ("ff", "fb", "hq") for i in range(2)]
    HEAD_UNITS.append([[_u] for _u in _units] + [[]] * (PIECES - len(_units)))
BY_ACT = ("hv", "ff", "fb", "hq")


ARG_OF = {0: 0, 1: 1, 2: 2, 3: 3, 4: 4, 5: 5, 7: 6}
ARGS = len(ARG_OF)


def bank_uses(n, by_act):
    return sum((UNITS[i][0] in BY_ACT) == by_act for i in range(n + 1))


def hybrid_block(nc, x, w_in, w_out, attn_norm_w, mlp_norm_w, q_norm_w, k_norm_w, rpb, hg_norm_w,
                 lb_fwd, lb_bwd, w_up, w_down, tables, masks, out):
    ctx = ExitStack()
    with ctx:
        def sem(name):
            return ctx.enter_context(nc.semaphore(name))

        at = [int(nc.sbuf_base) + 31 & ~31]

        def place(name, shape, dt, size=4):
            t = nc.alloc_sbuf_tensor_at(name, shape, dt, offset=at[0])
            at[0] += int(np.prod(shape[1:])) * size + 31 & ~31
            return t

        uT_hi = place("uT_hi", [P, KT, S], F32R)
        uT_lo = place("uT_lo", [P, KT, S], F32R)
        w_hi = place("w_hi", [P, RING, 1024], F32R)
        w_lo = place("w_lo", [P, RING, 1024], F32R)
        stage = place("stage", [P, STAGE, 1024], F32)
        tab = place("tab", [P, 3 * P], F32)
        hg_mask = place("hg_mask", [P, NLEV, P], U8, 1)
        scan_mask = place("scan_mask", [P, S + 4], U8, 1)
        norm_w = place("norm_w", [P, 2, KT], F32)
        qk_w = place("qk_w", [P, 2], F32)
        gnorm = place("gnorm", [P, 1], F32)
        lb_raw = place("lb_raw", [P, 2, 2, HG_HEADS], F32)
        lb = place("lb", [P, 2, HG_HEADS], F32)
        lb_rest = place("lb_rest", [P, 2, HG_HEADS], F32)
        lb_neg = place("lb_neg", [P, 2, HG_HEADS], F32)
        ssq = place("ssq", [P, 2, TT], F32)
        rstd = place("rstd", [P, 2, TT], F32)
        s_min = place("s_min", [P, STEPS * NG], F32)
        s_sum = place("s_sum", [P, STEPS * NG], F32)
        s_inv = place("s_inv", [P, STEPS * NG], F32)
        g_chunk = place("g_chunk", [P, 2, NCH], F32)
        eps_col = place("eps_col", [P, 1], F32)
        one_col = place("one_col", [P, 1], F32)
        work = at[0]
        ident, head_mean, all_mean = tab[:, 0:P], tab[:, P:2 * P], tab[:, 2 * P:3 * P]

        q_hi = place("q_hi", [P, 2, NG, NB, P], F32R)
        q_lo = place("q_lo", [P, 2, NG, NB, P], F32R)
        k_hi = place("k_hi", [P, 2, S], F32R)
        k_lo = place("k_lo", [P, 2, S], F32R)
        v_hi = place("v_hi", [P, 2, NG, P], F32R)
        v_lo = place("v_lo", [P, 2, NG, P], F32R)
        probs = place("probs", [P, 2, STEP_W], F32)
        pT_hi = place("pT_hi", [P, 2, 384], F32R)
        pT_lo = place("pT_lo", [P, 2, 384], F32R)
        bias = place("bias", [P, BIAS_ROWS, BAND], F32)
        rpb_win = place("rpb_win", [P, 12 * RPB_PITCH], F32)
        na_mask = place("na_mask", [P, 3, BIAS_ROWS, BAND], U8, 1)
        qk_t = place("qk_t", [P, 3, HALF], F32)
        mix_hi = place("mix_hi", [P, S], F32R)
        mix_lo = place("mix_lo", [P, S], F32R)
        end_attention = at[0]
        vs = nc.alloc_sbuf_tensor_at("vs", [P, 2, 2, 256], F32, offset=end_attention - 8192)
        x_tok = nc.alloc_sbuf_tensor_at("x_tok", [P, TT, D], F32, offset=work)

        at[0] = work
        zz = place("zz", [P, 2, 2, S], F32)
        k_tok = place("k_tok", [P, S], F32)
        state = place("state", [P, 2, NCH - 1, P], F32)
        scores = place("scores", [P, NCH, P], F32)
        tmp = place("tmp", [P, 2, HALF], F32)
        gate_t = place("gate_t", [P, HALF], F32)
        h_cum = place("h_cum", [P, 2, 2, S], F32)
        h_key = place("h_key", [P, 2, 2, S], F32)
        h_q = place("h_q", [P, 2, S], F32)
        h_gate = place("h_gate", [P, S], F32)
        h_v = place("h_v", [P, TT, 512], F32)
        end_hgrn = at[0]

        at[0] = work
        resid = place("resid", [P, TT, D], F32)
        act_hi = place("act_hi", [P, 2, FBLK, S], F32R)
        act_lo = place("act_lo", [P, 2, FBLK, S], F32R)
        u_tok = place("u_tok", [P, TT, D], F32)
        end_mlp = at[0]
        assert max(end_attention, end_hgrn, end_mlp) <= int(nc.sbuf_usable_end), (
            end_attention, end_hgrn, end_mlp, int(nc.sbuf_usable_end))

        bank = [ctx.enter_context(nc.psum_tensor(f"bank{i}", [P, HALF], F32)) for i in range(8)]
        v_dram = [nc.dram_tensor(f"v_dram{i}", [S, 512], F32).ap() for i in range(2)]
        mix_dram = [nc.dram_tensor(f"mix_dram{i}", [S, S], F32).ap() for i in range(2)]

        c_load = sem("c_load")
        x_load = [sem(f"x_load{t}") for t in range(TT)]
        w_load = [sem(f"w_load{i}") for i in range(STAGE)]
        w_split = sem("w_split")
        w_used = sem("w_used")
        act_own = sem("act_own")
        dve_own = sem("dve_own")
        sq_done = sem("sq_done")
        u_ready = sem("u_ready")
        uT_done = sem("uT_done")
        uT_act = sem("uT_act")
        uT_dve = sem("uT_dve")
        proj_done = sem("proj_done")
        act_freed = sem("act_freed")
        dve_freed = sem("dve_freed")
        unit_act = sem("unit_act")
        unit_dve = sem("unit_dve")
        qk_sq = sem("qk_sq")
        qk_mean = sem("qk_mean")
        qk_ready = sem("qk_ready")
        v_stored = [sem(f"v_stored{i}") for i in range(2)]
        v_load = [sem(f"v_load{i}") for i in range(2)]
        rpb_load = sem("rpb_load")
        bias_done = sem("bias_done")
        score_done = sem("score_done")
        masked = sem("masked")
        exp_done = sem("exp_done")
        prob_done = sem("prob_done")
        pT_done = sem("pT_done")
        pT_act = sem("pT_act")
        pT_dve = sem("pT_dve")
        pv_done = sem("pv_done")
        mix_act = sem("mix_act")
        mix_dve = sem("mix_dve")
        mix_store = [sem(f"mix_store{i}") for i in range(2)]
        z_arg = sem("z_arg")
        z_exp = sem("z_exp")
        z_ready = sem("z_ready")
        lev_done = sem("lev_done")
        lev_taken = sem("lev_taken")
        kT_done = sem("kT_done")
        kT_act = sem("kT_act")
        g_ready = sem("g_ready")
        upd_done = sem("upd_done")
        st_done = sem("st_done")
        o_done = sem("o_done")
        o_sq = sem("o_sq")
        o_mean = sem("o_mean")
        o_rs = sem("o_rs")
        o_norm = sem("o_norm")
        y_act = sem("y_act")
        y_dve = sem("y_dve")
        act_load = [sem(f"act_load{i}") for i in range(2)]
        down_done = sem("down_done")
        added = sem("added")
        up_done = sem("up_done")
        relu_done = sem("relu_done")
        sqr_done = sem("sqr_done")
        a_hi = sem("a_hi")
        a_lo = sem("a_lo")
        out_store = sem("out_store")
        mask_load = sem("mask_load")
        resid_load = sem("resid_load")
        ready_cols = sem("ready_cols")
        lb_exp = sem("lb_exp")
        lb_diff = sem("lb_diff")
        params = sem("params")
        cleared = sem("cleared")

        def z_turn(h, i):
            return (h * PIECES + i) % 2

        CONSTS = 16 * 12
        FIRST_QK = UNIT[("q", 0, 0)]
        heads = (slice(0, 64), slice(64, 128))

        def freed(n):
            by_act = UNITS[n][0] in BY_ACT
            return (act_freed if by_act else dve_freed), bank_uses(n, by_act)

        def act_hands(n):
            return sum({"v": 1, "q": 2, "k": 2, "ff": 1, "fb": 1, "hg": 2}.get(UNITS[i][0], 0) for i in range(n))

        def dve_hands(n):
            return sum({"ff": 2, "fb": 2, "hg": 1}.get(UNITS[i][0], 0) for i in range(n))

        def gate_t_free(eng, n):
            before = [i for i in range(n) if UNITS[i][0] in ("ff", "fb", "hg")]
            if before and UNITS[before[-1]][0] == "hg":
                eng.wait_ge(*freed(before[-1]))
            elif before:
                eng.wait_ge(unit_dve, dve_hands(n))

        def operands_free(eng, h, i):
            n = h * PIECES + i - 2
            if n < 0:
                return
            hh, j = divmod(n, PIECES)
            if j < NLEV:
                eng.wait_ge(lev_done, 2 * (NLEV * hh + j + 1))
            elif j == 7:
                eng.wait_ge(kT_done, 4 * (hh + 1))
            else:
                eng.wait_ge(o_done, 2 * (hh + 1))

        def hgrn_may_start(eng):
            eng.wait_ge(mix_store[0], 32 * PAIRS)
            eng.wait_ge(pv_done, NG * STEPS)

        def after(h, i):
            return (h, i + 1) if i + 1 < PIECES else (h + 1, 0)

        def q_place(t, p, g, h):
            return t[heads[h], p % 2, g, :, 64 * h:64 * h + 64].rearrange("p n (r c) -> p r n c", c=16)

        def q_source(g2, h):
            return qk_t[heads[h], 2, 256 * g2:256 * g2 + 256].rearrange("p (r n c) -> p r n c", n=NB, c=16)

        def mix_place(t, n, h):
            return t[heads[h], :].rearrange("p (g r n c) -> p g r n c", g=NG, r=4, n=NB)[:, :, :, n, :]

        def mix_source(h):
            return bank[6][heads[h], :].rearrange("p (g h r c) -> p g h r c", g=NG, h=2, r=4)[:, :, h, :, :]

        block = ctx.enter_context(nc.Block())

        @block.sync
        def _(sp):
            x_v = x.rearrange("b (t p) d -> p (b t) d", p=P)
            for t in range(TT):
                sp.dma_start(x_tok[:, t, :], x_v[:, t, :]).then_inc(x_load[t], 16)
                if t == 3:
                    sp.dma_start(tab[:, :], tables).then_inc(c_load, 16)
            with nc.allow_non_contiguous_dma(reason="small parameter vectors"):
                sp.dma_start(norm_w[:, 0, :], attn_norm_w.rearrange("o (k p) -> p (o k)", p=P)).then_inc(c_load, 16)
                sp.dma_start(norm_w[:, 1, :], mlp_norm_w.rearrange("o (k p) -> p (o k)", p=P)).then_inc(c_load, 16)
                for h in heads:
                    sp.dma_start(qk_w[h, 0:1], q_norm_w.rearrange("o d -> d o")).then_inc(c_load, 16)
                    sp.dma_start(qk_w[h, 1:2], k_norm_w.rearrange("o d -> d o")).then_inc(c_load, 16)
                sp.dma_start(gnorm[:, :], hg_norm_w.rearrange("o d -> d o")).then_inc(c_load, 16)
                for i, src in enumerate((lb_fwd, lb_bwd)):
                    for r in range(2):
                        sp.dma_start(lb_raw[:, i, r, :], src[r].rearrange("(h d) -> d h", d=P)).then_inc(c_load, 16)

            w_in_v = w_in.rearrange("o (k p) n -> p (o k) n", p=P)
            w_up_v = w_up.rearrange("o (k p) n -> p (o k) n", p=P)
            w_out_v = w_out.rearrange("o (k p) n -> k p (o n)", p=P)
            w_down_v = w_down.rearrange("o (k p) n -> k p (o n)", p=P)
            for n, (kind, where) in enumerate(TILES):
                if n >= STAGE:
                    sp.wait_ge(w_split, 2 * (n - STAGE + 1))
                dst = stage[:, n % STAGE, :]
                if kind == "in":
                    sp.dma_start(dst.rearrange("p (k c) -> p k c", k=KT),
                                 w_in_v[:, :, where:where + P]).then_inc(w_load[n % STAGE], 16)
                else:
                    sp.dma_start(dst, w_out_v[where]).then_inc(w_load[n % STAGE], 16)

            with sp.Fori(0, MLP_BLOCKS, 1) as b:
                for i in range(2 * FBLK):
                    sp.wait_ge(w_split, b * (4 * FBLK) + 2 * (len(TILES) + i - STAGE + 1))
                    dst = stage[:, i % STAGE, :]
                    if i < FBLK:
                        src = w_up_v[:, :, bass.ds(b * (FBLK * P) + i * P, P)]
                        sp.dma_start(dst.rearrange("p (k c) -> p k c", k=KT), src).then_inc(w_load[i % STAGE], 16)
                    else:
                        src = w_down.rearrange("o f n -> (o f) n")[bass.ds(b * (FBLK * P) + (i - FBLK) * P, P), :]
                        sp.dma_start(dst, src).then_inc(w_load[i % STAGE], 16)

            for t in range(TT):
                sp.wait_ge(added, 16 * (OUT_BLOCKS + MLP_BLOCKS - 1) + 2 * t + 2)
                sp.dma_start(out.rearrange("b (t p) d -> p (b t) d", p=P)[:, t, :], resid[:, t, :]).then_inc(out_store, 16)
            sp.wait_ge(out_store, 16 * TT)
            sp.wait_ge(v_stored[0], 32 * 8)
            sp.wait_ge(v_stored[1], 32 * 8)
            sp.wait_ge(mix_store[0], 32 * PAIRS)
            sp.wait_ge(mix_store[1], 64 * HG_HEADS)

        @block.gpsimd
        def _(pool):
            def split(i, loaded, used, turn):
                pool.wait_ge(w_load[i % STAGE], loaded)
                if used is not None:
                    pool.wait_ge(w_used, used)
                pool.tensor_tensor(w_hi[:, i, :], stage[:, i % STAGE, :],
                                   one_col[:, 0:1].to_broadcast([P, 1024]), ALU.mult).then_inc(w_split, 1)
                pool.wait_ge(w_split, turn + 1)
                pool.tensor_tensor(w_lo[:, i, :], stage[:, i % STAGE, :], w_hi[:, i, :].bitcast(F32),
                                   ALU.subtract).then_inc(w_split, 1)

            pool.wait_ge(ready_cols, 2)
            for i in range(RING):
                split(i, 16 * (i // STAGE + 1), None, 2 * i)
            with pool.Fori(1, N_TILES // RING, 1) as r:
                for i in range(RING):
                    split(i, r * (16 * RING // STAGE) + 16 * (i // STAGE + 1),
                          r * RING + (i + 1 - RING), r * (2 * RING) + 2 * i)

        @block.scalar
        def _(act):
            own = [0]

            def step(ins):
                ins.then_inc(act_own, 1)
                own[0] += 1
                act.wait_ge(act_own, own[0])

            def load_bias_window(p):
                if p >= 1:
                    act.wait_ge(bias_done, 3 * p)
                for h in range(2):
                    for r in range(4):
                        src = rpb[2 * p + h, :, 3 - r:15 - r, :].rearrange("c r v -> c (r v)")
                        act.dma_start(rpb_win[64 * h + 16 * r:64 * h + 16 * r + 16, :], src).then_inc(rpb_load, 16)

            def load_band(s):
                p, n = divmod(s, NB)
                if s >= 2:
                    act.wait_ge(pv_done, NG * (s - 1))
                for i, dst in enumerate((v_hi, v_lo)):
                    for r in range(4):
                        src = v_dram[i].rearrange("(g r c) e -> r c g e", r=4, c=GRID)[
                            r, BAND_START[n]:BAND_START[n] + BAND, :, P * p:P * p + P]
                        act.dma_start(dst[32 * r:32 * r + 32, s % 2, :, :].bitcast(F32), src).then_inc(v_load[s % 2], 16)

            def rms(norm, t):
                if norm == 0:
                    src, scratch = x_tok, vs[:, :, :, :].rearrange("p a b c -> p (a b c)")
                else:
                    src, scratch = resid, u_tok[:, t, :]
                step(act.activation(scratch, src[:, t, :], ACT.Square, accum_out=ssq[:, norm, t:t + 1]))
                step(act.activation(rstd[:, norm, t:t + 1], ssq[:, norm, t:t + 1], ACT.Ln,
                                    scale=1.0 / D, bias=eps_col[:, 0:1]))
                act.activation(rstd[:, norm, t:t + 1], rstd[:, norm, t:t + 1], ACT.Exp,
                               scale=-0.5).then_inc(sq_done, 1)

            def take_uT(norm, n):
                k, half = n % KT, n // KT
                act.wait_ge(uT_done, norm * 16 + n + 1)
                act.activation(uT_hi[:, k, half * HALF:half * HALF + HALF], bank[2 + n % 2][:, :], ACT.Copy,
                               scale=norm_w[:, norm, k:k + 1]).then_inc(uT_act, 1)

            def unit(n):
                kind, what, part = UNITS[n]
                b = bank[n % 2]
                cols = slice(part * HALF, part * HALF + HALF)
                act.wait_ge(proj_done, n + 1)
                if kind == "v":
                    if n >= 2:
                        act.wait_ge(v_stored[n % 2], 32 * (n // 2))
                    act.activation(vs[:, n % 2, 0, :].bitcast(F32R), b[:, 0:256], ACT.Copy).then_inc(unit_act, 1)
                    act.wait_ge(*freed(n))
                    for i in range(2):
                        act.dma_start(v_dram[i][P * part:P * part + P, 256 * what:256 * what + 256],
                                      vs[:, n % 2, i, :]).then_inc(v_stored[n % 2], 16)
                elif kind == "hv":
                    act.activation(h_v[:, part, 256 * what:256 * what + 256], b[:, 0:256], ACT.Copy).then_inc(act_freed, 1)
                elif kind == "hq":
                    if what >= 2:
                        act.wait_ge(z_ready, PIECES * (what - 1))
                        act.wait_ge(lev_done, 2 * NLEV * (what - 1))
                    act.activation(h_q[:, what % 2, cols], b[:, :], ACT.Copy).then_inc(act_freed, 1)
                elif kind in ("ff", "fb"):
                    d = ("ff", "fb").index(kind)
                    gate_t_free(act, n)
                    act.activation(gate_t[:, :], b[:, :], ACT.Exp, scale=-1.0).then_inc(act_freed, 1)
                    act.wait_ge(unit_dve, dve_hands(n) + 1)
                    step(act.activation(gate_t[:, :], gate_t[:, :], ACT.Ln, bias=one_col[:, 0:1]))
                    step(act.activation(gate_t[:, :], gate_t[:, :], ACT.Exp, scale=-1.0))
                    if what >= 2:
                        act.wait_ge(z_arg, ARGS * (what - 1))
                    act.activation(h_cum[:, what % 2, d, cols], gate_t[:, :], ACT.Ln,
                                   scale=lb_rest[:, d, what:what + 1], bias=lb[:, d, what:what + 1]).then_inc(unit_act, 1)
                elif kind == "hg":
                    gate_t_free(act, n)
                    act.activation(gate_t[:, :], b[:, :], ACT.Exp, scale=-1.0).then_inc(unit_act, 1)
                    act.wait_ge(unit_dve, dve_hands(n) + 1)
                    step(act.activation(gate_t[:, :], gate_t[:, :], ACT.Ln, bias=one_col[:, 0:1]))
                    act.activation(gate_t[:, :], gate_t[:, :], ACT.Exp, scale=-1.0).then_inc(unit_act, 1)

            def qk_square(n):
                act.wait_ge(proj_done, n + 1)
                if n > FIRST_QK:
                    act.wait_ge(qk_mean, n - FIRST_QK)
                act.activation(qk_t[:, 0, :], bank[n % 2][:, :], ACT.Square).then_inc(qk_sq, 1)

            def qk_rest(n):
                kind, p, part = UNITS[n]
                act.wait_ge(qk_mean, n - FIRST_QK + 1)
                if n > FIRST_QK:
                    act.wait_ge(*freed(n - 1))
                step(act.activation(qk_t[:, 1, :], bank[7][:, :], ACT.Ln, bias=eps_col[:, 0:1]))
                act.activation(qk_t[:, 1, :], qk_t[:, 1, :], ACT.Exp, scale=-0.5).then_inc(unit_act, 1)
                act.wait_ge(*freed(n))
                if p >= 2:
                    act.wait_ge(score_done, NG * NB * (p - 1))
                if kind == "k":
                    ins = act.activation(k_hi[:, p % 2, part * HALF:part * HALF + HALF], qk_t[:, 2, :], ACT.Copy)
                else:
                    if n == FIRST_QK:
                        act.wait_ge(cleared, 1)
                    for g2 in range(2):
                        for h in range(2):
                            ins = act.activation(q_place(q_hi, p, 2 * part + g2, h), q_source(g2, h), ACT.Copy)
                            if (g2, h) != (1, 1):
                                step(ins)
                ins.then_inc(unit_act, 1)

            def score_exp(s, g):
                i = NG * s + g
                t = probs[:, s % 2, TILE_OFF[g]:TILE_OFF[g] + TILE_W[g]]
                act.wait_ge(masked, i + 1)
                act.activation(t, t, ACT.Exp, scale=-1.0, bias=s_min[:, i:i + 1],
                               accum_out=s_sum[:, i:i + 1]).then_inc(exp_done, 1)

            def take_pT(s, kg):
                i = NG * s + kg
                w = P * len(KG_GROUPS[kg])
                act.wait_ge(pT_done, i + 1)
                if i >= 2:
                    act.wait_ge(pv_done, i - 1)
                act.activation(pT_hi[:, i % 2, 0:w], bank[4 + i % 2][:, 0:w], ACT.Copy).then_inc(pT_act, 1)

            def take_mix(s):
                p, n = divmod(s, NB)
                act.wait_ge(pv_done, NG * (s + 1))
                if n == 0 and p:
                    act.wait_ge(mix_store[0], 32 * p)
                step(act.activation(mix_place(mix_hi, n, 0), mix_source(0), ACT.Copy))
                act.activation(mix_place(mix_hi, n, 1), mix_source(1), ACT.Copy).then_inc(mix_act, 1)

            def store_mix(p):
                act.wait_ge(mix_act, NB * (p + 1))
                act.wait_ge(mix_dve, NB * (p + 1))
                act.dma_start(mix_dram[0][P * p:P * p + P, :], mix_hi[:, :].bitcast(F32)).then_inc(mix_store[0], 16)
                act.dma_start(mix_dram[1][P * p:P * p + P, :], mix_lo[:, :].bitcast(F32)).then_inc(mix_store[0], 16)

            def z_exponentials(h, i):
                if i == 6:
                    return
                t = z_turn(h, i)
                if i == 8:
                    operands_free(act, h, i)
                    act.activation(zz[:, t, :, :], h_cum[:, h % 2, :, :], ACT.Exp).then_inc(z_exp, 1)
                else:
                    act.wait_ge(z_arg, ARGS * h + ARG_OF[i] + 1)
                    act.activation(zz[:, t, :, :], zz[:, t, :, :], ACT.Exp).then_inc(z_exp, 1)

            def chunk_decays(h):
                act.wait_ge(z_arg, ARGS * h + 1)
                if h:
                    act.wait_ge(st_done, 4 * h)
                step(act.activation(g_chunk[:, 0, :], h_cum[:, h % 2, 0, CHUNK - 1::CHUNK], ACT.Exp))
                act.activation(g_chunk[:, 1, :], h_cum[:, h % 2, 1, 0::CHUNK], ACT.Exp).then_inc(g_ready, 1)

            def take_k_tok(h):
                for d in range(2):
                    for cg in range(2):
                        n = 4 * h + 2 * d + cg
                        act.wait_ge(kT_done, n + 1)
                        if cg == 0 and n:
                            act.wait_ge(upd_done, n)
                            if d == 0:
                                act.wait_ge(mix_store[1], 64 * h)
                        act.activation(k_tok[:, HALF * cg:HALF * cg + HALF], bank[4 + cg][:, :], ACT.Copy).then_inc(kT_act, 1)

            def head_output(h, part):
                n = 2 * h + part
                act.wait_ge(o_done, n + 1)
                if n:
                    act.wait_ge(y_dve, n)
                act.activation(tmp[:, 0, :], bank[6 + part][:, :], ACT.Square).then_inc(o_sq, 1)
                act.wait_ge(o_mean, n + 1)
                step(act.activation(tmp[:, 1, :], bank[4 + part][:, :], ACT.Ln, bias=eps_col[:, 0:1]))
                act.activation(tmp[:, 1, :], tmp[:, 1, :], ACT.Exp, scale=-0.5).then_inc(o_rs, 1)
                act.wait_ge(o_norm, 2 * n + 2)
                if part:
                    act.wait_ge(mix_store[1], 64 * h + 32)
                act.activation(k_tok[:, 0:HALF].bitcast(F32R), tmp[:, 0, :], ACT.Copy).then_inc(y_act, 1)
                act.wait_ge(y_dve, n + 1)
                for j in range(2):
                    act.dma_start(mix_dram[j][512 + P * h:512 + P * h + P, part * HALF:part * HALF + HALF],
                                  k_tok[:, HALF * j:HALF * j + HALF]).then_inc(mix_store[1], 16)

            act.preload_act_table_set("natural_log_exp_and_others")
            act.dma_start(na_mask[:, :, :, :].rearrange("p s r c -> p (s r c)").bitcast(I32), masks[:, M_NA // 4:M_SCAN // 4]).then_inc(mask_load, 16)
            act.dma_start(hg_mask[:, :, :].rearrange("p l i -> p (l i)").bitcast(I32), masks[:, M_HG // 4:M_NA // 4]).then_inc(mask_load, 16)
            act.dma_start(scan_mask[:, :].bitcast(I32), masks[:, M_SCAN // 4:M_END // 4]).then_inc(mask_load, 16)
            load_bias_window(0)
            act.wait_ge(ready_cols, 2)
            for half in range(2):
                for t in range(4 * half, 4 * half + 4):
                    act.wait_ge(x_load[t], 16)
                    rms(0, t)
                act.wait_ge(c_load, CONSTS)
                for n in range(KT * half, KT * half + KT):
                    take_uT(0, n)
            act.wait_ge(lb_diff, 1)
            act.activation(lb[:, :, :], lb[:, :, :], ACT.Exp).then_inc(lb_exp, 1)
            for n in range(FIRST_QK):
                unit(n)
            for i in range(2):
                act.wait_ge(v_stored[i], 32 * 8)
            load_band(0)
            load_band(1)
            for n in range(FIRST_QK, BEFORE - 1):
                qk_square(n)
                qk_rest(n)
            for s in range(-1, STEPS):
                if s <= 9:
                    qk_square(BEFORE + s)
                if s + 1 < STEPS:
                    for g in range(NG):
                        score_exp(s + 1, g)
                    if s >= 1:
                        load_band(s + 1)
                if s >= 0:
                    for kg in range(NG):
                        take_pT(s, kg)
                    take_mix(s)
                    if s % NB == NB - 1:
                        store_mix(s // NB)
                if s <= 9:
                    qk_rest(BEFORE + s)
                if (s + 2) % NB == 0 and 1 <= (s + 2) // NB < PAIRS:
                    load_bias_window((s + 2) // NB)
            hgrn_may_start(act)
            for n in FIRST_HEAD:
                unit(n)
            z_exponentials(0, 0)
            for h in range(HG_HEADS):
                for i in range(PIECES):
                    hh, j = after(h, i)
                    if hh < HG_HEADS:
                        z_exponentials(hh, j)
                    if i == 0:
                        chunk_decays(h)
                    if i == 7:
                        take_k_tok(h)
                    if i == 8:
                        for part in range(2):
                            head_output(h, part)
                    for n in HEAD_UNITS[h][i]:
                        unit(n)
            act.wait_ge(y_act, 2 * HG_HEADS)
            act.wait_ge(mix_store[0], 32 * PAIRS)
            act.wait_ge(mix_store[1], 64 * HG_HEADS)
            act.dma_start(resid[:, :, :], x.rearrange("b (t p) d -> p (b t) d", p=P)).then_inc(resid_load, 16)
            for b in range(OUT_BLOCKS):
                if b >= 2:
                    act.wait_ge(down_done, 16 * (b - 1))
                for j, dst in enumerate((act_hi, act_lo)):
                    act.dma_start(dst[:, b % 2, :, :].bitcast(F32), mix_dram[j][FBLK * P * b:FBLK * P * (b + 1), :]
                                  .rearrange("(f p) s -> p f s", p=P)).then_inc(act_load[b % 2], 16)
            for half in range(2):
                for t in range(4 * half, 4 * half + 4):
                    act.wait_ge(added, 16 * (OUT_BLOCKS - 1) + 2 * t + 2)
                    rms(1, t)
                for n in range(KT * half, KT * half + KT):
                    take_uT(1, n)
            with act.Fori(0, MLP_BLOCKS, 1) as b:
                for i in range(2 * FBLK):
                    f, half = divmod(i, 2)
                    act.wait_ge(up_done, b * 4 + (i + 1))
                    act.wait_ge(a_lo, b * 4 + i)
                    act.activation(u_tok[:, i, 0:HALF], bank[i][:, :], ACT.Relu).then_inc(relu_done, 1)
                    act.wait_ge(sqr_done, b * 4 + (i + 1))
                    act.wait_ge(down_done, b * 16 + 16 * OUT_BLOCKS)
                    act.activation(act_hi[:, 0, f, half * HALF:half * HALF + HALF], u_tok[:, i, HALF:D], ACT.Copy).then_inc(a_hi, 1)

        @block.vector
        def _(dve):
            own = [0]

            def step(ins):
                ins.then_inc(dve_own, 1)
                own[0] += 1
                dve.wait_ge(dve_own, own[0])

            def normalise_tokens(norm, t):
                src, dst = ((x_tok, x_tok), (resid, u_tok))[norm]
                dve.wait_ge(sq_done, TT * norm + t + 1)
                dve.tensor_scalar(dst[:, t, :], src[:, t, :], rstd[:, norm, t:t + 1], None, ALU.mult).then_inc(u_ready, 1)

            def take_uT(norm, n):
                k, half = n % KT, n // KT
                dve.wait_ge(uT_act, 16 * norm + n + 1)
                cols = slice(half * HALF, half * HALF + HALF)
                dve.scalar_tensor_tensor(uT_lo[:, k, cols], bank[2 + n % 2][:, :], norm_w[:, norm, k:k + 1],
                                         uT_hi[:, k, cols].bitcast(F32), ALU.mult, ALU.subtract).then_inc(uT_dve, 1)

            def unit(n):
                kind, what, part = UNITS[n]
                b = bank[n % 2]
                cols = slice(part * HALF, part * HALF + HALF)
                if kind == "v":
                    dve.wait_ge(unit_act, act_hands(n) + 1)
                    dve.tensor_tensor(vs[:, n % 2, 1, :].bitcast(F32R), b[:, 0:256], vs[:, n % 2, 0, :],
                                      ALU.subtract).then_inc(dve_freed, 1)
                elif kind in ("ff", "fb"):
                    d = ("ff", "fb").index(kind)
                    cum = h_cum[:, what % 2, d, cols]
                    dve.wait_ge(*freed(n))
                    dve.tensor_scalar(gate_t[:, :], gate_t[:, :], SIG_MAX, None, ALU.min).then_inc(unit_dve, 1)
                    dve.wait_ge(unit_act, act_hands(n) + 1)
                    step(dve.tensor_scalar(cum, cum, LOG_F_MIN, None, ALU.max))
                    dve.tensor_scalar(h_key[:, what % 2, d, cols], gate_t[:, :], lb_neg[:, d, what:what + 1],
                                      lb_rest[:, d, what:what + 1], ALU.mult, ALU.add).then_inc(unit_dve, 1)
                    if part == 1:
                        t = h_cum[:, what % 2, d, :]
                        if d == 0:
                            step(dve.tensor_tensor_scan(t, scan_mask[:, 0:S], t, 0.0, ALU.mult, ALU.add))
                        else:
                            step(dve.tensor_tensor_scan(t[:, ::-1], scan_mask[:, 1:S + 1][:, ::-1], t[:, ::-1], 0.0,
                                                        ALU.mult, ALU.add))
                elif kind == "hg":
                    dve.wait_ge(unit_act, act_hands(n) + 1)
                    dve.tensor_scalar(gate_t[:, :], gate_t[:, :], SIG_MAX, None, ALU.min).then_inc(unit_dve, 1)
                    dve.wait_ge(unit_act, act_hands(n) + 2)
                    dve.tensor_tensor(h_gate[:, cols], b[:, :], gate_t[:, :], ALU.mult).then_inc(dve_freed, 1)

            def qk_unit(n):
                kind, p, part = UNITS[n]
                c = "qk".index(kind)
                dve.wait_ge(unit_act, act_hands(n) + 1)
                dve.wait_ge(qk_ready, n - FIRST_QK)
                dve.scalar_tensor_tensor(qk_t[:, 2, :], bank[n % 2][:, :], qk_w[:, c:c + 1], qk_t[:, 1, :],
                                         ALU.mult, ALU.mult).then_inc(dve_freed, 1)
                dve.wait_ge(*freed(n))
                dve.wait_ge(unit_act, act_hands(n) + 2)
                if kind == "k":
                    cols = slice(part * HALF, part * HALF + HALF)
                    ins = dve.tensor_tensor(k_lo[:, p % 2, cols], qk_t[:, 2, :], k_hi[:, p % 2, cols].bitcast(F32),
                                            ALU.subtract)
                else:
                    for g2 in range(2):
                        for h in range(2):
                            ins = dve.tensor_tensor(q_place(q_lo, p, 2 * part + g2, h), q_source(g2, h),
                                                    q_place(q_hi, p, 2 * part + g2, h).bitcast(F32), ALU.subtract)
                            if (g2, h) != (1, 1):
                                step(ins)
                ins.then_inc(qk_ready, 1)

            def build_bias(s):
                p, n = divmod(s, NB)
                if n == 2:
                    return
                k = BAND_CLASS[n]
                if n == 0:
                    dve.wait_ge(rpb_load, 16 * 8 * (p + 1))
                if s:
                    dve.wait_ge(masked, NG * s)
                win = rpb_win[:, :].rearrange("p (r c) -> p r c", c=RPB_PITCH)
                c0 = 16 + CLASS_SHIFT[k]
                for a, b, u in ((0, 8, 4), (8, 20, 0), (20, 28, 0)):
                    ins = dve.scalar_tensor_tensor(bias[:, a:b, :], na_mask[:, k, a:b, :], BIG,
                                                   win[:, u:u + b - a, c0:c0 + BAND], ALU.mult, ALU.subtract)
                    if b < BIAS_ROWS:
                        step(ins)
                ins.then_inc(bias_done, 1)

            def mask_scores(s, g):
                i = NG * s + g
                w = TILE_W[g]
                if g == 0:
                    dve.wait_ge(bias_done, 3 * (s // NB) + (1, 2, 2, 3)[s % NB])
                    if s >= 2:
                        dve.wait_ge(pT_done, NG * (s - 1))
                dve.wait_ge(score_done, i + 1)
                dve.tensor_tensor_reduce(probs[:, s % 2, TILE_OFF[g]:TILE_OFF[g] + w], bank[2 + i % 2][:, 0:w],
                                         bias[:, :, :].rearrange("p r c -> p (r c)")[:, BIAS_OFF[g]:BIAS_OFF[g] + w],
                                         1.0, 3e38, ALU.add, ALU.min, s_min[:, i:i + 1]).then_inc(masked, 1)

            def normalise_probs(s):
                dve.wait_ge(exp_done, NG * (s + 1))
                step(dve.reciprocal(s_inv[:, NG * s:NG * s + NG], s_sum[:, NG * s:NG * s + NG]))
                for g in range(NG):
                    t = probs[:, s % 2, TILE_OFF[g]:TILE_OFF[g] + TILE_W[g]]
                    dve.tensor_scalar(t, t, s_inv[:, NG * s + g:NG * s + g + 1], None, ALU.mult).then_inc(prob_done, 1)

            def take_pT(s, kg):
                i = NG * s + kg
                w = P * len(KG_GROUPS[kg])
                dve.wait_ge(pT_act, i + 1)
                dve.tensor_tensor(pT_lo[:, i % 2, 0:w], bank[4 + i % 2][:, 0:w], pT_hi[:, i % 2, 0:w].bitcast(F32),
                                  ALU.subtract).then_inc(pT_dve, 1)

            def take_mix(s):
                n = s % NB
                dve.wait_ge(mix_act, s + 1)
                step(dve.tensor_tensor(mix_place(mix_lo, n, 0), mix_source(0), mix_place(mix_hi, n, 0).bitcast(F32),
                                       ALU.subtract))
                dve.tensor_tensor(mix_place(mix_lo, n, 1), mix_source(1), mix_place(mix_hi, n, 1).bitcast(F32),
                                  ALU.subtract).then_inc(mix_dve, 1)

            def halves(t, size):
                v = t.rearrange("p (b s) -> p b s", s=size)
                return v[:, :, 0:size // 2], v[:, :, size // 2:]

            def z_arguments(h, i):
                if i not in ARG_OF:
                    return
                t = z_turn(h, i)
                zk, zq = zz[:, t, 0, :], zz[:, t, 1, :]
                f, b = h_cum[:, h % 2, 0, :], h_cum[:, h % 2, 1, :]
                operands_free(dve, h, i)
                if i < 4:
                    size = LEVELS[i]
                    (fl, fr), (bl, br) = halves(f, size), halves(b, size)
                    (kl, kr), (ql, qr) = halves(zk, size), halves(zq, size)
                    shape = [P, S // size, size // 2]
                    f_mid = fl[:, :, size // 2 - 1:size // 2].to_broadcast(shape)
                    b_mid = br[:, :, 0:1].to_broadcast(shape)
                    step(dve.tensor_tensor(kl, f_mid, fl, ALU.subtract))
                    step(dve.tensor_tensor(qr, fr, f_mid, ALU.subtract))
                    step(dve.tensor_tensor(kr, b_mid, br, ALU.subtract))
                    dve.tensor_tensor(ql, bl, b_mid, ALU.subtract).then_inc(z_arg, 1)
                elif i < 6:
                    src, mid = ((f, 3), (b, 4))[i - 4]
                    v, vk, vq = (a.rearrange("p (b s) -> p b s", s=8) for a in (src, zk, zq))
                    m = v[:, :, mid:mid + 1].to_broadcast([P, S // 8, 8])
                    step(dve.tensor_tensor(vk, m, v, ALU.subtract))
                    dve.tensor_tensor(vq, v, m, ALU.subtract).then_inc(z_arg, 1)
                else:
                    fv, bv, v0, v1 = (a.rearrange("p (b s) -> p b s", s=CHUNK) for a in (f, b, zk, zq))
                    shape = [P, NCH, CHUNK]
                    step(dve.tensor_tensor(v0, fv[:, :, CHUNK - 1:CHUNK].to_broadcast(shape), fv, ALU.subtract))
                    dve.tensor_tensor(v1, bv[:, :, 0:1].to_broadcast(shape), bv, ALU.subtract).then_inc(z_arg, 1)

            def z_products(h, i):
                t = z_turn(h, i)
                zk, zq = zz[:, t, 0, :], zz[:, t, 1, :]
                q, kf, kb = h_q[:, h % 2, :], h_key[:, h % 2, 0, :], h_key[:, h % 2, 1, :]
                if i == 0:
                    dve.wait_ge(*freed(UNIT[("hq", h, 1)]))
                if i == 6:
                    operands_free(dve, h, i)
                    dve.tensor_tensor(zk, kf, kb, ALU.add).then_inc(z_ready, 1)
                    return
                dve.wait_ge(z_exp, 8 * h + (i if i < 6 else i - 1) + 1)
                if i < 4:
                    kl, kr = halves(zk, LEVELS[i])
                    step(dve.tensor_tensor(kl, kl, halves(kf, LEVELS[i])[0], ALU.mult))
                    step(dve.tensor_tensor(kr, kr, halves(kb, LEVELS[i])[1], ALU.mult))
                    dve.tensor_tensor(zq, zq, q, ALU.mult).then_inc(z_ready, 1)
                elif i < 6:
                    step(dve.tensor_tensor(zk, zk, (kf, kb)[i - 4], ALU.mult))
                    dve.tensor_tensor(zq, zq, q, ALU.mult).then_inc(z_ready, 1)
                elif i == 7:
                    dve.tensor_tensor(zz[:, t, :, :], zz[:, t, :, :], h_key[:, h % 2, :, :], ALU.mult).then_inc(z_ready, 1)
                else:
                    step(dve.tensor_tensor(zk, zk, q, ALU.mult))
                    dve.tensor_tensor(zq, zq, q, ALU.mult).then_inc(z_ready, 1)

            def take_level(h, i):
                for cg in range(2):
                    n = 2 * (NLEV * h + i) + cg
                    dve.wait_ge(lev_done, n + 1)
                    if i == 0:
                        if h:
                            dve.wait_ge(o_done, 2 * h)
                    else:
                        dve.wait_ge(lev_taken, n - 1)
                    dve.copy_predicated(scores[:, 4 * cg:4 * cg + 4, :],
                                        hg_mask[:, i:i + 1, :].to_broadcast([P, 4, P]),
                                        bank[2 + cg][:, :].rearrange("p (c i) -> p c i", c=4)).then_inc(lev_taken, 1)

            def chain_states(h):
                dve.wait_ge(g_ready, h + 1)
                if h:
                    dve.wait_ge(o_done, 2 * h)
                for d in range(2):
                    for j in range(2):
                        chunks = (((0, 1, 2, 3), (4, 5, 6)), ((7, 6, 5, 4), (3, 2, 1)))[d][j]
                        dve.wait_ge(upd_done, 4 * h + 2 * d + j + 1)
                        for k, c in enumerate(chunks):
                            src = bank[4 + j][:, P * k:P * k + P]
                            dst = state[:, d, c - d, :]
                            if c == (0, 7)[d]:
                                ins = dve.tensor_copy(dst, src)
                            else:
                                last = state[:, d, c - 1 if d == 0 else c, :]
                                ins = dve.scalar_tensor_tensor(dst, last, g_chunk[:, d, c:c + 1], src, ALU.mult, ALU.add)
                            if k < len(chunks) - 1:
                                step(ins)
                        ins.then_inc(st_done, 1)
                        dve.wait_ge(st_done, 4 * h + 2 * d + j + 1)

            def head_output(h, part):
                n = 2 * h + part
                cols = slice(part * HALF, part * HALF + HALF)
                dve.wait_ge(o_rs, n + 1)
                dve.scalar_tensor_tensor(tmp[:, 0, :], bank[6 + part][:, :], gnorm[:, 0:1], tmp[:, 1, :],
                                         ALU.mult, ALU.mult).then_inc(o_norm, 1)
                dve.wait_ge(o_norm, 2 * n + 1)
                dve.tensor_tensor(tmp[:, 0, :], tmp[:, 0, :], h_gate[:, cols], ALU.mult).then_inc(o_norm, 1)
                dve.wait_ge(y_act, n + 1)
                dve.tensor_tensor(k_tok[:, HALF:].bitcast(F32R), tmp[:, 0, :], k_tok[:, 0:HALF],
                                  ALU.subtract).then_inc(y_dve, 1)

            dve.memset(eps_col[:, :], EPS).then_inc(ready_cols, 1)
            dve.memset(one_col[:, :], 1.0).then_inc(ready_cols, 1)
            for half in range(2):
                for t in range(4 * half, 4 * half + 4):
                    normalise_tokens(0, t)
                dve.wait_ge(c_load, CONSTS)
                for n in range(KT * half, KT * half + KT):
                    take_uT(0, n)
            dve.tensor_tensor(lb[:, :, :], lb_raw[:, :, 1, :], lb_raw[:, :, 0, :], ALU.subtract).then_inc(lb_diff, 1)
            dve.wait_ge(lb_exp, 1)
            step(dve.tensor_scalar(lb[:, :, :], lb[:, :, :], BIG, 1.0, ALU.min, ALU.add))
            step(dve.reciprocal(lb[:, :, :], lb[:, :, :]))
            step(dve.tensor_scalar(lb_rest[:, :, :], lb[:, :, :], -1.0, 1.0, ALU.mult, ALU.add))
            step(dve.tensor_scalar(lb_neg[:, :, :], lb[:, :, :], 1.0, None, ALU.subtract))
            dve.tensor_scalar(qk_w[:, 0:1], qk_w[:, 0:1], -float(NA_DIM) ** -0.5, None, ALU.mult).then_inc(params, 1)
            dve.wait_ge(params, 1)
            dve.wait_ge(uT_done, 16)
            step(dve.memset(q_hi[:, :, :, :, :].bitcast(F32), 0.0))
            dve.memset(q_lo[:, :, :, :, :].bitcast(F32), 0.0).then_inc(cleared, 1)
            dve.wait_ge(mask_load, 48)
            for n in range(FIRST_QK):
                unit(n)
            for n in range(FIRST_QK, BEFORE - 1):
                qk_unit(n)
            for s in range(-1, STEPS):
                if s + 1 < STEPS:
                    build_bias(s + 1)
                    for g in range(NG):
                        mask_scores(s + 1, g)
                if s >= 0:
                    for kg in range(NG):
                        take_pT(s, kg)
                    take_mix(s)
                if s <= 9:
                    qk_unit(BEFORE + s)
                if s + 1 < STEPS:
                    normalise_probs(s + 1)
            hgrn_may_start(dve)
            for n in FIRST_HEAD:
                unit(n)
            z_arguments(0, 0)
            z_products(0, 0)
            for h in range(HG_HEADS):
                for i in range(PIECES):
                    hh, j = after(h, i)
                    if hh < HG_HEADS:
                        z_arguments(hh, j)
                    if i < NLEV:
                        take_level(h, i)
                    if i == 7:
                        chain_states(h)
                    if i == 8:
                        for part in range(2):
                            head_output(h, part)
                    if hh < HG_HEADS:
                        z_products(hh, j)
                    for n in HEAD_UNITS[h][i]:
                        unit(n)
            def add_bank(i):
                t, half = divmod(i, 2)
                r = resid[:, t, half * HALF:half * HALF + HALF]
                return dve.tensor_tensor(r, r, bank[4 + i % 4][:, :], ALU.add)

            dve.wait_ge(resid_load, 16)
            for b in range(OUT_BLOCKS):
                for i in range(2 * TT):
                    dve.wait_ge(down_done, 16 * b + i + 1)
                    add_bank(i).then_inc(added, 1)
            for half in range(2):
                for t in range(4 * half, 4 * half + 4):
                    normalise_tokens(1, t)
                for n in range(KT * half, KT * half + KT):
                    take_uT(1, n)
            with dve.Fori(0, MLP_BLOCKS, 1) as b:
                for i in range(2 * FBLK):
                    f, half = divmod(i, 2)
                    cols = slice(half * HALF, half * HALF + HALF)
                    r, a = u_tok[:, i, 0:HALF], u_tok[:, i, HALF:D]
                    dve.wait_ge(relu_done, b * 4 + (i + 1))
                    dve.tensor_tensor(a, r, r, ALU.mult).then_inc(sqr_done, 1)
                    dve.wait_ge(sqr_done, b * 4 + (i + 1))
                    dve.wait_ge(a_hi, b * 4 + (i + 1))
                    dve.tensor_tensor(act_lo[:, 0, f, cols], a, act_hi[:, 0, f, cols].bitcast(F32),
                                      ALU.subtract).then_inc(a_lo, 1)
                for i in range(2 * TT):
                    dve.wait_ge(down_done, b * 16 + (16 * OUT_BLOCKS + i + 1))
                    dve.wait_ge(added, b * 16 + (16 * (OUT_BLOCKS - 1) + i + 1))
                    add_bank(i).then_inc(added, 1)

        @block.tensor
        def _(pe):
            def product(dst, a, b, first=True, last=True, skip=False):
                pe.matmul(dst, a[0], b[0], start=first, stop=False, skip_group_check=skip)
                pe.matmul(dst, a[0], b[1], start=False, stop=False, skip_group_check=skip)
                return pe.matmul(dst, a[1], b[0], start=False, stop=last, skip_group_check=skip)

            ring = (w_hi, w_lo)
            uT = (uT_hi, uT_lo)

            def transpose_tokens(norm, n):
                k, half = n % KT, n // KT
                src = (x_tok, u_tok)[norm]
                if n >= 2:
                    pe.wait_ge(uT_dve, 16 * norm + n - 1)
                pe.wait_ge(u_ready, TT * norm + 4 * half + 4)
                for t in range(4):
                    ins = pe.transpose(bank[2 + n % 2][:, P * t:P * t + P], src[:, 4 * half + t, P * k:P * k + P], ident)
                ins.then_inc(uT_done, 1)

            def projection(n):
                kind, what, part = UNITS[n]
                if n >= 2:
                    pe.wait_ge(*freed(n - 2))
                b = bank[n % 2]
                done = 0
                if n:
                    k1, _, p1 = UNITS[n - 1]
                    done = 2 * (p1 == TT - 1) if k1 in ("v", "hv") else int(p1 == 1)
                if kind in ("v", "hv"):
                    tile = TILE_OF[("in", (C_V if kind == "v" else C_HV) + 256 * what)]
                    pe.wait_ge(w_split, 2 * (tile + 2))
                    pe.wait_ge(uT_dve, 8 if part < 4 else 16)
                    r = tile % RING
                    for k in range(KT):
                        a = [t[:, k, P * part:P * part + P] for t in uT]
                        w = [t[:, r:r + 2, P * k:P * k + P] for t in ring]
                        dst = b[:, 0:256]
                        first = pe.matmul(dst, a[0], w[0], start=k == 0, stop=False)
                        if k == 0 and done:
                            first.then_inc(w_used, done)
                        pe.matmul(dst, a[0], w[1], start=False, stop=False)
                        ins = pe.matmul(dst, a[1], w[0], start=False, stop=k == KT - 1)
                else:
                    tile = TILE_OF[("in", COL[kind] + P * what)]
                    pe.wait_ge(w_split, 2 * (tile + 1))
                    pe.wait_ge(uT_dve, 16)
                    r = tile % RING
                    for k in range(KT):
                        w = [t[:, r, P * k:P * k + P] for t in ring]
                        u = [t[:, k, part * HALF:part * HALF + HALF] for t in uT]
                        first = pe.matmul(b[:, :], w[0], u[0], start=k == 0, stop=False)
                        if k == 0 and done:
                            first.then_inc(w_used, done)
                        pe.matmul(b[:, :], w[0], u[1], start=False, stop=False)
                        ins = pe.matmul(b[:, :], w[1], u[0], start=False, stop=k == KT - 1)
                ins.then_inc(proj_done, 1)

            def qk_average(n):
                pe.wait_ge(qk_sq, n - FIRST_QK + 1)
                if n > FIRST_QK:
                    pe.wait_ge(unit_act, act_hands(n - 1) + 1)
                pe.matmul(bank[7][:, :], head_mean, qk_t[:, 0, :], start=True, stop=True).then_inc(qk_mean, 1)

            def score_tiles(s):
                p, n = divmod(s, NB)
                pe.wait_ge(qk_ready, 4 * (p + 1))
                for g in range(NG):
                    i = NG * s + g
                    if i >= 2:
                        pe.wait_ge(masked, i - 1)
                    rows = slice(KEY_ROW0[g], KEY_ROW0[g] + KEY_ROWS[g])
                    cols = slice(BAND_START[n], BAND_START[n] + BAND)
                    keys = [t[:, p % 2, :].rearrange("p (r c) -> p r c", c=GRID)[:, rows, cols] for t in (k_hi, k_lo)]
                    product(bank[2 + i % 2][:, 0:TILE_W[g]], [t[:, p % 2, g, n, :] for t in (q_hi, q_lo)],
                            keys).then_inc(score_done, 1)

            def transpose_probs(s, kg):
                i = NG * s + kg
                if kg == 0:
                    pe.wait_ge(prob_done, NG * (s + 1))
                if i >= 2:
                    pe.wait_ge(pT_dve, i - 1)
                for j, g in enumerate(KG_GROUPS[kg]):
                    at = TILE_OFF[g] + P * (kg - KG0[g])
                    ins = pe.transpose(bank[4 + i % 2][:, P * j:P * j + P], probs[:, s % 2, at:at + P], ident)
                ins.then_inc(pT_done, 1)

            def times_values(s, kg):
                i = NG * s + kg
                g0, w = KG_GROUPS[kg][0], P * len(KG_GROUPS[kg])
                pe.wait_ge(pT_dve, i + 1)
                if kg == 0:
                    pe.wait_ge(v_load[s % 2], 16 * 8 * (s // 2 + 1))
                    if s:
                        pe.wait_ge(mix_dve, s)
                product(bank[6][:, P * g0:P * g0 + w], [t[:, s % 2, kg, :] for t in (v_hi, v_lo)],
                        [t[:, i % 2, 0:w] for t in (pT_hi, pT_lo)], first=kg == 0, last=kg == NG - 1,
                        skip=True).then_inc(pv_done, 1)

            def chunk(t, c):
                return t[:, P * c:P * c + P]

            def level(h, i):
                t = z_turn(h, i)
                pe.wait_ge(z_ready, PIECES * h + i + 1)
                for cg in range(2):
                    n = 2 * (NLEV * h + i) + cg
                    if n >= 2:
                        pe.wait_ge(lev_taken, n - 1)
                    else:
                        pe.wait_ge(masked, NG * STEPS)
                    for c in range(4 * cg, 4 * cg + 4):
                        q = h_q[:, h % 2, :] if i == 6 else zz[:, t, 1, :]
                        ins = pe.matmul(bank[2 + cg][:, P * (c % 4):P * (c % 4) + P], chunk(zz[:, t, 0, :], c),
                                        chunk(q, c), start=True, stop=True)
                    ins.then_inc(lev_done, 1)

            def chunk_products(h):
                t = z_turn(h, 7)
                pe.wait_ge(z_ready, PIECES * h + 8)
                for d in range(2):
                    for cg in range(2):
                        if d == 0:
                            if h:
                                pe.wait_ge(o_rs, 2 * h)
                            else:
                                pe.wait_ge(pT_dve, NG * STEPS)
                        else:
                            pe.wait_ge(st_done, 4 * h + cg + 1)
                        for c in range(4 * cg, 4 * cg + 4):
                            ins = pe.transpose(bank[4 + cg][:, P * (c % 4):P * (c % 4) + P], chunk(zz[:, t, d, :], c), ident)
                        ins.then_inc(kT_done, 1)
                    pe.wait_ge(kT_act, 4 * h + 2 * d + 2)
                    for j in range(2):
                        for k, c in enumerate((((0, 1, 2, 3), (4, 5, 6)), ((7, 6, 5, 4), (3, 2, 1)))[d][j]):
                            ins = pe.matmul(bank[4 + j][:, P * k:P * k + P], chunk(k_tok, c), h_v[:, c, P * h:P * h + P],
                                            start=True, stop=True)
                        ins.then_inc(upd_done, 1)

            def head_outputs(h):
                t = z_turn(h, 8)
                pe.wait_ge(z_ready, PIECES * (h + 1))
                pe.wait_ge(st_done, 4 * (h + 1))
                pe.wait_ge(lev_taken, 2 * NLEV * (h + 1))
                for part in range(2):
                    if h:
                        pe.wait_ge(o_norm, 4 * h)
                    else:
                        pe.wait_ge(mix_dve, STEPS)
                        pe.wait_ge(unit_act, act_hands(UNIT[("hv", 0, 0)]))
                    for c in range(4 * part, 4 * part + 4):
                        dst = bank[6 + part][:, P * (c % 4):P * (c % 4) + P]
                        pe.matmul(dst, h_v[:, c, P * h:P * h + P], scores[:, c, :], start=True, stop=False)
                        if c >= 1:
                            ins = pe.matmul(dst, state[:, 0, c - 1, :], chunk(zz[:, t, 0, :], c), start=False, stop=c == 7)
                        if c <= 6:
                            ins = pe.matmul(dst, state[:, 1, c, :], chunk(zz[:, t, 1, :], c), start=False, stop=True)
                    ins.then_inc(o_done, 1)
                for part in range(2):
                    pe.wait_ge(o_sq, 2 * h + part + 1)
                    pe.matmul(bank[4 + part][:, :], all_mean, tmp[:, 0, :], start=True, stop=True).then_inc(o_mean, 1)

            pe.wait_ge(c_load, CONSTS)
            for n in range(2 * KT):
                transpose_tokens(0, n)
            for n in range(FIRST_QK + 1):
                projection(n)
            for n in range(FIRST_QK + 1, BEFORE):
                projection(n)
                qk_average(n - 1)
            for s in range(-1, STEPS):
                if s + 1 < STEPS:
                    if s == -1:
                        pe.wait_ge(uT_dve, 16)
                    score_tiles(s + 1)
                if s <= 9:
                    qk_average(BEFORE + s)
                if s >= 0:
                    transpose_probs(s, 0)
                    transpose_probs(s, 1)
                    times_values(s, 0)
                    transpose_probs(s, 2)
                    times_values(s, 1)
                    transpose_probs(s, 3)
                    times_values(s, 2)
                    times_values(s, 3)
                for n in STEP_UNITS[s]:
                    projection(n)
            for n in FIRST_HEAD:
                projection(n)
            for h in range(HG_HEADS):
                for i in range(PIECES):
                    if i < NLEV:
                        level(h, i)
                    elif i == 7:
                        chunk_products(h)
                    else:
                        head_outputs(h)
                    for n in HEAD_UNITS[h][i]:
                        projection(n)

            def add_product(i, turn, place, finished, free):
                t, half = divmod(i, 2)
                pe.wait_ge(added, free)
                dst = bank[4 + i % 4][:, :]
                for f in range(FBLK):
                    a = [x_[:, turn, f, P * t:P * t + P] for x_ in (act_hi, act_lo)]
                    w = [x_[:, place + f, half * HALF:half * HALF + HALF] for x_ in ring]
                    first = pe.matmul(dst, a[0], w[0], start=f == 0, stop=False)
                    if f == 0 and finished:
                        first.then_inc(w_used, finished)
                    pe.matmul(dst, a[0], w[1], start=False, stop=False)
                    ins = pe.matmul(dst, a[1], w[0], start=False, stop=f == FBLK - 1)
                ins.then_inc(down_done, 1)

            for b in range(OUT_BLOCKS):
                pe.wait_ge(w_split, 2 * (N_IN + FBLK * (b + 1)))
                pe.wait_ge(act_load[b % 2], 32 * (b // 2 + 1))
                if b == 0:
                    pe.wait_ge(y_dve, 2 * HG_HEADS)
                for i in range(2 * TT):
                    add_product(i, b % 2, FBLK * b % RING, (1 if b == 0 else FBLK) if i == 0 else 0,
                                max(16 * b + i - 3, 0))
            for n in range(2 * KT):
                transpose_tokens(1, n)
            pe.wait_ge(uT_dve, 32)
            with pe.Fori(0, MLP_BLOCKS, 1) as b:
                for i in range(2 * FBLK):
                    f, half = divmod(i, 2)
                    pe.wait_ge(relu_done, b * 4)
                    pe.wait_ge(w_split, b * 8 + 2 * (len(TILES) + f + 1))
                    for k in range(KT):
                        w = [t[:, f, P * k:P * k + P] for t in ring]
                        u = [t[:, k, half * HALF:half * HALF + HALF] for t in uT]
                        first = pe.matmul(bank[i][:, :], w[0], u[0], start=k == 0, stop=False)
                        if k == 0 and half == 0:
                            first.then_inc(w_used, FBLK if f == 0 else 1)
                        pe.matmul(bank[i][:, :], w[0], u[1], start=False, stop=False)
                        ins = pe.matmul(bank[i][:, :], w[1], u[0], start=False, stop=k == KT - 1)
                    ins.then_inc(up_done, 1)
                pe.wait_ge(a_lo, b * 4 + 4)
                pe.wait_ge(w_split, b * 8 + 2 * (len(TILES) + 2 * FBLK))
                for i in range(2 * TT):
                    add_product(i, 0, FBLK, 1 if i == 0 else 0, b * 16 + (16 * OUT_BLOCKS + i - 3))


_INS = ["x", "w_in", "w_out", "attn_norm_w", "mlp_norm_w", "q_norm_w", "k_norm_w", "rpb", "hg_norm_w",
        "lb_fwd", "lb_bwd", "w_up", "w_down"]


def kernel(**inputs):
    import numpy as _np
    import concourse.bacc as _bacc
    from concourse import mybir as _mybir
    from concourse.bass_utils import run_bass_kernel_spmd as _run

    nc = _bacc.Bacc("TRN2", target_bir_lowering=False, num_devices=1)
    data = {name: _np.ascontiguousarray(inputs[name]) for name in _INS}
    rpb = _np.zeros((NA_HEADS, 16, 15, RPB_PITCH), data["rpb"].dtype)
    for c in range(16):
        rpb[:, c, :, 1 + c:32 + c] = data["rpb"][0]
    data["rpb"] = rpb
    data["tables"], data["masks"] = shape_tables()
    arrays, args = {}, []
    for name, a in data.items():
        arrays[f"in_{name}"] = a
        args.append(nc.dram_tensor(f"in_{name}", a.shape, _mybir.dt.from_np(a.dtype), kind="ExternalInput").ap())
    out = nc.dram_tensor("out_0", (1, S, D), F32, kind="ExternalOutput").ap()
    hybrid_block(nc, *args, out)
    r = _run(nc, [arrays], core_ids=[0])
    return r.results[0]["out_0"]
```

```python
from contextlib import ExitStack

import numpy as np
import concourse.bass as bass
from concourse import mybir

F32 = mybir.dt.float32
F32R = mybir.dt.float32r
U8 = mybir.dt.uint8
I32 = mybir.dt.int32
ALU = mybir.AluOpType
ACT = mybir.ActivationFunctionType

P = 128
D = 1024
S = 1024
KT = D // P
TT = S // P
HALF = 512
NA_HEADS, NA_DIM = 8, 64
PAIRS = NA_HEADS // 2
GRID = 64
NG, NB = 4, 4
BAND = 32
BAND_START = [0, 8, 24, 32]
BAND_CLASS = [0, 1, 1, 2]
CLASS_SHIFT = [0, -8, -16]
KEY_ROW0 = [0, 0, 4, 8]
KEY_ROWS = [8, 12, 12, 8]
MASK_ROW0 = [4, 0, 0, 0]
TILE_W = [r * BAND for r in KEY_ROWS]
TILE_OFF = [0, 256, 640, 1024]
STEP_W = 1280
KG_GROUPS = [(0, 1), (0, 1, 2), (1, 2, 3), (2, 3)]
KG0 = [0, 0, 1, 2]
STEPS = PAIRS * NB
BIAS_ROWS = 28
BIAS_OFF = [0, 8 * BAND, 8 * BAND, 20 * BAND]
RPB_PITCH = 64
HG_HEADS = 4
CHUNK = 128
NCH = S // CHUNK
LEVELS = [128, 64, 32, 16]
NLEV = 7
EPS = 1e-6
BIG = 1e30
LOG_F_MIN = -18.0
GATE_MIN = -41.0
RING, STAGE = 4, 2
FBLK = 2
MLP_BLOCKS = 4 * D // P // FBLK
OUT_BLOCKS = KT // FBLK
LAST = MLP_BLOCKS - 1
MLP_TURNS = (MLP_BLOCKS - 2) // 2
C_Q, C_K, C_V, C_HQ, C_FF, C_FB, C_HV, C_HG = [512 * i for i in range(8)]
M_HG, M_NA, M_SCAN = 0, NLEV * P, NLEV * P + 3 * BIAS_ROWS * BAND
M_END = M_SCAN + S + 4


def shape_tables():
    f = np.zeros((P, 3 * P), np.float32)
    f[:, 0:P] = np.eye(P)
    for h in range(2):
        f[64 * h:64 * h + 64, P + 64 * h:P + 64 * h + 64] = 1.0 / 64
    f[:, 2 * P:] = 1.0 / P
    m = np.zeros((P, M_END), np.uint8)
    j, i = np.arange(P)[:, None], np.arange(P)[None, :]
    for n, b in enumerate(LEVELS):
        m[:, n * P:(n + 1) * P] = (j // b == i // b) & (j // (b // 2) != i // (b // 2))
    m[:, 4 * P:5 * P] = (j // 8 == i // 8) & (j < i)
    m[:, 5 * P:6 * P] = (j // 8 == i // 8) & (j > i)
    m[:, 6 * P:7 * P] = j == i
    p = np.arange(P)
    rr, c = (p % 64 // 16)[:, None, None], (p % 16)[:, None, None]
    col = np.arange(BAND)[None, None, :]
    for k, n in enumerate([0, 1, 3]):
        first = np.clip(16 * n + c - 8, 0, GRID - 16) - BAND_START[n]
        out_col = (col < first) | (col >= first + 16)
        u = np.arange(12)[None, :, None]
        row_in = (u - rr >= 0) & (u - rr <= 7)
        parts = [np.broadcast_to(out_col, (P, 8, BAND)), out_col | ~row_in,
                 np.broadcast_to(out_col, (P, 8, BAND))]
        at = M_NA + k * BIAS_ROWS * BAND
        m[:, at:at + BIAS_ROWS * BAND] = np.concatenate(parts, axis=1).reshape(P, -1)
    m[:, M_SCAN:] = (np.arange(S + 4) % CHUNK != 0)[None, :]
    return f, m.view(np.int32)


def weight_tiles():
    order = [("in", C_V + P * c) for c in range(4)]
    for p in range(PAIRS):
        order += [("in", C_Q + P * p), ("in", C_K + P * p)]
    order += [("in", C_HV + P * c) for c in range(4)]
    order += [("in", C_FF), ("in", C_FB), ("in", C_HQ)]
    for h in range(HG_HEADS):
        if h + 1 < HG_HEADS:
            order += [("in", c + P * (h + 1)) for c in (C_FF, C_FB, C_HQ)]
        order += [("in", C_HG + P * h)]
    order += [("out", k) for k in range(KT)]
    return order


UT_SPREAD = [(8, 9, 10, 11), (12, 13, 14, 15), (), ()]

TILES = weight_tiles()
N_IN = 32
N_TILES = len(TILES) + 2 * 4 * D // P


def proj_units():
    u = [("v", c, t) for c in range(2) for t in range(TT)]
    for p in range(PAIRS):
        u += [("q", p, 0), ("q", p, 1), ("k", p, 0), ("k", p, 1)]
    u += [("hv", c, t) for c in range(2) for t in range(TT)]
    for h in range(HG_HEADS):
        if h == 0:
            u += [(k, 0, i) for k in ("ff", "fb", "hq") for i in range(2)]
        if h + 1 < HG_HEADS:
            u += [(k, h + 1, i) for k in ("ff", "fb", "hq") for i in range(2)]
        u += [("hg", h, i) for i in range(2)]
    return u


UNITS = proj_units()
UNIT = {u: n for n, u in enumerate(UNITS)}
TILE_OF = {("in", c): n for n, (k, c) in enumerate(TILES) if k == "in"}
COL = {"q": C_Q, "k": C_K, "ff": C_FF, "fb": C_FB, "hq": C_HQ, "hg": C_HG}

BEFORE = 16 + 6
STEP_UNIT = {s: BEFORE + 1 + s for s in range(-1, 9)}
FIRST_HEAD = list(range(BEFORE + 10, UNIT[("hq", 0, 1)] + 1))
PIECES = 9
HEAD_UNITS = []
for _h in range(HG_HEADS):
    _units = [UNIT[(k, _h + 1, i)] for k in ("ff", "fb", "hq") for i in range(2)] if _h + 1 < HG_HEADS else []
    _units += [UNIT[("hg", _h, i)] for i in range(2)]
    HEAD_UNITS.append([[_u] for _u in _units] + [[]] * (PIECES - len(_units)))
BY_ACT = ("hv", "hq")
ARG_STEPS = [4, 4, 4, 4, 2, 2, 0, 2, 0]
PRODUCT_STEPS = [3, 3, 3, 3, 2, 2, 1, 1, 2]


def steps_to(steps, h, i):
    return sum(steps) * h + sum(steps[:i + 1])


def bank_uses(n, by_act):
    return sum((UNITS[i][0] in BY_ACT) == by_act for i in range(n + 1))


def hybrid_block(nc, x, w_in, w_out, attn_norm_w, mlp_norm_w, q_norm_w, k_norm_w, rpb, hg_norm_w,
                 lb_fwd, lb_bwd, w_up, w_down, tables, masks, out):
    ctx = ExitStack()
    with ctx:
        def sem(name):
            return ctx.enter_context(nc.semaphore(name))

        at = [int(nc.sbuf_base) + 31 & ~31]

        def place(name, shape, dt, size=4):
            t = nc.alloc_sbuf_tensor_at(name, shape, dt, offset=at[0])
            at[0] += int(np.prod(shape[1:])) * size + 31 & ~31
            return t

        uT_hi = place("uT_hi", [P, KT, S], F32R)
        uT_lo = place("uT_lo", [P, KT, S], F32R)
        w_hi = place("w_hi", [P, RING, 1024], F32R)
        w_lo = place("w_lo", [P, RING, 1024], F32R)
        stage = place("stage", [P, STAGE, 1024], F32)
        tab = place("tab", [P, 3 * P], F32)
        hg_mask = place("hg_mask", [P, NLEV, P], U8, 1)
        scan_mask = place("scan_mask", [P, S + 4], U8, 1)
        norm_w = place("norm_w", [P, 2, KT], F32)
        qk_w = place("qk_w", [P, 2], F32)
        gnorm = place("gnorm", [P, 1], F32)
        lb_raw = place("lb_raw", [P, 2, 2, HG_HEADS], F32)
        lb = place("lb", [P, 2, HG_HEADS], F32)
        lb_rest = place("lb_rest", [P, 2, HG_HEADS], F32)
        lb_neg = place("lb_neg", [P, 2, HG_HEADS], F32)
        ssq = place("ssq", [P, 2, TT], F32)
        rstd = place("rstd", [P, 2, TT], F32)
        s_min = place("s_min", [P, STEPS * NG], F32)
        s_sum = place("s_sum", [P, STEPS * NG], F32)
        s_inv = place("s_inv", [P, STEPS * NG], F32)
        g_chunk = place("g_chunk", [P, 2, NCH], F32)
        eps_col = place("eps_col", [P, 1], F32)
        one_col = place("one_col", [P, 1], F32)
        work = at[0]
        ident, head_mean, all_mean = tab[:, 0:P], tab[:, P:2 * P], tab[:, 2 * P:3 * P]

        q_hi = place("q_hi", [P, 2, NG, NB, P], F32R)
        q_lo = place("q_lo", [P, 2, NG, NB, P], F32R)
        k_hi = place("k_hi", [P, 2, S], F32R)
        k_lo = place("k_lo", [P, 2, S], F32R)
        v_hi = place("v_hi", [P, 2, NG, P], F32R)
        v_lo = place("v_lo", [P, 2, NG, P], F32R)
        probs = place("probs", [P, 2, STEP_W], F32)
        pT_hi = place("pT_hi", [P, 2, 384], F32R)
        pT_lo = place("pT_lo", [P, 2, 384], F32R)
        bias = place("bias", [P, BIAS_ROWS, BAND], F32)
        rpb_win = place("rpb_win", [P, 12 * RPB_PITCH], F32)
        na_mask = place("na_mask", [P, 3, BIAS_ROWS, BAND], U8, 1)
        qk_t = place("qk_t", [P, 3, HALF], F32)
        mix_na = place("mix_na", [P, S], F32)
        end_attention = at[0]
        vs = nc.alloc_sbuf_tensor_at("vs", [P, 2, 2, 256], F32, offset=end_attention)
        x_tok = nc.alloc_sbuf_tensor_at("x_tok", [P, TT, D], F32, offset=work)

        at[0] = work
        h_v = place("h_v", [P, TT, 512], F32)
        h_gates = place("h_gates", [P, 2, 4, S], F32)
        h_gate = place("h_gate", [P, S], F32)
        tmp = place("tmp", [P, 2, HALF], F32)
        k_tok = place("k_tok", [P, S], F32)
        h_q = place("h_q", [P, 2, S], F32)
        zz = place("zz", [P, 2, 2, S], F32)
        state = place("state", [P, 2, NCH - 1, P], F32)
        scores = place("scores", [P, NCH, P], F32)
        gate_t = place("gate_t", [P, HALF], F32)
        end_hgrn = at[0]

        def h_cum(h, d):
            return h_gates[:, h % 2, d, :]

        def h_key(h, d):
            return h_gates[:, h % 2, 2 + d, :]

        at[0] = work
        u_tok = place("u_tok", [P, TT, D], F32)
        acts = place("acts", [P, 2, 2, FBLK, S], F32R)
        resid = place("resid", [P, TT, D], F32)
        end_mlp = at[0]
        na_back = nc.alloc_sbuf_tensor_at("na_back", [P, PAIRS, S], F32, offset=work + TT * 512 * 4)
        assert max(end_attention + 8192, end_hgrn, end_mlp) <= int(nc.sbuf_usable_end), (
            end_attention, end_hgrn, end_mlp, int(nc.sbuf_usable_end))

        bank = [ctx.enter_context(nc.psum_tensor(f"bank{i}", [P, HALF], F32)) for i in range(8)]
        v_dram = [nc.dram_tensor(f"v_dram{i}", [S, 512], F32).ap() for i in range(2)]
        na_dram = nc.dram_tensor("na_dram", [PAIRS * P, S], F32).ap()

        c_load = sem("c_load")
        x_load = [sem(f"x_load{t}") for t in range(TT)]
        w_load = [sem(f"w_load{i}") for i in range(STAGE)]
        w_split = sem("w_split")
        w_used = sem("w_used")
        act_own = sem("act_own")
        dve_own = sem("dve_own")
        sq_done = sem("sq_done")
        u_ready = sem("u_ready")
        uT_done = sem("uT_done")
        uT_act = sem("uT_act")
        uT_dve = sem("uT_dve")
        proj_done = sem("proj_done")
        act_freed = sem("act_freed")
        dve_freed = sem("dve_freed")
        unit_act = sem("unit_act")
        unit_dve = sem("unit_dve")
        qk_sq = sem("qk_sq")
        qk_mean = sem("qk_mean")
        qk_ready = sem("qk_ready")
        v_stored = [sem(f"v_stored{i}") for i in range(2)]
        v_load = [sem(f"v_load{i}") for i in range(2)]
        rpb_load = sem("rpb_load")
        bias_done = sem("bias_done")
        score_done = sem("score_done")
        masked = sem("masked")
        exp_done = sem("exp_done")
        prob_done = sem("prob_done")
        pT_done = sem("pT_done")
        pT_act = sem("pT_act")
        pT_dve = sem("pT_dve")
        pv_done = sem("pv_done")
        mix_done = sem("mix_done")
        na_store = sem("na_store")
        z_arg = sem("z_arg")
        z_exp = sem("z_exp")
        z_ready = sem("z_ready")
        lev_done = sem("lev_done")
        lev_taken = sem("lev_taken")
        kT_done = sem("kT_done")
        kT_act = sem("kT_act")
        g_ready = sem("g_ready")
        upd_done = sem("upd_done")
        st_done = sem("st_done")
        o_done = sem("o_done")
        o_sq = sem("o_sq")
        o_mean = sem("o_mean")
        o_rs = sem("o_rs")
        o_norm = sem("o_norm")
        y_done = sem("y_done")
        na_load = sem("na_load")
        m_hi = sem("m_hi")
        m_lo = sem("m_lo")
        down_done = sem("down_done")
        added = sem("added")
        up_done = sem("up_done")
        relu_done = sem("relu_done")
        sqr_done = sem("sqr_done")
        a_hi = sem("a_hi")
        a_lo = sem("a_lo")
        out_store = sem("out_store")
        mask_load = sem("mask_load")
        resid_load = [sem(f"resid_load{t}") for t in range(TT)]
        ready_cols = sem("ready_cols")
        lb_exp = sem("lb_exp")
        lb_diff = sem("lb_diff")
        params = sem("params")
        cleared = sem("cleared")

        def z_turn(h, i):
            return (h * PIECES + i) % 2

        def count(r, per_turn, n):
            return n if r is None else r * per_turn + n

        def up_order(j):
            return [divmod(i, 2) for i in range(2 * FBLK)] if j else [(0, 0), (1, 0), (0, 1), (1, 1)]

        CONSTS = 16 * 12
        FIRST_QK = UNIT[("q", 0, 0)]
        heads = (slice(0, 64), slice(64, 128))

        def freed(n):
            by_act = UNITS[n][0] in BY_ACT
            return (act_freed if by_act else dve_freed), bank_uses(n, by_act)

        def act_hands(n):
            return sum({"v": 1, "q": 5, "k": 2, "ff": 1, "fb": 1, "hg": 1}.get(UNITS[i][0], 0) for i in range(n))

        def dve_hands(n):
            return sum({"ff": 1, "fb": 1, "hg": 1}.get(UNITS[i][0], 0) for i in range(n))

        def qk_count(n):
            return sum({"q": 4, "k": 1}[UNITS[i][0]] for i in range(FIRST_QK, n + 1))

        def operands_free(eng, h, i):
            n = h * PIECES + i - 2
            if n < 0:
                return
            hh, j = divmod(n, PIECES)
            if j < NLEV:
                eng.wait_ge(lev_done, 2 * (NLEV * hh + j + 1))
            elif j == 7:
                eng.wait_ge(kT_done, 4 * (hh + 1))
            else:
                eng.wait_ge(o_done, 2 * (hh + 1))

        def hgrn_may_start(eng):
            eng.wait_ge(na_store, 16 * PAIRS)
            eng.wait_ge(pv_done, NG * STEPS)

        def uT_bank(norm, n):
            return bank[2 + n % 2] if norm == 0 else bank[4 + n % (4 if n >= KT else 2)]

        def mixer_tile(k):
            return na_back[:, k, :] if k < PAIRS else h_v[:, :, P * (k - PAIRS):P * (k - PAIRS) + P]

        def after(h, i, n):
            return divmod(h * PIECES + i + n, PIECES)

        def q_place(t, p, g, h):
            return t[heads[h], p % 2, g, :, 64 * h:64 * h + 64].rearrange("p n (r c) -> p r n c", c=16)

        def q_source(g2, h):
            return qk_t[heads[h], 2, 256 * g2:256 * g2 + 256].rearrange("p (r n c) -> p r n c", n=NB, c=16)

        def mix_place(t, n, h):
            return t[heads[h], :].rearrange("p (g r n c) -> p g r n c", g=NG, r=4, n=NB)[:, :, :, n, :]

        def mix_source(h):
            return bank[6][heads[h], :].rearrange("p (g h r c) -> p g h r c", g=NG, h=2, r=4)[:, :, h, :, :]

        block = ctx.enter_context(nc.Block())

        @block.sync
        def _(sp):
            x_v = x.rearrange("b (t p) d -> p (b t) d", p=P)
            for t in range(TT):
                sp.dma_start(x_tok[:, t, :], x_v[:, t, :]).then_inc(x_load[t], 16)
                if t == 3:
                    sp.dma_start(tab[:, :], tables).then_inc(c_load, 16)
            with nc.allow_non_contiguous_dma(reason="small parameter vectors"):
                sp.dma_start(norm_w[:, 0, :], attn_norm_w.rearrange("o (k p) -> p (o k)", p=P)).then_inc(c_load, 16)
                sp.dma_start(norm_w[:, 1, :], mlp_norm_w.rearrange("o (k p) -> p (o k)", p=P)).then_inc(c_load, 16)
                for h in heads:
                    sp.dma_start(qk_w[h, 0:1], q_norm_w.rearrange("o d -> d o")).then_inc(c_load, 16)
                    sp.dma_start(qk_w[h, 1:2], k_norm_w.rearrange("o d -> d o")).then_inc(c_load, 16)
                sp.dma_start(gnorm[:, :], hg_norm_w.rearrange("o d -> d o")).then_inc(c_load, 16)
                for i, src in enumerate((lb_fwd, lb_bwd)):
                    for r in range(2):
                        sp.dma_start(lb_raw[:, i, r, :], src[r].rearrange("(h d) -> d h", d=P)).then_inc(c_load, 16)

            w_in_v = w_in.rearrange("o (k p) n -> p (o k) n", p=P)
            w_out_v = w_out.rearrange("o (k p) n -> k p (o n)", p=P)
            w_down_v = w_down.rearrange("o (k p) n -> k p (o n)", p=P)
            def load_bias_window(p):
                if p >= 1:
                    sp.wait_ge(bias_done, 9 * p)
                for h in range(2):
                    for r in range(4):
                        src = rpb[2 * p + h, :, 3 - r:15 - r, :].rearrange("c r v -> c (r v)")
                        sp.dma_start(rpb_win[64 * h + 16 * r:64 * h + 16 * r + 16, :], src).then_inc(rpb_load, 16)

            def load_band(s):
                p, n = divmod(s, NB)
                if s >= 2:
                    sp.wait_ge(pv_done, NG * (s - 1))
                for i, dst in enumerate((v_hi, v_lo)):
                    for r in range(4):
                        src = v_dram[i].rearrange("(g r c) e -> r c g e", r=4, c=GRID)[
                            r, BAND_START[n]:BAND_START[n] + BAND, :, P * p:P * p + P]
                        sp.dma_start(dst[32 * r:32 * r + 32, s % 2, :, :].bitcast(F32), src).then_inc(v_load[s % 2], 16)

            w_up_v = w_up.rearrange("o (k p) n -> p (o k) n", p=P)
            for n, (kind, where) in enumerate(TILES):
                if n == 4:
                    load_bias_window(0)
                if n == 10:
                    for i in range(2):
                        sp.wait_ge(v_stored[i], 32 * 8)
                    load_band(0)
                    load_band(1)
                if n == 14:
                    for s in range(2, STEPS):
                        if (s + 1) % NB == 0 and (s + 1) // NB < PAIRS:
                            load_bias_window((s + 1) // NB)
                        load_band(s)
                if n == N_IN + RING:
                    sp.wait_ge(z_ready, steps_to(PRODUCT_STEPS, HG_HEADS - 1, -1))
                    sp.wait_ge(g_ready, HG_HEADS - 1)
                    sp.wait_ge(na_store, 16 * PAIRS)
                    sp.dma_start(na_back[:, :, :], na_dram.rearrange("(f p) s -> p f s", p=P)).then_inc(na_load, 16)
                if n == N_IN + RING + 1:
                    sp.wait_ge(o_done, 2 * HG_HEADS)
                    for t in range(TT):
                        sp.dma_start(resid[:, t, :], x_v[:, t, :]).then_inc(resid_load[t], 16)
                if n >= STAGE:
                    sp.wait_ge(w_split, 2 * (n - STAGE + 1))
                dst = stage[:, n % STAGE, :]
                if kind == "in":
                    sp.dma_start(dst.rearrange("p (k c) -> p k c", k=KT),
                                 w_in_v[:, :, where:where + P]).then_inc(w_load[n % STAGE], 16)
                else:
                    sp.dma_start(dst, w_out_v[where]).then_inc(w_load[n % STAGE], 16)

            def mlp_tiles(kind, r, j, at):
                for f in range(FBLK):
                    n = len(TILES) + at + f
                    sp.wait_ge(w_split, count(r, 8 * FBLK, 2 * (n - STAGE + 1)))
                    dst = stage[:, n % STAGE, :]
                    col = count(r, 2 * FBLK * P, (j * FBLK + f) * P)
                    if kind == "up":
                        sp.dma_start(dst.rearrange("p (k c) -> p k c", k=KT),
                                     w_up_v[:, :, bass.ds(col, P)]).then_inc(w_load[n % STAGE], 16)
                    else:
                        sp.dma_start(dst, w_down.rearrange("o f n -> (o f) n")[bass.ds(col, P), :]).then_inc(w_load[n % STAGE], 16)

            mlp_tiles("up", None, 0, 0)
            with sp.Fori(0, MLP_TURNS, 1) as r:
                mlp_tiles("up", r, 1, 2)
                mlp_tiles("down", r, 0, 4)
                mlp_tiles("up", r, 2, 6)
                mlp_tiles("down", r, 1, 8)
            mlp_tiles("up", None, LAST, 4 * LAST - 2)
            mlp_tiles("down", None, LAST - 1, 4 * LAST)
            mlp_tiles("down", None, LAST, 4 * LAST + 2)

            for t in range(TT):
                sp.wait_ge(added, 16 * (OUT_BLOCKS + MLP_BLOCKS - 1) + 2 * t + 2)
                sp.dma_start(out.rearrange("b (t p) d -> p (b t) d", p=P)[:, t, :], resid[:, t, :]).then_inc(out_store, 16)
            sp.wait_ge(out_store, 16 * TT)
            sp.wait_ge(v_stored[0], 32 * 8)
            sp.wait_ge(v_stored[1], 32 * 8)
            sp.wait_ge(na_store, 16 * PAIRS)

        @block.gpsimd
        def _(pool):
            def split(i, loaded, used, turn):
                pool.wait_ge(w_load[i % STAGE], loaded)
                if used is not None:
                    pool.wait_ge(w_used, used)
                pool.tensor_tensor(w_hi[:, i, :], stage[:, i % STAGE, :],
                                   one_col[:, 0:1].to_broadcast([P, 1024]), ALU.mult).then_inc(w_split, 1)
                pool.wait_ge(w_split, turn + 1)
                pool.tensor_tensor(w_lo[:, i, :], stage[:, i % STAGE, :], w_hi[:, i, :].bitcast(F32),
                                   ALU.subtract).then_inc(w_split, 1)

            pool.wait_ge(ready_cols, 2)
            for i in range(RING):
                split(i, 16 * (i // STAGE + 1), None, 2 * i)
            with pool.Fori(1, N_TILES // RING, 1) as r:
                for i in range(RING):
                    split(i, r * (16 * RING // STAGE) + 16 * (i // STAGE + 1),
                          r * RING + (i + 1 - RING), r * (2 * RING) + 2 * i)

        @block.scalar
        def _(act):
            own = [0]

            def step(ins):
                ins.then_inc(act_own, 1)
                own[0] += 1
                act.wait_ge(act_own, own[0])

            def rms(norm, t):
                if norm == 0:
                    src, scratch = x_tok, vs[:, :, :, :].rearrange("p a b c -> p (a b c)")
                else:
                    src, scratch = resid, u_tok[:, t, :]
                step(act.activation(scratch, src[:, t, :], ACT.Square, accum_out=ssq[:, norm, t:t + 1]))
                step(act.activation(rstd[:, norm, t:t + 1], ssq[:, norm, t:t + 1], ACT.Ln,
                                    scale=1.0 / D, bias=eps_col[:, 0:1]))
                act.activation(rstd[:, norm, t:t + 1], rstd[:, norm, t:t + 1], ACT.Exp,
                               scale=-0.5).then_inc(sq_done, 1)

            def take_uT(norm, n):
                k, half = n % KT, n // KT
                act.wait_ge(uT_done, norm * 16 + n + 1)
                act.activation(uT_hi[:, k, half * HALF:half * HALF + HALF], uT_bank(norm, n)[:, :], ACT.Copy,
                               scale=norm_w[:, norm, k:k + 1]).then_inc(uT_act, 1)

            def unit(n):
                kind, what, part = UNITS[n]
                b = bank[n % 2]
                cols = slice(part * HALF, part * HALF + HALF)
                if kind in ("v", "hv", "hq"):
                    act.wait_ge(proj_done, n + 1)
                if kind == "v":
                    if n >= 2:
                        act.wait_ge(v_stored[n % 2], 32 * (n // 2))
                    act.activation(vs[:, n % 2, 0, :].bitcast(F32R), b[:, 0:256], ACT.Copy).then_inc(unit_act, 1)
                    act.wait_ge(*freed(n))
                    for i in range(2):
                        act.dma_start(v_dram[i][P * part:P * part + P, 256 * what:256 * what + 256],
                                      vs[:, n % 2, i, :]).then_inc(v_stored[n % 2], 16)
                elif kind == "hv":
                    act.activation(h_v[:, part, 256 * what:256 * what + 256], b[:, 0:256], ACT.Copy).then_inc(act_freed, 1)
                elif kind == "hq":
                    if what >= 2:
                        act.wait_ge(z_ready, steps_to(PRODUCT_STEPS, what - 1, -1))
                        act.wait_ge(lev_done, 2 * NLEV * (what - 1))
                    act.activation(h_q[:, what % 2, cols], b[:, :], ACT.Copy).then_inc(act_freed, 1)
                elif kind in ("ff", "fb"):
                    d = ("ff", "fb").index(kind)
                    act.wait_ge(*freed(n))
                    step(act.activation(gate_t[:, :], gate_t[:, :], ACT.Exp, scale=-1.0))
                    step(act.activation(gate_t[:, :], gate_t[:, :], ACT.Ln, bias=one_col[:, 0:1]))
                    step(act.activation(gate_t[:, :], gate_t[:, :], ACT.Exp, scale=-1.0))
                    if what >= 2:
                        act.wait_ge(z_arg, steps_to(ARG_STEPS, what - 1, -1))
                    act.activation(h_cum(what, d)[:, cols], gate_t[:, :], ACT.Ln,
                                   scale=lb_rest[:, d, what:what + 1], bias=lb[:, d, what:what + 1]).then_inc(unit_act, 1)
                elif kind == "hg":
                    act.wait_ge(unit_dve, dve_hands(n) + 1)
                    step(act.activation(gate_t[:, :], gate_t[:, :], ACT.Exp, scale=-1.0))
                    step(act.activation(gate_t[:, :], gate_t[:, :], ACT.Ln, bias=one_col[:, 0:1]))
                    act.activation(gate_t[:, :], gate_t[:, :], ACT.Exp, scale=-1.0).then_inc(unit_act, 1)

            def qk_square(n):
                act.wait_ge(proj_done, n + 1)
                if n > FIRST_QK:
                    act.wait_ge(qk_mean, n - FIRST_QK)
                act.activation(qk_t[:, 0, :], bank[n % 2][:, :], ACT.Square).then_inc(qk_sq, 1)

            def qk_root(n):
                act.wait_ge(qk_mean, n - FIRST_QK + 1)
                if n > FIRST_QK:
                    act.wait_ge(*freed(n - 1))
                step(act.activation(qk_t[:, 1, :], bank[7][:, :], ACT.Ln, bias=eps_col[:, 0:1]))
                act.activation(qk_t[:, 1, :], qk_t[:, 1, :], ACT.Exp, scale=-0.5).then_inc(unit_act, 1)

            def qk_hi(n):
                kind, p, part = UNITS[n]
                act.wait_ge(*freed(n))
                if p >= 2:
                    act.wait_ge(score_done, NG * NB * (p - 1))
                if kind == "k":
                    act.activation(k_hi[:, p % 2, part * HALF:part * HALF + HALF], qk_t[:, 2, :],
                                   ACT.Copy).then_inc(unit_act, 1)
                else:
                    if n == FIRST_QK:
                        act.wait_ge(cleared, 1)
                    for g2 in range(2):
                        for h in range(2):
                            act.activation(q_place(q_hi, p, 2 * part + g2, h), q_source(g2, h),
                                           ACT.Copy).then_inc(unit_act, 1)

            def score_exp(s, g):
                i = NG * s + g
                t = probs[:, s % 2, TILE_OFF[g]:TILE_OFF[g] + TILE_W[g]]
                act.wait_ge(masked, i + 1)
                act.activation(t, t, ACT.Exp, scale=-1.0, bias=s_min[:, i:i + 1],
                               accum_out=s_sum[:, i:i + 1]).then_inc(exp_done, 1)

            def take_pT(s, kg):
                i = NG * s + kg
                w = P * len(KG_GROUPS[kg])
                act.wait_ge(pT_done, i + 1)
                if i >= 2:
                    act.wait_ge(pv_done, i - 1)
                act.activation(pT_hi[:, i % 2, 0:w], bank[4 + i % 2][:, 0:w], ACT.Copy).then_inc(pT_act, 1)

            def take_mix(s):
                p, n = divmod(s, NB)
                act.wait_ge(pv_done, NG * (s + 1))
                if n == 0 and p:
                    act.wait_ge(na_store, 16 * p)
                for h in range(2):
                    act.activation(mix_place(mix_na, n, h), mix_source(h), ACT.Copy).then_inc(mix_done, 1)

            def store_mix(p):
                act.wait_ge(mix_done, 2 * NB * (p + 1))
                act.dma_start(na_dram[P * p:P * p + P, :], mix_na[:, :]).then_inc(na_store, 16)

            def z_exponentials(h, i):
                if i == 6:
                    return
                t = z_turn(h, i)
                if i == 8:
                    operands_free(act, h, i)
                    act.activation(zz[:, t, :, :], h_gates[:, h % 2, 0:2, :], ACT.Exp).then_inc(z_exp, 1)
                else:
                    act.wait_ge(z_arg, steps_to(ARG_STEPS, h, i))
                    act.activation(zz[:, t, :, :], zz[:, t, :, :], ACT.Exp).then_inc(z_exp, 1)

            def chunk_decays(h):
                act.wait_ge(z_arg, steps_to(ARG_STEPS, h, 0))
                if h:
                    act.wait_ge(st_done, 4 * h)
                step(act.activation(g_chunk[:, 0, :], h_cum(h, 0)[:, CHUNK - 1::CHUNK], ACT.Exp))
                act.activation(g_chunk[:, 1, :], h_cum(h, 1)[:, 0::CHUNK], ACT.Exp).then_inc(g_ready, 1)

            def take_k_tok(h):
                for d in range(2):
                    for cg in range(2):
                        n = 4 * h + 2 * d + cg
                        act.wait_ge(kT_done, n + 1)
                        if cg == 0 and n:
                            act.wait_ge(upd_done, n)
                        act.activation(k_tok[:, HALF * cg:HALF * cg + HALF], bank[4 + 2 * d + cg][:, :], ACT.Copy).then_inc(kT_act, 1)

            def head_squares(h):
                for part in range(2):
                    act.wait_ge(o_done, 2 * h + part + 1)
                    if h:
                        act.wait_ge(y_done, 2 * h)
                    act.activation(tmp[:, part, :], bank[6 + part][:, :], ACT.Square).then_inc(o_sq, 1)

            def head_roots(h):
                for part in range(2):
                    act.wait_ge(o_mean, 2 * h + part + 1)
                    step(act.activation(tmp[:, part, :], bank[4 + part][:, :], ACT.Ln, bias=eps_col[:, 0:1]))
                    act.activation(tmp[:, part, :], tmp[:, part, :], ACT.Exp, scale=-0.5).then_inc(o_rs, 1)

            def mixer_hi(b):
                if b == 0:
                    act.wait_ge(z_ready, steps_to(PRODUCT_STEPS, HG_HEADS, -1))
                    act.wait_ge(na_load, 16)
                if b == 1:
                    act.wait_ge(y_done, 2 * HG_HEADS)
                if b >= 2:
                    act.wait_ge(down_done, 16 * (b - 1))
                for f in range(FBLK):
                    dst = acts[:, b % 2, 0, f, :]
                    if b >= 2:
                        act.activation(dst.rearrange("p (c i) -> p c i", i=P), mixer_tile(FBLK * b + f), ACT.Copy).then_inc(m_hi, 1)
                    else:
                        act.activation(dst, mixer_tile(FBLK * b + f), ACT.Copy).then_inc(m_hi, 1)

            def activations(r, j, spread=()):
                for i, (f, half) in enumerate(up_order(j)):
                    act.wait_ge(up_done, count(r, 8, 4 * j + i + 1))
                    if i or j:
                        act.wait_ge(a_lo, count(r, 8, 4 * j + i))
                    act.activation(u_tok[:, i, 0:HALF], bank[2 * f + half][:, :], ACT.Relu).then_inc(relu_done, 1)
                    act.wait_ge(sqr_done, count(r, 8, 4 * j + i + 1))
                    act.wait_ge(down_done, count(r, 32, 16 * (OUT_BLOCKS + max(j - 1, 0))))
                    act.activation(acts[:, j % 2, 0, f, half * HALF:half * HALF + HALF], u_tok[:, i, HALF:D],
                                   ACT.Copy).then_inc(a_hi, 1)
                    for n in (spread[i] if spread else ()):
                        take_uT(1, n)

            act.preload_act_table_set("natural_log_exp_and_others")
            act.dma_start(na_mask[:, :, :, :].rearrange("p s r c -> p (s r c)").bitcast(I32), masks[:, M_NA // 4:M_SCAN // 4]).then_inc(mask_load, 16)
            act.dma_start(hg_mask[:, :, :].rearrange("p l i -> p (l i)").bitcast(I32), masks[:, M_HG // 4:M_NA // 4]).then_inc(mask_load, 16)
            act.dma_start(scan_mask[:, :].bitcast(I32), masks[:, M_SCAN // 4:M_END // 4]).then_inc(mask_load, 16)
            act.wait_ge(ready_cols, 2)
            for t in range(TT):
                if t == 4:
                    act.wait_ge(c_load, CONSTS)
                if t >= 4:
                    take_uT(0, 2 * t - 8)
                    take_uT(0, 2 * t - 7)
                act.wait_ge(x_load[t], 16)
                rms(0, t)
            act.wait_ge(lb_diff, 1)
            act.activation(lb[:, :, :], lb[:, :, :], ACT.Exp).then_inc(lb_exp, 1)
            for n in range(FIRST_QK):
                unit(n)
                if n < 4:
                    take_uT(0, KT + 2 * n)
                    take_uT(0, KT + 2 * n + 1)
            for n in range(FIRST_QK, BEFORE - 1):
                qk_square(n)
                qk_root(n)
                qk_hi(n)
            for s in range(-2, STEPS):
                qk = BEFORE + s if -1 <= s <= 9 else None
                if qk is not None:
                    qk_square(qk)
                if s >= 0:
                    take_pT(s, 0)
                    take_pT(s, 1)
                if qk is not None:
                    qk_root(qk)
                if s >= 0:
                    take_pT(s, 2)
                    take_pT(s, 3)
                if qk is not None:
                    qk_hi(qk)
                if s + 2 < STEPS:
                    for g in range(NG):
                        score_exp(s + 2, g)
                if s >= 0:
                    take_mix(s)
                    if s % NB == NB - 1:
                        store_mix(s // NB)
            hgrn_may_start(act)
            for n in FIRST_HEAD:
                unit(n)
            z_exponentials(0, 0)
            last = []
            for h in range(HG_HEADS):
                for i in range(PIECES):
                    if after(h, i, 1)[0] < HG_HEADS:
                        z_exponentials(*after(h, i, 1))
                    if i == 0:
                        chunk_decays(h)
                        if h:
                            head_roots(h - 1)
                    if i == 7:
                        take_k_tok(h)
                    for n in last:
                        unit(n)
                    if i == 8:
                        if h == HG_HEADS - 1:
                            mixer_hi(0)
                        head_squares(h)
                    last = HEAD_UNITS[h][i]
            head_roots(HG_HEADS - 1)
            for b in range(1, OUT_BLOCKS):
                mixer_hi(b)
            for t in range(TT):
                if t >= 5:
                    for n in range(max(2 * t - 11, 0), 2 * t - 9):
                        take_uT(1, n)
                act.wait_ge(added, 16 * (OUT_BLOCKS - 1) + 2 * t + 2)
                rms(1, t)
            for n in (5, 6, 7):
                take_uT(1, n)
            activations(None, 0, UT_SPREAD)
            with act.Fori(0, MLP_TURNS, 1) as r:
                activations(r, 1)
                activations(r, 2)
            activations(None, LAST)

        @block.vector
        def _(dve):
            own = [0]

            def step(ins):
                ins.then_inc(dve_own, 1)
                own[0] += 1
                dve.wait_ge(dve_own, own[0])

            def normalise_tokens(norm, t):
                src, dst = ((x_tok, x_tok), (resid, u_tok))[norm]
                dve.wait_ge(sq_done, TT * norm + t + 1)
                dve.tensor_scalar(dst[:, t, :], src[:, t, :], rstd[:, norm, t:t + 1], None, ALU.mult).then_inc(u_ready, 1)

            def take_uT(norm, n):
                k, half = n % KT, n // KT
                dve.wait_ge(uT_act, 16 * norm + n + 1)
                cols = slice(half * HALF, half * HALF + HALF)
                dve.scalar_tensor_tensor(uT_lo[:, k, cols], uT_bank(norm, n)[:, :], norm_w[:, norm, k:k + 1],
                                         uT_hi[:, k, cols].bitcast(F32), ALU.mult, ALU.subtract).then_inc(uT_dve, 1)

            def value_lo(n):
                b = bank[n % 2]
                dve.wait_ge(unit_act, act_hands(n) + 1)
                dve.tensor_tensor(vs[:, n % 2, 1, :].bitcast(F32R), b[:, 0:256], vs[:, n % 2, 0, :],
                                  ALU.subtract).then_inc(dve_freed, 1)

            def clamp_gate(n):
                kind = UNITS[n][0]
                if kind in ("ff", "fb", "hg"):
                    dve.wait_ge(proj_done, n + 1)
                    ins = dve.tensor_scalar(gate_t[:, :], bank[n % 2][:, :], GATE_MIN, None, ALU.max)
                    if kind == "hg":
                        ins.then_inc(unit_dve, 1)
                    else:
                        ins.then_inc(dve_freed, 1)

            def finish_gate(n):
                kind, what, part = UNITS[n]
                cols = slice(part * HALF, part * HALF + HALF)
                if kind in ("ff", "fb"):
                    d = ("ff", "fb").index(kind)
                    cum = h_cum(what, d)[:, cols]
                    dve.wait_ge(unit_act, act_hands(n) + 1)
                    step(dve.tensor_scalar(cum, cum, LOG_F_MIN, None, ALU.max))
                    dve.tensor_scalar(h_key(what, d)[:, cols], gate_t[:, :], lb_neg[:, d, what:what + 1],
                                      lb_rest[:, d, what:what + 1], ALU.mult, ALU.add).then_inc(unit_dve, 1)
                    dve.wait_ge(unit_dve, dve_hands(n) + 1)
                    if part == 1:
                        t = h_cum(what, d)
                        if d == 0:
                            step(dve.tensor_tensor_scan(t, scan_mask[:, 0:S], t, 0.0, ALU.mult, ALU.add))
                        else:
                            step(dve.tensor_tensor_scan(t[:, ::-1], scan_mask[:, 1:S + 1][:, ::-1], t[:, ::-1], 0.0,
                                                        ALU.mult, ALU.add))
                elif kind == "hg":
                    dve.wait_ge(unit_act, act_hands(n) + 1)
                    dve.tensor_tensor(h_gate[:, cols], bank[n % 2][:, :], gate_t[:, :], ALU.mult).then_inc(dve_freed, 1)
                    dve.wait_ge(*freed(n))

            def qk_product(n):
                c = "qk".index(UNITS[n][0])
                dve.wait_ge(unit_act, act_hands(n) + 1)
                if n > FIRST_QK:
                    dve.wait_ge(qk_ready, qk_count(n - 1))
                dve.scalar_tensor_tensor(qk_t[:, 2, :], bank[n % 2][:, :], qk_w[:, c:c + 1], qk_t[:, 1, :],
                                         ALU.mult, ALU.mult).then_inc(dve_freed, 1)

            def qk_lo(n):
                kind, p, part = UNITS[n]
                dve.wait_ge(*freed(n))
                dve.wait_ge(unit_act, act_hands(n + 1))
                if kind == "k":
                    cols = slice(part * HALF, part * HALF + HALF)
                    dve.tensor_tensor(k_lo[:, p % 2, cols], qk_t[:, 2, :], k_hi[:, p % 2, cols].bitcast(F32),
                                      ALU.subtract).then_inc(qk_ready, 1)
                else:
                    for g2 in range(2):
                        for h in range(2):
                            dve.tensor_tensor(q_place(q_lo, p, 2 * part + g2, h), q_source(g2, h),
                                              q_place(q_hi, p, 2 * part + g2, h).bitcast(F32),
                                              ALU.subtract).then_inc(qk_ready, 1)

            def build_bias(s):
                p, n = divmod(s, NB)
                if n == 2:
                    return
                k = BAND_CLASS[n]
                if n == 0:
                    dve.wait_ge(rpb_load, 16 * 8 * (p + 1))
                if s:
                    dve.wait_ge(masked, NG * s)
                win = rpb_win[:, :].rearrange("p (r c) -> p r c", c=RPB_PITCH)
                c0 = 16 + CLASS_SHIFT[k]
                for a, b, u in ((0, 8, 4), (8, 20, 0), (20, 28, 0)):
                    dve.scalar_tensor_tensor(bias[:, a:b, :], na_mask[:, k, a:b, :], BIG,
                                             win[:, u:u + b - a, c0:c0 + BAND], ALU.mult, ALU.subtract).then_inc(bias_done, 1)

            def mask_scores(s, g):
                i = NG * s + g
                w = TILE_W[g]
                if g == 0:
                    dve.wait_ge(bias_done, 3 * (3 * (s // NB) + (1, 2, 2, 3)[s % NB]))
                    if s >= 2:
                        dve.wait_ge(pT_done, NG * (s - 1))
                dve.wait_ge(score_done, i + 1)
                dve.tensor_tensor_reduce(probs[:, s % 2, TILE_OFF[g]:TILE_OFF[g] + w], bank[2 + i % 2][:, 0:w],
                                         bias[:, :, :].rearrange("p r c -> p (r c)")[:, BIAS_OFF[g]:BIAS_OFF[g] + w],
                                         1.0, 3e38, ALU.add, ALU.min, s_min[:, i:i + 1]).then_inc(masked, 1)

            def normalise_probs(s, g0):
                i = NG * s + g0
                dve.wait_ge(exp_done, i + 2)
                step(dve.reciprocal(s_inv[:, i:i + 2], s_sum[:, i:i + 2]))
                for g in (g0, g0 + 1):
                    t = probs[:, s % 2, TILE_OFF[g]:TILE_OFF[g] + TILE_W[g]]
                    dve.tensor_scalar(t, t, s_inv[:, NG * s + g:NG * s + g + 1], None, ALU.mult).then_inc(prob_done, 1)

            def take_pT(s, kg):
                i = NG * s + kg
                w = P * len(KG_GROUPS[kg])
                dve.wait_ge(pT_act, i + 1)
                dve.tensor_tensor(pT_lo[:, i % 2, 0:w], bank[4 + i % 2][:, 0:w], pT_hi[:, i % 2, 0:w].bitcast(F32),
                                  ALU.subtract).then_inc(pT_dve, 1)

            def halves(t, size):
                v = t.rearrange("p (b s) -> p b s", s=size)
                return v[:, :, 0:size // 2], v[:, :, size // 2:]

            def z_arguments(h, i):
                if not ARG_STEPS[i]:
                    return
                t = z_turn(h, i)
                zk, zq = zz[:, t, 0, :], zz[:, t, 1, :]
                f, b = h_cum(h, 0), h_cum(h, 1)
                operands_free(dve, h, i)
                if i < 4:
                    size = LEVELS[i]
                    (fl, fr), (bl, br) = halves(f, size), halves(b, size)
                    (kl, kr), (ql, qr) = halves(zk, size), halves(zq, size)
                    shape = [P, S // size, size // 2]
                    f_mid = fl[:, :, size // 2 - 1:size // 2].to_broadcast(shape)
                    b_mid = br[:, :, 0:1].to_broadcast(shape)
                    todo = [(kl, f_mid, fl), (qr, fr, f_mid), (kr, b_mid, br), (ql, bl, b_mid)]
                elif i < 6:
                    src, mid = ((f, 3), (b, 4))[i - 4]
                    v, vk, vq = (a.rearrange("p (b s) -> p b s", s=8) for a in (src, zk, zq))
                    m = v[:, :, mid:mid + 1].to_broadcast([P, S // 8, 8])
                    todo = [(vk, m, v), (vq, v, m)]
                else:
                    fv, bv, v0, v1 = (a.rearrange("p (b s) -> p b s", s=CHUNK) for a in (f, b, zk, zq))
                    shape = [P, NCH, CHUNK]
                    todo = [(v0, fv[:, :, CHUNK - 1:CHUNK].to_broadcast(shape), fv), (v1, bv[:, :, 0:1].to_broadcast(shape), bv)]
                for dst, a, b in todo:
                    dve.tensor_tensor(dst, a, b, ALU.subtract).then_inc(z_arg, 1)

            def z_products(h, i):
                t = z_turn(h, i)
                zk, zq = zz[:, t, 0, :], zz[:, t, 1, :]
                q, kf, kb = h_q[:, h % 2, :], h_key(h, 0), h_key(h, 1)
                if i == 0:
                    dve.wait_ge(*freed(UNIT[("hq", h, 1)]))
                if i == 6:
                    operands_free(dve, h, i)
                    dve.tensor_tensor(zk, kf, kb, ALU.add).then_inc(z_ready, 1)
                    return
                dve.wait_ge(z_exp, 8 * h + (i if i < 6 else i - 1) + 1)
                if i < 4:
                    kl, kr = halves(zk, LEVELS[i])
                    dve.tensor_tensor(kl, kl, halves(kf, LEVELS[i])[0], ALU.mult).then_inc(z_ready, 1)
                    dve.tensor_tensor(kr, kr, halves(kb, LEVELS[i])[1], ALU.mult).then_inc(z_ready, 1)
                    dve.tensor_tensor(zq, zq, q, ALU.mult).then_inc(z_ready, 1)
                elif i < 6:
                    dve.tensor_tensor(zk, zk, (kf, kb)[i - 4], ALU.mult).then_inc(z_ready, 1)
                    dve.tensor_tensor(zq, zq, q, ALU.mult).then_inc(z_ready, 1)
                elif i == 7:
                    dve.tensor_tensor(zz[:, t, :, :], zz[:, t, :, :], h_gates[:, h % 2, 2:4, :], ALU.mult).then_inc(z_ready, 1)
                else:
                    dve.tensor_tensor(zk, zk, q, ALU.mult).then_inc(z_ready, 1)
                    dve.tensor_tensor(zq, zq, q, ALU.mult).then_inc(z_ready, 1)

            def take_level(h, i):
                for cg in range(2):
                    n = 2 * (NLEV * h + i) + cg
                    dve.wait_ge(lev_done, n + 1)
                    if i == 0:
                        if h:
                            dve.wait_ge(o_done, 2 * h)
                    else:
                        dve.wait_ge(lev_taken, n - 1)
                    dve.copy_predicated(scores[:, 4 * cg:4 * cg + 4, :],
                                        hg_mask[:, i:i + 1, :].to_broadcast([P, 4, P]),
                                        bank[2 + cg][:, :].rearrange("p (c i) -> p c i", c=4)).then_inc(lev_taken, 1)

            def chain_states(h):
                dve.wait_ge(g_ready, h + 1)
                if h:
                    dve.wait_ge(o_done, 2 * h)
                for d in range(2):
                    for j in range(2):
                        chunks = (((0, 1, 2, 3), (4, 5, 6)), ((7, 6, 5, 4), (3, 2, 1)))[d][j]
                        dve.wait_ge(upd_done, 4 * h + 2 * d + j + 1)
                        for k, c in enumerate(chunks):
                            src = bank[4 + 2 * d + j][:, P * k:P * k + P]
                            dst = state[:, d, c - d, :]
                            if c == (0, 7)[d]:
                                ins = dve.tensor_copy(dst, src)
                            else:
                                last = state[:, d, c - 1 if d == 0 else c, :]
                                ins = dve.scalar_tensor_tensor(dst, last, g_chunk[:, d, c:c + 1], src, ALU.mult, ALU.add)
                            if k < len(chunks) - 1:
                                step(ins)
                        ins.then_inc(st_done, 1)
                        dve.wait_ge(st_done, 4 * h + 2 * d + j + 1)

            def head_result(h):
                for part in range(2):
                    n = 2 * h + part
                    dve.wait_ge(o_rs, n + 1)
                    dve.scalar_tensor_tensor(tmp[:, part, :], bank[6 + part][:, :], gnorm[:, 0:1],
                                             tmp[:, part, :], ALU.mult, ALU.mult).then_inc(o_norm, 1)
                for part in range(2):
                    n = 2 * h + part
                    dve.wait_ge(o_norm, n + 1)
                    y = mixer_tile(PAIRS + h)[:, 4 * part:4 * part + 4, :]
                    cols = slice(part * HALF, part * HALF + HALF)
                    dve.tensor_tensor(y, tmp[:, part, :].rearrange("p (c i) -> p c i", i=P),
                                      h_gate[:, cols].rearrange("p (c i) -> p c i", i=P), ALU.mult).then_inc(y_done, 1)

            def mixer_lo(b):
                for f in range(FBLK):
                    k = FBLK * b + f
                    dve.wait_ge(m_hi, k + 1)
                    hi, lo, src = acts[:, b % 2, 0, f, :], acts[:, b % 2, 1, f, :], mixer_tile(k)
                    if b >= 2:
                        hi, lo = (a.rearrange("p (c i) -> p c i", i=P) for a in (hi, lo))
                    dve.tensor_tensor(lo, src, hi.bitcast(F32), ALU.subtract).then_inc(m_lo, 1)

            dve.memset(eps_col[:, :], EPS).then_inc(ready_cols, 1)
            dve.memset(one_col[:, :], 1.0).then_inc(ready_cols, 1)
            for t in range(TT):
                if t == 4:
                    dve.wait_ge(c_load, CONSTS)
                if t >= 4:
                    take_uT(0, 2 * t - 8)
                    take_uT(0, 2 * t - 7)
                normalise_tokens(0, t)
            dve.tensor_tensor(lb[:, :, :], lb_raw[:, :, 1, :], lb_raw[:, :, 0, :], ALU.subtract).then_inc(lb_diff, 1)
            dve.wait_ge(lb_exp, 1)
            step(dve.tensor_scalar(lb[:, :, :], lb[:, :, :], BIG, 1.0, ALU.min, ALU.add))
            step(dve.reciprocal(lb[:, :, :], lb[:, :, :]))
            step(dve.tensor_scalar(lb_rest[:, :, :], lb[:, :, :], -1.0, 1.0, ALU.mult, ALU.add))
            step(dve.tensor_scalar(lb_neg[:, :, :], lb[:, :, :], 1.0, None, ALU.subtract))
            dve.tensor_scalar(qk_w[:, 0:1], qk_w[:, 0:1], -float(NA_DIM) ** -0.5, None, ALU.mult).then_inc(params, 1)
            dve.wait_ge(params, 1)
            dve.wait_ge(mask_load, 48)
            for n in range(FIRST_QK):
                value_lo(n)
                if n < 4:
                    take_uT(0, KT + 2 * n)
                    take_uT(0, KT + 2 * n + 1)
                if n == 6:
                    dve.wait_ge(uT_done, 16)
                    step(dve.memset(q_hi[:, :, :, :, :].bitcast(F32), 0.0))
                if n == 8:
                    dve.memset(q_lo[:, :, :, :, :].bitcast(F32), 0.0).then_inc(cleared, 1)
            for n in range(FIRST_QK, BEFORE - 1):
                qk_product(n)
                qk_lo(n)
            for s in range(-2, STEPS):
                qk = BEFORE + s if -1 <= s <= 9 else None
                if s >= 0:
                    take_pT(s, 0)
                    take_pT(s, 1)
                if qk is not None:
                    qk_product(qk)
                if s + 2 < STEPS:
                    build_bias(s + 2)
                if s >= 0:
                    take_pT(s, 2)
                    take_pT(s, 3)
                if s + 2 < STEPS:
                    for g in range(NG):
                        mask_scores(s + 2, g)
                    normalise_probs(s + 2, 0)
                if qk is not None:
                    qk_lo(qk)
                if s + 2 < STEPS:
                    normalise_probs(s + 2, 2)
            hgrn_may_start(dve)
            for n in FIRST_HEAD:
                if UNITS[n][0] in ("ff", "fb"):
                    clamp_gate(n)
                    finish_gate(n)
            z_arguments(0, 0)
            z_arguments(0, 1)
            z_products(0, 0)
            last = []
            for h in range(HG_HEADS):
                for i in range(PIECES):
                    for n in last:
                        clamp_gate(n)
                    if i < NLEV:
                        take_level(h, i)
                    if after(h, i, 1)[0] < HG_HEADS:
                        z_products(*after(h, i, 1))
                    if i == 0 and h:
                        head_result(h - 1)
                    for n in last:
                        finish_gate(n)
                    if i == 7:
                        chain_states(h)
                    if after(h, i, 2)[0] < HG_HEADS:
                        z_arguments(*after(h, i, 2))
                    last = HEAD_UNITS[h][i]
            mixer_lo(0)
            head_result(HG_HEADS - 1)
            def add_bank(i, bank0):
                t, half = divmod(i, 2)
                r = resid[:, t, half * HALF:half * HALF + HALF]
                dve.tensor_tensor(r, r, bank[bank0 + i % 4][:, :], ALU.add).then_inc(added, 1)

            for b in range(OUT_BLOCKS):
                for i in range(2 * TT):
                    if b == 0 and i % 2 == 0:
                        dve.wait_ge(resid_load[i // 2], 16)
                    if b + 1 < OUT_BLOCKS and i == 8:
                        mixer_lo(b + 1)
                    dve.wait_ge(down_done, 16 * b + i + 1)
                    if b:
                        dve.wait_ge(added, 16 * (b - 1) + i + 1)
                    add_bank(i, 0)
                    if b == OUT_BLOCKS - 1 and i >= 3 and i % 2:
                        normalise_tokens(1, (i - 3) // 2)
                    if b == OUT_BLOCKS - 1 and i >= 10:
                        take_uT(1, i - 10)
            normalise_tokens(1, TT - 1)
            take_uT(1, 6)
            take_uT(1, 7)

            def activations(r, j, spread=()):
                for i, (f, half) in enumerate(up_order(j)):
                    cols = slice(half * HALF, half * HALF + HALF)
                    relu, a = u_tok[:, i, 0:HALF], u_tok[:, i, HALF:D]
                    dve.wait_ge(relu_done, count(r, 8, 4 * j + i + 1))
                    dve.tensor_tensor(a, relu, relu, ALU.mult).then_inc(sqr_done, 1)
                    dve.wait_ge(sqr_done, count(r, 8, 4 * j + i + 1))
                    dve.wait_ge(a_hi, count(r, 8, 4 * j + i + 1))
                    dve.tensor_tensor(acts[:, j % 2, 1, f, cols], a, acts[:, j % 2, 0, f, cols].bitcast(F32),
                                      ALU.subtract).then_inc(a_lo, 1)
                    for n in (spread[i] if spread else ()):
                        take_uT(1, n)

            def add_block(r, j):
                for i in range(2 * TT):
                    dve.wait_ge(down_done, count(r, 32, 16 * (OUT_BLOCKS + j) + i + 1))
                    dve.wait_ge(added, count(r, 32, 16 * (OUT_BLOCKS + j - 1) + i + 1))
                    add_bank(i, 4)

            activations(None, 0, UT_SPREAD)
            with dve.Fori(0, MLP_TURNS, 1) as r:
                activations(r, 1)
                add_block(r, 0)
                activations(r, 2)
                add_block(r, 1)
            activations(None, LAST)
            add_block(None, LAST - 1)
            add_block(None, LAST)

        @block.tensor
        def _(pe):
            def product(dst, a, b, first=True, last=True, skip=False):
                pe.matmul(dst, a[0], b[0], start=first, stop=False, skip_group_check=skip)
                pe.matmul(dst, a[0], b[1], start=False, stop=False, skip_group_check=skip)
                return pe.matmul(dst, a[1], b[0], start=False, stop=last, skip_group_check=skip)

            ring = (w_hi, w_lo)
            uT = (uT_hi, uT_lo)

            def transpose_tokens(norm, n):
                k, half = n % KT, n // KT
                src = (x_tok, u_tok)[norm]
                b = uT_bank(norm, n)
                if norm and half:
                    pe.wait_ge(uT_dve, 16 + max(n - 3, 8))
                elif n >= 2:
                    pe.wait_ge(uT_dve, 16 * norm + n - 1)
                pe.wait_ge(u_ready, TT * norm + 4 * half + 4)
                for t in range(4):
                    ins = pe.transpose(b[:, P * t:P * t + P], src[:, 4 * half + t, P * k:P * k + P], ident)
                ins.then_inc(uT_done, 1)

            def projection(n, ks=range(KT)):
                kind, what, part = UNITS[n]
                if n >= 2 and ks[0] == 0:
                    pe.wait_ge(*freed(n - 2))
                b = bank[n % 2]
                done = 0
                if n:
                    k1, _, p1 = UNITS[n - 1]
                    done = 2 * (p1 == TT - 1) if k1 in ("v", "hv") else int(p1 == 1)
                if kind in ("v", "hv"):
                    tile = TILE_OF[("in", (C_V if kind == "v" else C_HV) + 256 * what)]
                    pe.wait_ge(w_split, 2 * (tile + 2))
                    pe.wait_ge(uT_dve, 8 if part < 4 else 16)
                    r = tile % RING
                    for k in ks:
                        a = [t[:, k, P * part:P * part + P] for t in uT]
                        w = [t[:, r:r + 2, P * k:P * k + P] for t in ring]
                        dst = b[:, 0:256]
                        first = pe.matmul(dst, a[0], w[0], start=k == 0, stop=False)
                        if k == 0 and done:
                            first.then_inc(w_used, done)
                        pe.matmul(dst, a[0], w[1], start=False, stop=False)
                        ins = pe.matmul(dst, a[1], w[0], start=False, stop=k == KT - 1)
                else:
                    tile = TILE_OF[("in", COL[kind] + P * what)]
                    pe.wait_ge(w_split, 2 * (tile + 1))
                    pe.wait_ge(uT_dve, 16)
                    r = tile % RING
                    for k in ks:
                        w = [t[:, r, P * k:P * k + P] for t in ring]
                        u = [t[:, k, part * HALF:part * HALF + HALF] for t in uT]
                        first = pe.matmul(b[:, :], w[0], u[0], start=k == 0, stop=False)
                        if k == 0 and done:
                            first.then_inc(w_used, done)
                        pe.matmul(b[:, :], w[0], u[1], start=False, stop=False)
                        ins = pe.matmul(b[:, :], w[1], u[0], start=False, stop=k == KT - 1)
                if ks[-1] == KT - 1:
                    ins.then_inc(proj_done, 1)

            def qk_average(n):
                pe.wait_ge(qk_sq, n - FIRST_QK + 1)
                if n > FIRST_QK:
                    pe.wait_ge(unit_act, act_hands(n - 1) + 1)
                pe.matmul(bank[7][:, :], head_mean, qk_t[:, 0, :], start=True, stop=True).then_inc(qk_mean, 1)

            def score_tiles(s, groups):
                p, n = divmod(s, NB)
                if s >= STEPS:
                    return
                pe.wait_ge(qk_ready, qk_count(UNIT[("k", p, 1)]))
                for g in groups:
                    i = NG * s + g
                    if i >= 2:
                        pe.wait_ge(masked, i - 1)
                    rows = slice(KEY_ROW0[g], KEY_ROW0[g] + KEY_ROWS[g])
                    cols = slice(BAND_START[n], BAND_START[n] + BAND)
                    keys = [t[:, p % 2, :].rearrange("p (r c) -> p r c", c=GRID)[:, rows, cols] for t in (k_hi, k_lo)]
                    product(bank[2 + i % 2][:, 0:TILE_W[g]], [t[:, p % 2, g, n, :] for t in (q_hi, q_lo)],
                            keys).then_inc(score_done, 1)

            def transpose_probs(s, kg):
                i = NG * s + kg
                pe.wait_ge(prob_done, NG * s + KG_GROUPS[kg][-1] + 1)
                if i >= 2:
                    pe.wait_ge(pT_dve, i - 1)
                for j, g in enumerate(KG_GROUPS[kg]):
                    at = TILE_OFF[g] + P * (kg - KG0[g])
                    ins = pe.transpose(bank[4 + i % 2][:, P * j:P * j + P], probs[:, s % 2, at:at + P], ident)
                ins.then_inc(pT_done, 1)

            def times_values(s, kg):
                i = NG * s + kg
                g0, w = KG_GROUPS[kg][0], P * len(KG_GROUPS[kg])
                pe.wait_ge(pT_dve, i + 1)
                if kg == 0:
                    pe.wait_ge(v_load[s % 2], 16 * 8 * (s // 2 + 1))
                    if s:
                        pe.wait_ge(mix_done, 2 * s)
                product(bank[6][:, P * g0:P * g0 + w], [t[:, s % 2, kg, :] for t in (v_hi, v_lo)],
                        [t[:, i % 2, 0:w] for t in (pT_hi, pT_lo)], first=kg == 0, last=kg == NG - 1,
                        skip=True).then_inc(pv_done, 1)

            def chunk(t, c):
                return t[:, P * c:P * c + P]

            def level(h, i):
                t = z_turn(h, i)
                pe.wait_ge(z_ready, steps_to(PRODUCT_STEPS, h, i))
                for cg in range(2):
                    n = 2 * (NLEV * h + i) + cg
                    if n >= 2:
                        pe.wait_ge(lev_taken, n - 1)
                    else:
                        pe.wait_ge(masked, NG * STEPS)
                    for c in range(4 * cg, 4 * cg + 4):
                        q = h_q[:, h % 2, :] if i == 6 else zz[:, t, 1, :]
                        ins = pe.matmul(bank[2 + cg][:, P * (c % 4):P * (c % 4) + P], chunk(zz[:, t, 0, :], c),
                                        chunk(q, c), start=True, stop=True)
                    ins.then_inc(lev_done, 1)

            def chunk_products(h, share):
                t = z_turn(h, 7)
                pe.wait_ge(z_ready, steps_to(PRODUCT_STEPS, h, 7))
                for d in range(2):
                    if h:
                        pe.wait_ge(*((o_rs, 2 * h), (o_norm, 2 * h))[d])
                    elif d == 0:
                        pe.wait_ge(pT_dve, NG * STEPS)
                    else:
                        pe.wait_ge(mix_done, 2 * STEPS)
                        pe.wait_ge(unit_act, act_hands(UNIT[("hv", 0, 0)]))
                    for cg in range(2):
                        for c in range(4 * cg, 4 * cg + 4):
                            ins = pe.transpose(bank[4 + 2 * d + cg][:, P * (c % 4):P * (c % 4) + P],
                                               chunk(zz[:, t, d, :], c), ident)
                        ins.then_inc(kT_done, 1)
                for d in range(2):
                    share(2 * d)
                    pe.wait_ge(kT_act, 4 * h + 2 * d + 2)
                    for j in range(2):
                        for k, c in enumerate((((0, 1, 2, 3), (4, 5, 6)), ((7, 6, 5, 4), (3, 2, 1)))[d][j]):
                            ins = pe.matmul(bank[4 + 2 * d + j][:, P * k:P * k + P], chunk(k_tok, c),
                                            h_v[:, c, P * h:P * h + P], start=True, stop=True)
                        ins.then_inc(upd_done, 1)
                    share(2 * d + 1)

            def head_outputs(h):
                t = z_turn(h, 8)
                pe.wait_ge(z_ready, steps_to(PRODUCT_STEPS, h, 8))
                pe.wait_ge(st_done, 4 * (h + 1))
                pe.wait_ge(lev_taken, 2 * NLEV * (h + 1))
                for part in range(2):
                    for c in range(4 * part, 4 * part + 4):
                        dst = bank[6 + part][:, P * (c % 4):P * (c % 4) + P]
                        pe.matmul(dst, h_v[:, c, P * h:P * h + P], scores[:, c, :], start=True, stop=False)
                        if c >= 1:
                            ins = pe.matmul(dst, state[:, 0, c - 1, :], chunk(zz[:, t, 0, :], c), start=False, stop=c == 7)
                        if c <= 6:
                            ins = pe.matmul(dst, state[:, 1, c, :], chunk(zz[:, t, 1, :], c), start=False, stop=True)
                    ins.then_inc(o_done, 1)

            def head_means(h):
                for part in range(2):
                    pe.wait_ge(o_sq, 2 * h + part + 1)
                    pe.matmul(bank[4 + part][:, :], all_mean, tmp[:, part, :], start=True, stop=True).then_inc(o_mean, 1)

            pe.wait_ge(c_load, CONSTS)
            for n in range(KT):
                transpose_tokens(0, n)
            for n in range(FIRST_QK + 1):
                projection(n)
                if n < 4:
                    transpose_tokens(0, KT + 2 * n)
                    transpose_tokens(0, KT + 2 * n + 1)
            for n in range(FIRST_QK + 1, BEFORE):
                projection(n)
                qk_average(n - 1)
            for s in range(-2, STEPS):
                def share(i):
                    if s in STEP_UNIT:
                        projection(STEP_UNIT[s], range(2 * i, 2 * i + 2))

                if s >= 0:
                    transpose_probs(s, 0)
                    transpose_probs(s, 1)
                if -1 <= s <= 9:
                    qk_average(BEFORE + s)
                share(0)
                if s >= 0:
                    times_values(s, 0)
                    transpose_probs(s, 2)
                share(1)
                if s >= 0:
                    times_values(s, 1)
                    transpose_probs(s, 3)
                score_tiles(s + 2, (0, 1))
                share(2)
                if s >= 0:
                    times_values(s, 2)
                score_tiles(s + 2, (2,))
                share(3)
                if s >= 0:
                    times_values(s, 3)
                score_tiles(s + 2, (3,))
            for n in FIRST_HEAD:
                projection(n)
            for h in range(HG_HEADS):
                for i in range(PIECES):
                    units = HEAD_UNITS[h][i]
                    if i < NLEV:
                        level(h, i)
                        if i == 0 and h:
                            head_means(h - 1)
                        for n in units:
                            projection(n)
                    elif i == 7:
                        chunk_products(h, lambda q: [projection(n, range(2 * q, 2 * q + 2)) for n in units])
                    else:
                        head_outputs(h)

            def add_product(i, turn, place, bank0, finished, free):
                t, half = divmod(i, 2)
                pe.wait_ge(added, free)
                dst = bank[bank0 + i % 4][:, :]
                for f in range(FBLK):
                    a = [acts[:, turn, x_, f, P * t:P * t + P] for x_ in range(2)]
                    w = [x_[:, place + f, half * HALF:half * HALF + HALF] for x_ in ring]
                    first = pe.matmul(dst, a[0], w[0], start=f == 0, stop=False)
                    if f == 0 and finished:
                        first.then_inc(w_used, finished)
                    pe.matmul(dst, a[0], w[1], start=False, stop=False)
                    ins = pe.matmul(dst, a[1], w[0], start=False, stop=f == FBLK - 1)
                ins.then_inc(down_done, 1)

            pe.wait_ge(*freed(len(UNITS) - 1))
            for b in range(OUT_BLOCKS):
                pe.wait_ge(w_split, 2 * (N_IN + FBLK * (b + 1)))
                pe.wait_ge(m_lo, FBLK * (b + 1))
                for i in range(2 * TT):
                    if b == 0 and i == 4:
                        head_means(HG_HEADS - 1)
                    add_product(i, b % 2, FBLK * b % RING, 0, (1 if b == 0 else FBLK) if i == 0 else 0,
                                max(16 * b + i - 3, 0))
                    if b == OUT_BLOCKS - 1 and i >= 10:
                        transpose_tokens(1, i - 10)
            transpose_tokens(1, 6)
            transpose_tokens(1, 7)

            def up(r, j, spread=None):
                place = 2 if j else 0
                for i, (f, half) in enumerate(up_order(j)):
                    if j:
                        pe.wait_ge(relu_done, count(r, 8, 4 * j))
                        pe.wait_ge(w_split, count(r, 16, 2 * (len(TILES) + 4 * j - 2 + f + 1)))
                    else:
                        pe.wait_ge(added, 16 * OUT_BLOCKS)
                        pe.wait_ge(w_split, 2 * (len(TILES) + f + 1))
                        pe.wait_ge(uT_dve, 16 + (8 if half == 0 else 16))
                    dst = bank[2 * f + half][:, :]
                    for k in range(KT):
                        w = [t[:, place + f, P * k:P * k + P] for t in ring]
                        u = [t[:, k, half * HALF:half * HALF + HALF] for t in uT]
                        first = pe.matmul(dst, w[0], u[0], start=k == 0, stop=False)
                        if k == 0 and i == 0:
                            first.then_inc(w_used, FBLK)
                        if k == 0 and j and (f, half) == (1, 0):
                            first.then_inc(w_used, 1)
                        pe.matmul(dst, w[0], u[1], start=False, stop=False)
                        ins = pe.matmul(dst, w[1], u[0], start=False, stop=k == KT - 1)
                        if not j and k == KT // 2 - 1 and i == 1:
                            for n in UT_SPREAD[1]:
                                transpose_tokens(1, n)
                    ins.then_inc(up_done, 1)
                    if not j and i == 0:
                        for n in UT_SPREAD[0]:
                            transpose_tokens(1, n)

            def down(r, j):
                last = r is None and j == LAST
                pe.wait_ge(a_lo, count(r, 8, 4 * (j + 1)))
                pe.wait_ge(w_split, count(r, 16, 2 * (len(TILES) + 4 * j + (4 if last else 6))))
                for i in range(2 * TT):
                    add_product(i, j % 2, 2 if last else 0, 4, 1 if i == 0 else 0,
                                count(r, 32, 16 * (OUT_BLOCKS + j) + i - 3))

            up(None, 0)
            with pe.Fori(0, MLP_TURNS, 1) as r:
                up(r, 1)
                down(r, 0)
                up(r, 2)
                down(r, 1)
            up(None, LAST)
            down(None, LAST - 1)
            down(None, LAST)


_INS = ["x", "w_in", "w_out", "attn_norm_w", "mlp_norm_w", "q_norm_w", "k_norm_w", "rpb", "hg_norm_w",
        "lb_fwd", "lb_bwd", "w_up", "w_down"]


def kernel(**inputs):
    import numpy as _np
    import concourse.bacc as _bacc
    from concourse import mybir as _mybir
    from concourse.bass_utils import run_bass_kernel_spmd as _run

    nc = _bacc.Bacc("TRN2", target_bir_lowering=False, num_devices=1)
    data = {name: _np.ascontiguousarray(inputs[name]) for name in _INS}
    rpb = _np.zeros((NA_HEADS, 16, 15, RPB_PITCH), data["rpb"].dtype)
    for c in range(16):
        rpb[:, c, :, 1 + c:32 + c] = data["rpb"][0]
    data["rpb"] = rpb
    data["tables"], data["masks"] = shape_tables()
    arrays, args = {}, []
    for name, a in data.items():
        arrays[f"in_{name}"] = a
        args.append(nc.dram_tensor(f"in_{name}", a.shape, _mybir.dt.from_np(a.dtype), kind="ExternalInput").ap())
    out = nc.dram_tensor("out_0", (1, S, D), F32, kind="ExternalOutput").ap()
    hybrid_block(nc, *args, out)
    r = _run(nc, [arrays], core_ids=[0])
    return r.results[0]["out_0"]
```

```python
from contextlib import ExitStack

import numpy as np
import concourse.bass as bass
from concourse import mybir

F32 = mybir.dt.float32
F32R = mybir.dt.float32r
U8 = mybir.dt.uint8
I32 = mybir.dt.int32
ALU = mybir.AluOpType
ACT = mybir.ActivationFunctionType

P = 128
D = 1024
S = 1024
KT = D // P
TT = S // P
HALF = 512
NA_HEADS, NA_DIM = 8, 64
PAIRS = NA_HEADS // 2
GRID = 64
NG, NB = 4, 4
BAND = 32
BAND_START = [0, 8, 24, 32]
BAND_CLASS = [0, 1, 1, 2]
CLASS_SHIFT = [0, -8, -16]
KEY_ROW0 = [0, 0, 4, 8]
KEY_ROWS = [8, 12, 12, 8]
MASK_ROW0 = [4, 0, 0, 0]
TILE_W = [r * BAND for r in KEY_ROWS]
TILE_OFF = [0, 256, 640, 1024]
STEP_W = 1280
KG_GROUPS = [(0, 1), (0, 1, 2), (1, 2, 3), (2, 3)]
KG0 = [0, 0, 1, 2]
STEPS = PAIRS * NB
BIAS_ROWS = 28
BIAS_OFF = [0, 8 * BAND, 8 * BAND, 20 * BAND]
RPB_PITCH = 64
HG_HEADS = 4
CHUNK = 128
NCH = S // CHUNK
LEVELS = [128, 64, 32, 16]
NLEV = 7
EPS = 1e-6
BIG = 1e30
LOG_F_MIN = -18.0
GATE_MIN = -41.0
RING, STAGE = 4, 2
FBLK = 2
MLP_BLOCKS = 4 * D // P // FBLK
OUT_BLOCKS = KT // FBLK
LAST = MLP_BLOCKS - 1
MLP_TURNS = (MLP_BLOCKS - 2) // 2
C_Q, C_K, C_V, C_HQ, C_FF, C_FB, C_HV, C_HG = [512 * i for i in range(8)]
M_HG, M_NA, M_SCAN = 0, NLEV * P, NLEV * P + 3 * BIAS_ROWS * BAND
M_END = M_SCAN + S + 4


def shape_tables():
    f = np.zeros((P, 3 * P), np.float32)
    f[:, 0:P] = np.eye(P)
    for h in range(2):
        f[64 * h:64 * h + 64, P + 64 * h:P + 64 * h + 64] = 1.0 / 64
    f[:, 2 * P:] = 1.0 / P
    m = np.zeros((P, M_END), np.uint8)
    j, i = np.arange(P)[:, None], np.arange(P)[None, :]
    for n, b in enumerate(LEVELS):
        m[:, n * P:(n + 1) * P] = (j // b == i // b) & (j // (b // 2) != i // (b // 2))
    m[:, 4 * P:5 * P] = (j // 8 == i // 8) & (j < i)
    m[:, 5 * P:6 * P] = (j // 8 == i // 8) & (j > i)
    m[:, 6 * P:7 * P] = j == i
    p = np.arange(P)
    rr, c = (p % 64 // 16)[:, None, None], (p % 16)[:, None, None]
    col = np.arange(BAND)[None, None, :]
    for k, n in enumerate([0, 1, 3]):
        first = np.clip(16 * n + c - 8, 0, GRID - 16) - BAND_START[n]
        out_col = (col < first) | (col >= first + 16)
        u = np.arange(12)[None, :, None]
        row_in = (u - rr >= 0) & (u - rr <= 7)
        parts = [np.broadcast_to(out_col, (P, 8, BAND)), out_col | ~row_in,
                 np.broadcast_to(out_col, (P, 8, BAND))]
        at = M_NA + k * BIAS_ROWS * BAND
        m[:, at:at + BIAS_ROWS * BAND] = np.concatenate(parts, axis=1).reshape(P, -1)
    m[:, M_SCAN:] = (np.arange(S + 4) % CHUNK != 0)[None, :]
    return f, m.view(np.int32)


def weight_tiles():
    order = [("in", C_V + P * c) for c in range(4)]
    for p in range(PAIRS):
        order += [("in", C_Q + P * p), ("in", C_K + P * p)]
    order += [("in", C_HV + P * c) for c in range(4)]
    order += [("in", C_FF), ("in", C_FB), ("in", C_HQ)]
    for h in range(HG_HEADS):
        if h + 1 < HG_HEADS:
            order += [("in", c + P * (h + 1)) for c in (C_FF, C_FB, C_HQ)]
        order += [("in", C_HG + P * h)]
    order += [("out", k) for k in range(KT)]
    return order


UT_AFTER = {1: (8, 9, 10, 11), 2: (12, 13, 14, 15)}
UT_SPREAD = {(0, 3): (8, 9, 10, 11), (1, 1): (12, 13, 14, 15)}
UT_TAKEN = [(8, 9, 10, 11), (12, 13, 14, 15), (), ()]

TILES = weight_tiles()
N_IN = 32
N_TILES = len(TILES) + 2 * 4 * D // P


def proj_units():
    u = [("v", c, t) for c in range(2) for t in range(TT)]
    for p in range(PAIRS):
        u += [("q", p, 0), ("q", p, 1), ("k", p, 0), ("k", p, 1)]
    u += [("hv", c, t) for c in range(2) for t in range(TT)]
    for h in range(HG_HEADS):
        if h == 0:
            u += [(k, 0, i) for k in ("ff", "fb", "hq") for i in range(2)]
        if h + 1 < HG_HEADS:
            u += [(k, h + 1, i) for k in ("ff", "fb", "hq") for i in range(2)]
        u += [("hg", h, i) for i in range(2)]
    return u


UNITS = proj_units()
UNIT = {u: n for n, u in enumerate(UNITS)}
TILE_OF = {("in", c): n for n, (k, c) in enumerate(TILES) if k == "in"}
COL = {"q": C_Q, "k": C_K, "ff": C_FF, "fb": C_FB, "hq": C_HQ, "hg": C_HG}

BEFORE = 16 + 6
STEP_UNIT = {s: BEFORE + 1 + s for s in range(-2, 9)}
VALUE_UNITS = {10: (0, 1, 2), 11: (3, 4, 5), 12: (6, 7, 8), 13: (9, 10, 11), 14: (12, 13), 15: (14, 15)}
BANDS_BEFORE = {14: (2, 3, 4), 15: (5, 6), 16: (7, 8), 17: (9, 10, 11), 18: (12, 13, 14), 19: (15,)}
FIRST_HEAD = list(range(UNIT[("ff", 0, 0)], UNIT[("hq", 0, 1)] + 1))
PIECES = 9
_steps = [(u, k) for u in range(UNIT[("hq", 0, 1)] + 1, len(UNITS)) for k in range(KT)]
_counts = [[8 * KT * (i + 1) // PIECES - 8 * KT * i // PIECES for i in range(PIECES)] for _ in range(HG_HEADS - 2)]
_counts += [[7, 7, 7, 7, 7, 7, 6, 3, 3]]
_left = len(_steps) - sum(sum(c) for c in _counts)
_counts += [[_left * (i + 1) // PIECES - _left * i // PIECES for i in range(PIECES)]]
UNIT_STEPS = [[[_steps.pop(0) for _ in range(n)] for n in c] for c in _counts]
HEAD_UNITS = [[[u for u, k in p if k == KT - 1] for p in head] for head in UNIT_STEPS]
RESULT_AT = [next((i + 1 for i in range(PIECES) if UNIT[("hg", h, 1)] in HEAD_UNITS[h + 1][i]), 0)
             for h in range(HG_HEADS - 1)]
TILES_BEGUN = [[sum(k == 0 and UNITS[u][2] == 0 for u, k in p) for p in head] for head in UNIT_STEPS]
BY_ACT = ("hv", "hq")
DVE_ARGS = [2, 2, 2, 2, 1, 1, 0, 1, 0]
POOL_ARGS = [2, 2, 2, 2, 1, 1, 0, 1, 0]
PRODUCT_STEPS = [3, 3, 3, 3, 2, 2, 1, 1, 2]


def steps_to(steps, h, i):
    return sum(steps) * h + sum(steps[:i + 1])


def bank_uses(n, by_act):
    return sum((UNITS[i][0] in BY_ACT) == by_act for i in range(n + 1))


def hybrid_block(nc, x, w_in, w_out, attn_norm_w, mlp_norm_w, q_norm_w, k_norm_w, rpb, hg_norm_w,
                 lb_fwd, lb_bwd, w_up, w_down, tables, masks, out):
    ctx = ExitStack()
    with ctx:
        def sem(name):
            return ctx.enter_context(nc.semaphore(name))

        at = [int(nc.sbuf_base) + 31 & ~31]

        def place(name, shape, dt, size=4):
            t = nc.alloc_sbuf_tensor_at(name, shape, dt, offset=at[0])
            at[0] += int(np.prod(shape[1:])) * size + 31 & ~31
            return t

        uT_hi = place("uT_hi", [P, KT, S], F32R)
        uT_lo = place("uT_lo", [P, KT, S], F32R)
        w_hi = place("w_hi", [P, RING, 1024], F32R)
        w_lo = place("w_lo", [P, RING, 1024], F32R)
        stage = place("stage", [P, STAGE, 1024], F32)
        tab = place("tab", [P, 3 * P], F32)
        hg_mask = place("hg_mask", [P, NLEV, P], U8, 1)
        scan_mask = place("scan_mask", [P, S + 4], U8, 1)
        norm_w = place("norm_w", [P, 2, KT], F32)
        qk_w = place("qk_w", [P, 2], F32)
        gnorm = place("gnorm", [P, 1], F32)
        lb_raw = place("lb_raw", [P, 2, 2, HG_HEADS], F32)
        lb = place("lb", [P, 2, HG_HEADS], F32)
        lb_rest = place("lb_rest", [P, 2, HG_HEADS], F32)
        lb_neg = place("lb_neg", [P, 2, HG_HEADS], F32)
        ssq = place("ssq", [P, 2, TT], F32)
        rstd = place("rstd", [P, 2, TT], F32)
        s_min = place("s_min", [P, STEPS * NG], F32)
        s_sum = place("s_sum", [P, STEPS * NG], F32)
        s_inv = place("s_inv", [P, STEPS * NG], F32)
        g_chunk = place("g_chunk", [P, 2, NCH], F32)
        eps_col = place("eps_col", [P, 1], F32)
        one_col = place("one_col", [P, 1], F32)
        work = at[0]
        ident, head_mean, all_mean = tab[:, 0:P], tab[:, P:2 * P], tab[:, 2 * P:3 * P]

        q_tiles = place("q_tiles", [P, 2, 2, NG, NB, P], F32R)
        k_hi = place("k_hi", [P, 2, S], F32R)
        k_lo = place("k_lo", [P, 2, S], F32R)
        v_hi = place("v_hi", [P, 2, NG, P], F32R)
        v_lo = place("v_lo", [P, 2, NG, P], F32R)
        probs = place("probs", [P, 2, STEP_W], F32)
        pT_hi = place("pT_hi", [P, 2, 384], F32R)
        pT_lo = place("pT_lo", [P, 2, 384], F32R)
        bias = place("bias", [P, BIAS_ROWS, BAND], F32)
        rpb_win = place("rpb_win", [P, 12 * RPB_PITCH], F32)
        na_mask = place("na_mask", [P, 3, BIAS_ROWS, BAND], U8, 1)
        qk_t = place("qk_t", [P, 3, HALF], F32)
        mix_na = place("mix_na", [P, S], F32)
        end_attention = at[0]
        vs = nc.alloc_sbuf_tensor_at("vs", [P, 2, 2, 256], F32, offset=end_attention)
        x_tok = nc.alloc_sbuf_tensor_at("x_tok", [P, TT, D], F32, offset=work)

        at[0] = work
        h_v = place("h_v", [P, TT, 512], F32)
        h_gates = place("h_gates", [P, 2, 4, S], F32)
        h_gate = place("h_gate", [P, S], F32)
        tmp = place("tmp", [P, 2, HALF], F32)
        k_tok = place("k_tok", [P, S], F32)
        h_q = place("h_q", [P, 2, S], F32)
        zz = place("zz", [P, 2, 2, S], F32)
        state = place("state", [P, 2, NCH - 1, P], F32)
        scores = place("scores", [P, NCH, P], F32)
        gate_t = place("gate_t", [P, HALF], F32)
        end_hgrn = at[0]

        def h_cum(h, d):
            return h_gates[:, h % 2, d, :]

        def h_key(h, d):
            return h_gates[:, h % 2, 2 + d, :]

        at[0] = work
        u_tok = place("u_tok", [P, TT, D], F32)
        acts = place("acts", [P, 2, 2, FBLK, S], F32R)
        resid = place("resid", [P, TT, D], F32)
        end_mlp = at[0]
        na_back = nc.alloc_sbuf_tensor_at("na_back", [P, PAIRS, S], F32, offset=work + TT * 512 * 4)
        assert max(end_attention + 8192, end_hgrn, end_mlp) <= int(nc.sbuf_usable_end), (
            end_attention, end_hgrn, end_mlp, int(nc.sbuf_usable_end))

        bank = [ctx.enter_context(nc.psum_tensor(f"bank{i}", [P, HALF], F32)) for i in range(8)]
        v_dram = [nc.dram_tensor(f"v_dram{i}", [S, 512], F32).ap() for i in range(2)]
        na_dram = nc.dram_tensor("na_dram", [PAIRS * P, S], F32).ap()

        tab_load = sem("tab_load")
        norm_load = sem("norm_load")
        c_load = sem("c_load")
        x_load = [sem(f"x_load{t}") for t in range(TT)]
        w_load = [sem(f"w_load{i}") for i in range(STAGE)]
        w_split = sem("w_split")
        w_used = sem("w_used")
        act_own = sem("act_own")
        dve_own = sem("dve_own")
        sq_done = sem("sq_done")
        u_ready = sem("u_ready")
        uT_done = sem("uT_done")
        uT_act = sem("uT_act")
        uT_dve = sem("uT_dve")
        proj_done = sem("proj_done")
        act_freed = sem("act_freed")
        dve_freed = sem("dve_freed")
        unit_act = sem("unit_act")
        unit_dve = sem("unit_dve")
        qk_sq = sem("qk_sq")
        qk_mean = sem("qk_mean")
        qk_ready = sem("qk_ready")
        v_stored = [sem(f"v_stored{i}") for i in range(2)]
        v_load = [sem(f"v_load{i}") for i in range(2)]
        rpb_load = sem("rpb_load")
        bias_done = sem("bias_done")
        score_done = sem("score_done")
        masked = sem("masked")
        exp_done = sem("exp_done")
        prob_done = sem("prob_done")
        pT_done = sem("pT_done")
        pT_act = sem("pT_act")
        pT_dve = sem("pT_dve")
        pv_done = sem("pv_done")
        mix_done = sem("mix_done")
        na_store = sem("na_store")
        h_sums = sem("h_sums")
        z_pool = sem("z_pool")
        z_arg = sem("z_arg")
        z_exp = sem("z_exp")
        z_ready = sem("z_ready")
        lev_done = sem("lev_done")
        lev_taken = sem("lev_taken")
        kT_done = sem("kT_done")
        kT_act = sem("kT_act")
        g_ready = sem("g_ready")
        upd_done = sem("upd_done")
        st_done = sem("st_done")
        o_done = sem("o_done")
        o_sq = sem("o_sq")
        o_mean = sem("o_mean")
        o_rs = sem("o_rs")
        o_norm = sem("o_norm")
        y_done = sem("y_done")
        na_load = sem("na_load")
        m_hi = sem("m_hi")
        m_lo = sem("m_lo")
        down_done = sem("down_done")
        added = sem("added")
        up_done = sem("up_done")
        relu_done = sem("relu_done")
        sqr_done = sem("sqr_done")
        a_hi = sem("a_hi")
        a_lo = sem("a_lo")
        out_store = sem("out_store")
        mask_load = sem("mask_load")
        resid_load = [sem(f"resid_load{t}") for t in range(TT)]
        ready_cols = sem("ready_cols")
        lb_exp = sem("lb_exp")
        lb_diff = sem("lb_diff")
        params = sem("params")
        cleared = sem("cleared")

        def z_turn(h, i):
            return (h * PIECES + i) % 2

        def count(r, per_turn, n):
            return n if r is None else r * per_turn + n

        def up_order(j):
            return [divmod(i, 2) for i in range(2 * FBLK)] if j else [(0, 0), (1, 0), (0, 1), (1, 1)]

        CONSTS = 16 * 10
        FIRST_QK = UNIT[("q", 0, 0)]
        heads = (slice(0, 64), slice(64, 128))

        def freed(n):
            by_act = UNITS[n][0] in BY_ACT
            return (act_freed if by_act else dve_freed), bank_uses(n, by_act)

        def act_hands(n):
            return sum({"v": 1, "q": 5, "k": 2, "ff": 2, "fb": 2, "hg": 1}.get(UNITS[i][0], 0) for i in range(n))

        def dve_hands(n):
            return sum(UNITS[i][0] == "hg" for i in range(n))

        def qk_count(n):
            return sum({"q": 4, "k": 1}[UNITS[i][0]] for i in range(FIRST_QK, n + 1))

        def halves(t, size):
            v = t.rearrange("p (b s) -> p b s", s=size)
            return v[:, :, 0:size // 2], v[:, :, size // 2:]

        def z_differences(h, i):
            t = z_turn(h, i)
            zk, zq = zz[:, t, 0, :], zz[:, t, 1, :]
            f, b = h_cum(h, 0), h_cum(h, 1)
            if i < 4:
                size = LEVELS[i]
                (fl, fr), (bl, br) = halves(f, size), halves(b, size)
                (kl, kr), (ql, qr) = halves(zk, size), halves(zq, size)
                shape = [P, S // size, size // 2]
                f_mid = fl[:, :, size // 2 - 1:size // 2].to_broadcast(shape)
                b_mid = br[:, :, 0:1].to_broadcast(shape)
                return [(kl, f_mid, fl), (qr, fr, f_mid), (kr, b_mid, br), (ql, bl, b_mid)]
            if i < 6:
                src, mid = ((f, 3), (b, 4))[i - 4]
                v, vk, vq = (a.rearrange("p (b s) -> p b s", s=8) for a in (src, zk, zq))
                m = v[:, :, mid:mid + 1].to_broadcast([P, S // 8, 8])
                return [(vk, m, v), (vq, v, m)]
            fv, bv, v0, v1 = (a.rearrange("p (b s) -> p b s", s=CHUNK) for a in (f, b, zk, zq))
            shape = [P, NCH, CHUNK]
            return [(v0, fv[:, :, CHUNK - 1:CHUNK].to_broadcast(shape), fv), (v1, bv[:, :, 0:1].to_broadcast(shape), bv)]

        def operands_free(eng, h, i):
            n = h * PIECES + i - 2
            if n < 0:
                return
            hh, j = divmod(n, PIECES)
            if j < NLEV:
                eng.wait_ge(lev_done, 2 * (NLEV * hh + j + 1))
            elif j == 7:
                eng.wait_ge(kT_done, 4 * (hh + 1))
            else:
                eng.wait_ge(o_done, 2 * (hh + 1))

        def hgrn_may_start(eng):
            eng.wait_ge(na_store, 16 * PAIRS)
            eng.wait_ge(pv_done, NG * STEPS)

        def out_bank(i, bank0):
            return bank[bank0 + (i + 2) % 4]

        def uT_bank(n):
            return bank[4 + n % 4]

        def mixer_tile(k):
            return na_back[:, k, :] if k < PAIRS else h_v[:, :, P * (k - PAIRS):P * (k - PAIRS) + P]

        def after(h, i, n):
            return divmod(h * PIECES + i + n, PIECES)

        def q_place(part, p, g, h):
            return q_tiles[heads[h], p % 2, part, g, :, 64 * h:64 * h + 64].rearrange("p n (r c) -> p r n c", c=16)

        def q_source(g2, h):
            return qk_t[heads[h], 2, 256 * g2:256 * g2 + 256].rearrange("p (r n c) -> p r n c", n=NB, c=16)

        def mix_place(t, n, h):
            return t[heads[h], :].rearrange("p (g r n c) -> p g r n c", g=NG, r=4, n=NB)[:, :, :, n, :]

        def mix_source(h):
            return bank[6][heads[h], :].rearrange("p (g h r c) -> p g h r c", g=NG, h=2, r=4)[:, :, h, :, :]

        block = ctx.enter_context(nc.Block())

        @block.sync
        def _(sp):
            x_v = x.rearrange("b (t p) d -> p (b t) d", p=P)

            def load_x(t):
                sp.dma_start(x_tok[:, t, :], x_v[:, t, :]).then_inc(x_load[t], 16)

            def load_parameters():
                with nc.allow_non_contiguous_dma(reason="small parameter vectors"):
                    sp.dma_start(norm_w[:, 1, :], mlp_norm_w.rearrange("o (k p) -> p (o k)", p=P)).then_inc(c_load, 16)
                    for h in heads:
                        sp.dma_start(qk_w[h, 0:1], q_norm_w.rearrange("o d -> d o")).then_inc(c_load, 16)
                        sp.dma_start(qk_w[h, 1:2], k_norm_w.rearrange("o d -> d o")).then_inc(c_load, 16)
                    sp.dma_start(gnorm[:, :], hg_norm_w.rearrange("o d -> d o")).then_inc(c_load, 16)
                    for i, src in enumerate((lb_fwd, lb_bwd)):
                        for r in range(2):
                            sp.dma_start(lb_raw[:, i, r, :], src[r].rearrange("(h d) -> d h", d=P)).then_inc(c_load, 16)

            w_in_v = w_in.rearrange("o (k p) n -> p (o k) n", p=P)
            w_out_v = w_out.rearrange("o (k p) n -> k p (o n)", p=P)
            w_down_v = w_down.rearrange("o (k p) n -> k p (o n)", p=P)
            def load_bias_window(p):
                if p >= 1:
                    sp.wait_ge(bias_done, 9 * p)
                for h in range(2):
                    for r in range(4):
                        src = rpb[2 * p + h, :, 3 - r:15 - r, :].rearrange("c r v -> c (r v)")
                        sp.dma_start(rpb_win[64 * h + 16 * r:64 * h + 16 * r + 16, :], src).then_inc(rpb_load, 16)

            def load_band(s):
                p, n = divmod(s, NB)
                if s >= 2:
                    sp.wait_ge(pv_done, NG * (s - 1))
                for i, dst in enumerate((v_hi, v_lo)):
                    for r in range(4):
                        src = v_dram[i].rearrange("(g r c) e -> r c g e", r=4, c=GRID)[
                            r, BAND_START[n]:BAND_START[n] + BAND, :, P * p:P * p + P]
                        sp.dma_start(dst[32 * r:32 * r + 32, s % 2, :, :].bitcast(F32), src).then_inc(v_load[s % 2], 16)

            w_up_v = w_up.rearrange("o (k p) n -> p (o k) n", p=P)
            for t in range(4):
                load_x(t)
            sp.dma_start(tab[:, :], tables).then_inc(tab_load, 16)
            for n, (kind, where) in enumerate(TILES):
                if n == 2:
                    with nc.allow_non_contiguous_dma(reason="small parameter vector"):
                        sp.dma_start(norm_w[:, 0, :], attn_norm_w.rearrange("o (k p) -> p (o k)", p=P)).then_inc(norm_load, 16)
                    for t in range(4, TT):
                        load_x(t)
                if n == 4:
                    load_parameters()
                    load_bias_window(0)
                if n == 10:
                    for i in range(2):
                        sp.wait_ge(v_stored[i], 32 * 8)
                    load_band(0)
                    load_band(1)
                for s in BANDS_BEFORE.get(n, ()):
                    if (s + 1) % NB == 0 and (s + 1) // NB < PAIRS:
                        load_bias_window((s + 1) // NB)
                    load_band(s)
                if n == N_IN + RING:
                    sp.wait_ge(z_ready, steps_to(PRODUCT_STEPS, HG_HEADS - 1, -1))
                    sp.wait_ge(g_ready, HG_HEADS - 1)
                    sp.wait_ge(na_store, 16 * PAIRS)
                    sp.dma_start(na_back[:, :, :], na_dram.rearrange("(f p) s -> p f s", p=P)).then_inc(na_load, 16)
                if n == N_IN + RING + 1:
                    sp.wait_ge(o_done, 2 * HG_HEADS)
                    for t in range(TT):
                        if t == TT - 1:
                            sp.wait_ge(*freed(len(UNITS) - 1))
                        sp.dma_start(resid[:, t, :], x_v[:, t, :]).then_inc(resid_load[t], 16)
                if n >= STAGE:
                    sp.wait_ge(w_split, 2 * (n - STAGE + 1))
                dst = stage[:, n % STAGE, :]
                if kind == "in":
                    sp.dma_start(dst.rearrange("p (k c) -> p k c", k=KT),
                                 w_in_v[:, :, where:where + P]).then_inc(w_load[n % STAGE], 16)
                else:
                    sp.dma_start(dst, w_out_v[where]).then_inc(w_load[n % STAGE], 16)

            def mlp_tiles(kind, r, j, at):
                for f in range(FBLK):
                    n = len(TILES) + at + f
                    sp.wait_ge(w_split, count(r, 8 * FBLK, 2 * (n - STAGE + 1)))
                    dst = stage[:, n % STAGE, :]
                    col = count(r, 2 * FBLK * P, (j * FBLK + f) * P)
                    if kind == "up":
                        sp.dma_start(dst.rearrange("p (k c) -> p k c", k=KT),
                                     w_up_v[:, :, bass.ds(col, P)]).then_inc(w_load[n % STAGE], 16)
                    else:
                        sp.dma_start(dst, w_down.rearrange("o f n -> (o f) n")[bass.ds(col, P), :]).then_inc(w_load[n % STAGE], 16)

            mlp_tiles("up", None, 0, 0)
            with sp.Fori(0, MLP_TURNS, 1) as r:
                mlp_tiles("up", r, 1, 2)
                mlp_tiles("down", r, 0, 4)
                mlp_tiles("up", r, 2, 6)
                mlp_tiles("down", r, 1, 8)
            mlp_tiles("up", None, LAST, 4 * LAST - 2)
            mlp_tiles("down", None, LAST - 1, 4 * LAST)
            mlp_tiles("down", None, LAST, 4 * LAST + 2)

            for t in range(TT):
                sp.wait_ge(added, 16 * (OUT_BLOCKS + MLP_BLOCKS - 1) + 2 * t + 2)
                sp.dma_start(out.rearrange("b (t p) d -> p (b t) d", p=P)[:, t, :], resid[:, t, :]).then_inc(out_store, 16)
            sp.wait_ge(out_store, 16 * TT)
            sp.wait_ge(v_stored[0], 32 * 8)
            sp.wait_ge(v_stored[1], 32 * 8)
            sp.wait_ge(na_store, 16 * PAIRS)

        @block.gpsimd
        def _(pool):
            def split(i, loaded, used, turn):
                pool.wait_ge(w_load[i % STAGE], loaded)
                if used is not None:
                    pool.wait_ge(w_used, used)
                pool.tensor_tensor(w_hi[:, i, :], stage[:, i % STAGE, :],
                                   one_col[:, 0:1].to_broadcast([P, 1024]), ALU.mult).then_inc(w_split, 1)
                pool.wait_ge(w_split, turn + 1)
                pool.tensor_tensor(w_lo[:, i, :], stage[:, i % STAGE, :], w_hi[:, i, :].bitcast(F32),
                                   ALU.subtract).then_inc(w_split, 1)

            pool.wait_ge(ready_cols, 2)
            for i in range(RING):
                split(i, 16 * (i // STAGE + 1), None, 2 * i)
            def split_turns(first, end):
                with pool.Fori(first, end, 1) as r:
                    for i in range(RING):
                        split(i, r * (16 * RING // STAGE) + 16 * (i // STAGE + 1),
                              r * RING + (i + 1 - RING), r * (2 * RING) + 2 * i)

            def split_tile(n):
                split(n % RING, 16 * (n // STAGE + 1), n - RING + 1, 2 * n)

            def z_arguments(h, i):
                if POOL_ARGS[i]:
                    pool.wait_ge(h_sums, 2 * (h + 1))
                    operands_free(pool, h, i)
                    for dst, a, b in z_differences(h, i)[DVE_ARGS[i]:]:
                        pool.tensor_tensor(dst, a, b, ALU.subtract).then_inc(z_pool, 1)

            first = TILE_OF[("in", C_FF + P)]
            split_turns(1, first // RING + 1)
            for n in range(first // RING * RING + RING, first + RING - 1):
                split_tile(n)
            hgrn_may_start(pool)
            z_arguments(0, 0)
            z_arguments(0, 1)
            tile = first + RING - 1
            for h in range(HG_HEADS):
                for i in range(PIECES):
                    if after(h, i, 2)[0] < HG_HEADS:
                        z_arguments(*after(h, i, 2))
                    for _ in range(TILES_BEGUN[h][i]):
                        split_tile(tile)
                        tile += 1
            while tile % RING:
                split_tile(tile)
                tile += 1
            split_turns(tile // RING, N_TILES // RING)

        @block.scalar
        def _(act):
            own = [0]

            def step(ins):
                ins.then_inc(act_own, 1)
                own[0] += 1
                act.wait_ge(act_own, own[0])

            def rms(norm, t):
                if norm == 0:
                    src, scratch = x_tok, vs[:, :, :, :].rearrange("p a b c -> p (a b c)")
                else:
                    src, scratch = resid, u_tok[:, t, :]
                step(act.activation(scratch, src[:, t, :], ACT.Square, accum_out=ssq[:, norm, t:t + 1]))
                step(act.activation(rstd[:, norm, t:t + 1], ssq[:, norm, t:t + 1], ACT.Ln,
                                    scale=1.0 / D, bias=eps_col[:, 0:1]))
                act.activation(rstd[:, norm, t:t + 1], rstd[:, norm, t:t + 1], ACT.Exp,
                               scale=-0.5).then_inc(sq_done, 1)

            def take_uT(norm, n):
                k, half = n % KT, n // KT
                act.wait_ge(uT_done, norm * 16 + n + 1)
                act.activation(uT_hi[:, k, half * HALF:half * HALF + HALF], uT_bank(n)[:, :], ACT.Copy,
                               scale=norm_w[:, norm, k:k + 1]).then_inc(uT_act, 1)

            def unit(n):
                kind, what, part = UNITS[n]
                b = bank[n % 2]
                cols = slice(part * HALF, part * HALF + HALF)
                if kind in ("v", "hv", "hq"):
                    act.wait_ge(proj_done, n + 1)
                if kind == "v":
                    if n >= 2:
                        act.wait_ge(v_stored[n % 2], 32 * (n // 2))
                    act.activation(vs[:, n % 2, 0, :].bitcast(F32R), b[:, 0:256], ACT.Copy).then_inc(unit_act, 1)
                    act.wait_ge(*freed(n))
                    for i in range(2):
                        act.dma_start(v_dram[i][P * part:P * part + P, 256 * what:256 * what + 256],
                                      vs[:, n % 2, i, :]).then_inc(v_stored[n % 2], 16)
                elif kind == "hv":
                    if (what, part) == (0, 0):
                        act.wait_ge(score_done, NG * NB * (PAIRS - 1))
                    act.activation(h_v[:, part, 256 * what:256 * what + 256], b[:, 0:256], ACT.Copy).then_inc(act_freed, 1)
                elif kind == "hq":
                    if what >= 2:
                        act.wait_ge(z_ready, steps_to(PRODUCT_STEPS, what - 1, -1))
                        act.wait_ge(lev_done, 2 * NLEV * (what - 1))
                    act.activation(h_q[:, what % 2, cols], b[:, :], ACT.Copy).then_inc(act_freed, 1)
                elif kind in ("ff", "fb"):
                    d = ("ff", "fb").index(kind)
                    act.wait_ge(*freed(n))
                    step(act.activation(gate_t[:, :], gate_t[:, :], ACT.Exp, scale=-1.0))
                    step(act.activation(gate_t[:, :], gate_t[:, :], ACT.Ln, bias=one_col[:, 0:1]))
                    step(act.activation(gate_t[:, :], gate_t[:, :], ACT.Exp, scale=-1.0))
                    if what >= 2:
                        act.wait_ge(z_arg, steps_to(DVE_ARGS, what - 1, -1))
                        act.wait_ge(z_pool, steps_to(POOL_ARGS, what - 1, -1))
                    act.activation(h_cum(what, d)[:, cols], gate_t[:, :], ACT.Ln,
                                   scale=lb_rest[:, d, what:what + 1], bias=lb[:, d, what:what + 1]).then_inc(unit_act, 1)
                    if what >= 2:
                        act.wait_ge(z_ready, steps_to(PRODUCT_STEPS, what - 1, -1))
                    act.activation(h_key(what, d)[:, cols], gate_t[:, :], ACT.Identity,
                                   scale=lb_neg[:, d, what:what + 1], bias=lb_rest[:, d, what:what + 1]).then_inc(unit_act, 1)
                elif kind == "hg":
                    act.wait_ge(unit_dve, dve_hands(n) + 1)
                    step(act.activation(gate_t[:, :], gate_t[:, :], ACT.Exp, scale=-1.0))
                    step(act.activation(gate_t[:, :], gate_t[:, :], ACT.Ln, bias=one_col[:, 0:1]))
                    act.activation(gate_t[:, :], gate_t[:, :], ACT.Exp, scale=-1.0).then_inc(unit_act, 1)

            def qk_square(n):
                act.wait_ge(proj_done, n + 1)
                if n > FIRST_QK:
                    act.wait_ge(qk_mean, n - FIRST_QK)
                act.activation(qk_t[:, 0, :], bank[n % 2][:, :], ACT.Square).then_inc(qk_sq, 1)

            def qk_root(n):
                act.wait_ge(qk_mean, n - FIRST_QK + 1)
                if n > FIRST_QK:
                    act.wait_ge(*freed(n - 1))
                step(act.activation(qk_t[:, 1, :], bank[7][:, :], ACT.Ln, bias=eps_col[:, 0:1]))
                act.activation(qk_t[:, 1, :], qk_t[:, 1, :], ACT.Exp, scale=-0.5).then_inc(unit_act, 1)

            def qk_hi(n):
                kind, p, part = UNITS[n]
                act.wait_ge(*freed(n))
                if p >= 2:
                    act.wait_ge(score_done, NG * NB * (p - 1))
                if kind == "k":
                    act.activation(k_hi[:, p % 2, part * HALF:part * HALF + HALF], qk_t[:, 2, :],
                                   ACT.Copy).then_inc(unit_act, 1)
                else:
                    if n == FIRST_QK:
                        act.wait_ge(cleared, 2)
                    for g2 in range(2):
                        for h in range(2):
                            act.activation(q_place(0, p, 2 * part + g2, h), q_source(g2, h),
                                           ACT.Copy).then_inc(unit_act, 1)

            def score_exp(s, g):
                i = NG * s + g
                t = probs[:, s % 2, TILE_OFF[g]:TILE_OFF[g] + TILE_W[g]]
                act.wait_ge(masked, i + 1)
                act.activation(t, t, ACT.Exp, scale=-1.0, bias=s_min[:, i:i + 1],
                               accum_out=s_sum[:, i:i + 1]).then_inc(exp_done, 1)

            def take_pT(s, kg):
                i = NG * s + kg
                w = P * len(KG_GROUPS[kg])
                act.wait_ge(pT_done, i + 1)
                if i >= 2:
                    act.wait_ge(pv_done, i - 1)
                act.activation(pT_hi[:, i % 2, 0:w], bank[4 + i % 2][:, 0:w], ACT.Copy).then_inc(pT_act, 1)

            def take_mix(s):
                p, n = divmod(s, NB)
                act.wait_ge(pv_done, NG * (s + 1))
                if n == 0 and p:
                    act.wait_ge(na_store, 16 * p)
                for h in range(2):
                    act.activation(mix_place(mix_na, n, h), mix_source(h), ACT.Copy).then_inc(mix_done, 1)

            def store_mix(p):
                act.wait_ge(mix_done, 2 * NB * (p + 1))
                act.dma_start(na_dram[P * p:P * p + P, :], mix_na[:, :]).then_inc(na_store, 16)

            def z_exponentials(h, i):
                if i == 6:
                    return
                t = z_turn(h, i)
                if i == 8:
                    operands_free(act, h, i)
                    act.activation(zz[:, t, :, :], h_gates[:, h % 2, 0:2, :], ACT.Exp).then_inc(z_exp, 1)
                else:
                    act.wait_ge(z_pool, steps_to(POOL_ARGS, h, i))
                    act.wait_ge(z_arg, steps_to(DVE_ARGS, h, i))
                    act.activation(zz[:, t, :, :], zz[:, t, :, :], ACT.Exp).then_inc(z_exp, 1)

            def chunk_decays(h):
                act.wait_ge(h_sums, 2 * (h + 1))
                if h:
                    act.wait_ge(st_done, 4 * h)
                step(act.activation(g_chunk[:, 0, :], h_cum(h, 0)[:, CHUNK - 1::CHUNK], ACT.Exp))
                act.activation(g_chunk[:, 1, :], h_cum(h, 1)[:, 0::CHUNK], ACT.Exp).then_inc(g_ready, 1)

            def take_k_tok(h):
                for d in range(2):
                    for cg in range(2):
                        n = 4 * h + 2 * d + cg
                        act.wait_ge(kT_done, n + 1)
                        if cg == 0 and n:
                            act.wait_ge(upd_done, n)
                        act.activation(k_tok[:, HALF * cg:HALF * cg + HALF], bank[4 + 2 * d + cg][:, :], ACT.Copy).then_inc(kT_act, 1)

            def head_squares(h):
                for part in range(2):
                    act.wait_ge(o_done, 2 * h + part + 1)
                    if h:
                        act.wait_ge(y_done, 2 * h)
                    act.activation(tmp[:, part, :], bank[6 + part][:, :], ACT.Square).then_inc(o_sq, 1)

            def head_roots(h):
                for part in range(2):
                    act.wait_ge(o_mean, 2 * h + part + 1)
                    step(act.activation(tmp[:, part, :], bank[4 + part][:, :], ACT.Ln, bias=eps_col[:, 0:1]))
                    act.activation(tmp[:, part, :], tmp[:, part, :], ACT.Exp, scale=-0.5).then_inc(o_rs, 1)

            def mixer_hi(b):
                if b == 0:
                    act.wait_ge(z_ready, steps_to(PRODUCT_STEPS, HG_HEADS, -1))
                    act.wait_ge(na_load, 16)
                if b == 1:
                    act.wait_ge(y_done, 2 * HG_HEADS)
                if b >= 2:
                    act.wait_ge(down_done, 16 * (b - 1))
                for f in range(FBLK):
                    dst = acts[:, b % 2, 0, f, :]
                    if b >= 2:
                        act.activation(dst.rearrange("p (c i) -> p c i", i=P), mixer_tile(FBLK * b + f), ACT.Copy).then_inc(m_hi, 1)
                    else:
                        act.activation(dst, mixer_tile(FBLK * b + f), ACT.Copy).then_inc(m_hi, 1)

            def activations(r, j, spread=()):
                for i, (f, half) in enumerate(up_order(j)):
                    for n in (spread[i] if spread else ()):
                        take_uT(1, n)
                    act.wait_ge(up_done, count(r, 8, 4 * j + i + 1))
                    if i or j:
                        act.wait_ge(a_lo, count(r, 8, 4 * j + i))
                    act.activation(u_tok[:, i, 0:HALF], bank[2 * f + half][:, :], ACT.Relu).then_inc(relu_done, 1)
                    act.wait_ge(sqr_done, count(r, 8, 4 * j + i + 1))
                    act.wait_ge(down_done, count(r, 32, 16 * (OUT_BLOCKS + max(j - 1, 0))))
                    act.activation(acts[:, j % 2, 0, f, half * HALF:half * HALF + HALF], u_tok[:, i, HALF:D],
                                   ACT.Copy).then_inc(a_hi, 1)

            act.preload_act_table_set("natural_log_exp_and_others")
            act.wait_ge(ready_cols, 2)
            for t in range(TT):
                if t == 4:
                    act.wait_ge(norm_load, 16)
                    for n in range(KT):
                        take_uT(0, n)
                act.wait_ge(x_load[t], 16)
                rms(0, t)
            for dst, a, b in ((na_mask[:, :, :, :].rearrange("p s r c -> p (s r c)"), M_NA, M_SCAN),
                              (hg_mask[:, :, :].rearrange("p l i -> p (l i)"), M_HG, M_NA),
                              (scan_mask[:, :], M_SCAN, M_END)):
                act.dma_start(dst.bitcast(I32), masks[:, a // 4:b // 4]).then_inc(mask_load, 16)
            for n in range(FIRST_QK):
                unit(n)
                for i in UT_AFTER.get(n, ()):
                    take_uT(0, i)
            act.wait_ge(lb_diff, 1)
            act.activation(lb[:, :, :], lb[:, :, :], ACT.Exp).then_inc(lb_exp, 1)
            for n in range(FIRST_QK, BEFORE - 2):
                qk_square(n)
                qk_root(n)
                qk_hi(n)
            qk_square(BEFORE - 2)
            for s in range(-2, STEPS):
                qk = BEFORE + s if -2 <= s <= 9 else None
                if s >= 0:
                    take_pT(s, 0)
                    take_pT(s, 1)
                if qk is not None:
                    qk_root(qk)
                values = [UNIT[("hv", 0, 0)] + i for i in VALUE_UNITS.get(s, ())]
                for n in values[:1]:
                    unit(n)
                if s >= 0:
                    take_pT(s, 2)
                for n in values[1:2]:
                    unit(n)
                if s >= 0:
                    take_pT(s, 3)
                for n in values[2:]:
                    unit(n)
                if qk is not None:
                    qk_hi(qk)
                if s + 2 < STEPS:
                    for g in range(NG):
                        if g == 3 and s in STEP_UNIT:
                            qk_square(STEP_UNIT[s])
                        score_exp(s + 2, g)
                if s >= 0:
                    take_mix(s)
                    if s % NB == NB - 1:
                        store_mix(s // NB)
            hgrn_may_start(act)
            for n in FIRST_HEAD:
                if n == UNIT[("hq", 0, 0)]:
                    z_exponentials(0, 0)
                unit(n)
            last = []
            for h in range(HG_HEADS):
                for i in range(PIECES):
                    if after(h, i, 1)[0] < HG_HEADS:
                        z_exponentials(*after(h, i, 1))
                    if i == 0:
                        chunk_decays(h)
                        if h:
                            head_roots(h - 1)
                    if i == 7:
                        take_k_tok(h)
                    for n in last:
                        unit(n)
                    if i == 8:
                        if h == HG_HEADS - 1:
                            mixer_hi(0)
                        head_squares(h)
                    last = HEAD_UNITS[h][i]
            for n in last:
                unit(n)
            head_roots(HG_HEADS - 1)
            for b in range(1, OUT_BLOCKS):
                mixer_hi(b)
            for t in range(TT):
                for n in {5: (0, 1), 6: range(2, KT)}.get(t, ()):
                    take_uT(1, n)
                act.wait_ge(added, 16 * (OUT_BLOCKS - 1) + 2 * t + 2)
                rms(1, t)
            activations(None, 0, UT_TAKEN)
            with act.Fori(0, MLP_TURNS, 1) as r:
                activations(r, 1)
                activations(r, 2)
            activations(None, LAST)

        @block.vector
        def _(dve):
            own = [0]

            def step(ins):
                ins.then_inc(dve_own, 1)
                own[0] += 1
                dve.wait_ge(dve_own, own[0])

            def normalise_tokens(norm, t):
                src, dst = ((x_tok, x_tok), (resid, u_tok))[norm]
                dve.wait_ge(sq_done, TT * norm + t + 1)
                dve.tensor_scalar(dst[:, t, :], src[:, t, :], rstd[:, norm, t:t + 1], None, ALU.mult).then_inc(u_ready, 1)

            def take_uT(norm, n):
                k, half = n % KT, n // KT
                dve.wait_ge(uT_act, 16 * norm + n + 1)
                cols = slice(half * HALF, half * HALF + HALF)
                dve.scalar_tensor_tensor(uT_lo[:, k, cols], uT_bank(n)[:, :], norm_w[:, norm, k:k + 1],
                                         uT_hi[:, k, cols].bitcast(F32), ALU.mult, ALU.subtract).then_inc(uT_dve, 1)

            def value_lo(n):
                b = bank[n % 2]
                dve.wait_ge(unit_act, act_hands(n) + 1)
                dve.tensor_tensor(vs[:, n % 2, 1, :].bitcast(F32R), b[:, 0:256], vs[:, n % 2, 0, :],
                                  ALU.subtract).then_inc(dve_freed, 1)

            def clamp_gate(n):
                kind = UNITS[n][0]
                if kind in ("ff", "fb", "hg"):
                    dve.wait_ge(proj_done, n + 1)
                    ins = dve.tensor_scalar(gate_t[:, :], bank[n % 2][:, :], GATE_MIN, None, ALU.max)
                    if kind == "hg":
                        ins.then_inc(unit_dve, 1)
                    else:
                        ins.then_inc(dve_freed, 1)

            def finish_gate(n):
                kind, what, part = UNITS[n]
                cols = slice(part * HALF, part * HALF + HALF)
                if kind in ("ff", "fb"):
                    d = ("ff", "fb").index(kind)
                    cum = h_cum(what, d)[:, cols]
                    dve.wait_ge(unit_act, act_hands(n) + 2)
                    step(dve.tensor_scalar(cum, cum, LOG_F_MIN, None, ALU.max))
                    if part == 1:
                        t = h_cum(what, d)
                        if d == 0:
                            dve.tensor_tensor_scan(t, scan_mask[:, 0:S], t, 0.0, ALU.mult, ALU.add).then_inc(h_sums, 1)
                        else:
                            dve.tensor_tensor_scan(t[:, ::-1], scan_mask[:, 1:S + 1][:, ::-1], t[:, ::-1], 0.0,
                                                   ALU.mult, ALU.add).then_inc(h_sums, 1)
                        dve.wait_ge(h_sums, 2 * what + d + 1)
                elif kind == "hg":
                    dve.wait_ge(unit_act, act_hands(n) + 1)
                    dve.tensor_tensor(h_gate[:, cols], bank[n % 2][:, :], gate_t[:, :], ALU.mult).then_inc(dve_freed, 1)
                    dve.wait_ge(*freed(n))

            def qk_product(n):
                c = "qk".index(UNITS[n][0])
                dve.wait_ge(unit_act, act_hands(n) + 1)
                if n > FIRST_QK:
                    dve.wait_ge(qk_ready, qk_count(n - 1))
                dve.scalar_tensor_tensor(qk_t[:, 2, :], bank[n % 2][:, :], qk_w[:, c:c + 1], qk_t[:, 1, :],
                                         ALU.mult, ALU.mult).then_inc(dve_freed, 1)

            def qk_lo(n):
                kind, p, part = UNITS[n]
                dve.wait_ge(*freed(n))
                dve.wait_ge(unit_act, act_hands(n + 1))
                if kind == "k":
                    cols = slice(part * HALF, part * HALF + HALF)
                    dve.tensor_tensor(k_lo[:, p % 2, cols], qk_t[:, 2, :], k_hi[:, p % 2, cols].bitcast(F32),
                                      ALU.subtract).then_inc(qk_ready, 1)
                else:
                    for g2 in range(2):
                        for h in range(2):
                            dve.tensor_tensor(q_place(1, p, 2 * part + g2, h), q_source(g2, h),
                                              q_place(0, p, 2 * part + g2, h).bitcast(F32),
                                              ALU.subtract).then_inc(qk_ready, 1)

            def build_bias(s):
                p, n = divmod(s, NB)
                if n == 2:
                    return
                k = BAND_CLASS[n]
                if n == 0:
                    dve.wait_ge(rpb_load, 16 * 8 * (p + 1))
                if s:
                    dve.wait_ge(masked, NG * s)
                win = rpb_win[:, :].rearrange("p (r c) -> p r c", c=RPB_PITCH)
                c0 = 16 + CLASS_SHIFT[k]
                for a, b, u in ((0, 8, 4), (8, 20, 0), (20, 28, 0)):
                    dve.scalar_tensor_tensor(bias[:, a:b, :], na_mask[:, k, a:b, :], BIG,
                                             win[:, u:u + b - a, c0:c0 + BAND], ALU.mult, ALU.subtract).then_inc(bias_done, 1)

            def mask_scores(s, g):
                i = NG * s + g
                w = TILE_W[g]
                if g == 0:
                    dve.wait_ge(bias_done, 3 * (3 * (s // NB) + (1, 2, 2, 3)[s % NB]))
                    if s >= 2:
                        dve.wait_ge(pT_done, NG * (s - 1))
                dve.wait_ge(score_done, i + 1)
                dve.tensor_tensor_reduce(probs[:, s % 2, TILE_OFF[g]:TILE_OFF[g] + w], bank[2 + i % 2][:, 0:w],
                                         bias[:, :, :].rearrange("p r c -> p (r c)")[:, BIAS_OFF[g]:BIAS_OFF[g] + w],
                                         1.0, 3e38, ALU.add, ALU.min, s_min[:, i:i + 1]).then_inc(masked, 1)

            def normalise_probs(s, g0):
                i = NG * s + g0
                dve.wait_ge(exp_done, i + 2)
                step(dve.reciprocal(s_inv[:, i:i + 2], s_sum[:, i:i + 2]))
                for g in (g0, g0 + 1):
                    t = probs[:, s % 2, TILE_OFF[g]:TILE_OFF[g] + TILE_W[g]]
                    dve.tensor_scalar(t, t, s_inv[:, NG * s + g:NG * s + g + 1], None, ALU.mult).then_inc(prob_done, 1)

            def take_pT(s, kg):
                i = NG * s + kg
                w = P * len(KG_GROUPS[kg])
                dve.wait_ge(pT_act, i + 1)
                dve.tensor_tensor(pT_lo[:, i % 2, 0:w], bank[4 + i % 2][:, 0:w], pT_hi[:, i % 2, 0:w].bitcast(F32),
                                  ALU.subtract).then_inc(pT_dve, 1)

            def z_arguments(h, i):
                if DVE_ARGS[i]:
                    operands_free(dve, h, i)
                    for dst, a, b in z_differences(h, i)[:DVE_ARGS[i]]:
                        dve.tensor_tensor(dst, a, b, ALU.subtract).then_inc(z_arg, 1)

            def z_products(h, i):
                t = z_turn(h, i)
                zk, zq = zz[:, t, 0, :], zz[:, t, 1, :]
                q, kf, kb = h_q[:, h % 2, :], h_key(h, 0), h_key(h, 1)
                if i == 0:
                    dve.wait_ge(*freed(UNIT[("hq", h, 1)]))
                if i == 6:
                    operands_free(dve, h, i)
                    dve.tensor_tensor(zk, kf, kb, ALU.add).then_inc(z_ready, 1)
                    return
                dve.wait_ge(z_exp, 8 * h + (i if i < 6 else i - 1) + 1)
                if i < 4:
                    kl, kr = halves(zk, LEVELS[i])
                    dve.tensor_tensor(kl, kl, halves(kf, LEVELS[i])[0], ALU.mult).then_inc(z_ready, 1)
                    dve.tensor_tensor(kr, kr, halves(kb, LEVELS[i])[1], ALU.mult).then_inc(z_ready, 1)
                    dve.tensor_tensor(zq, zq, q, ALU.mult).then_inc(z_ready, 1)
                elif i < 6:
                    dve.tensor_tensor(zk, zk, (kf, kb)[i - 4], ALU.mult).then_inc(z_ready, 1)
                    dve.tensor_tensor(zq, zq, q, ALU.mult).then_inc(z_ready, 1)
                elif i == 7:
                    dve.tensor_tensor(zz[:, t, :, :], zz[:, t, :, :], h_gates[:, h % 2, 2:4, :], ALU.mult).then_inc(z_ready, 1)
                else:
                    dve.tensor_tensor(zk, zk, q, ALU.mult).then_inc(z_ready, 1)
                    dve.tensor_tensor(zq, zq, q, ALU.mult).then_inc(z_ready, 1)

            def take_level(h, i):
                for cg in range(2):
                    n = 2 * (NLEV * h + i) + cg
                    dve.wait_ge(lev_done, n + 1)
                    if i == 0:
                        if h:
                            dve.wait_ge(o_done, 2 * h)
                    else:
                        dve.wait_ge(lev_taken, n - 1)
                    dve.copy_predicated(scores[:, 4 * cg:4 * cg + 4, :],
                                        hg_mask[:, i:i + 1, :].to_broadcast([P, 4, P]),
                                        bank[2 + cg][:, :].rearrange("p (c i) -> p c i", c=4)).then_inc(lev_taken, 1)

            def chain_states(h):
                dve.wait_ge(g_ready, h + 1)
                if h:
                    dve.wait_ge(o_done, 2 * h)
                for d in range(2):
                    for j in range(2):
                        chunks = (((0, 1, 2, 3), (4, 5, 6)), ((7, 6, 5, 4), (3, 2, 1)))[d][j]
                        dve.wait_ge(upd_done, 4 * h + 2 * d + j + 1)
                        for k, c in enumerate(chunks):
                            src = bank[4 + 2 * d + j][:, P * k:P * k + P]
                            dst = state[:, d, c - d, :]
                            if c == (0, 7)[d]:
                                ins = dve.tensor_copy(dst, src)
                            else:
                                last = state[:, d, c - 1 if d == 0 else c, :]
                                ins = dve.scalar_tensor_tensor(dst, last, g_chunk[:, d, c:c + 1], src, ALU.mult, ALU.add)
                            if k < len(chunks) - 1:
                                step(ins)
                        ins.then_inc(st_done, 1)
                        dve.wait_ge(st_done, 4 * h + 2 * d + j + 1)

            def head_result(h):
                for part in range(2):
                    n = 2 * h + part
                    dve.wait_ge(o_rs, n + 1)
                    dve.scalar_tensor_tensor(tmp[:, part, :], bank[6 + part][:, :], gnorm[:, 0:1],
                                             tmp[:, part, :], ALU.mult, ALU.mult).then_inc(o_norm, 1)
                for part in range(2):
                    n = 2 * h + part
                    dve.wait_ge(o_norm, n + 1)
                    y = mixer_tile(PAIRS + h)[:, 4 * part:4 * part + 4, :]
                    cols = slice(part * HALF, part * HALF + HALF)
                    dve.tensor_tensor(y, tmp[:, part, :].rearrange("p (c i) -> p c i", i=P),
                                      h_gate[:, cols].rearrange("p (c i) -> p c i", i=P), ALU.mult).then_inc(y_done, 1)

            def mixer_lo(b):
                for f in range(FBLK):
                    k = FBLK * b + f
                    dve.wait_ge(m_hi, k + 1)
                    hi, lo, src = acts[:, b % 2, 0, f, :], acts[:, b % 2, 1, f, :], mixer_tile(k)
                    if b >= 2:
                        hi, lo = (a.rearrange("p (c i) -> p c i", i=P) for a in (hi, lo))
                    dve.tensor_tensor(lo, src, hi.bitcast(F32), ALU.subtract).then_inc(m_lo, 1)

            dve.memset(eps_col[:, :], EPS).then_inc(ready_cols, 1)
            dve.memset(one_col[:, :], 1.0).then_inc(ready_cols, 1)
            for t in range(TT):
                if t == 4:
                    dve.wait_ge(norm_load, 16)
                    for n in range(KT):
                        take_uT(0, n)
                normalise_tokens(0, t)
            for n in range(FIRST_QK):
                value_lo(n)
                for i in UT_AFTER.get(n, ()):
                    take_uT(0, i)
                if n == 6:
                    dve.wait_ge(uT_done, 16)
                    dve.memset(q_tiles[:, 0, :, :, :, :].bitcast(F32), 0.0).then_inc(cleared, 1)
                if n == 8:
                    dve.memset(q_tiles[:, 1, :, :, :, :].bitcast(F32), 0.0).then_inc(cleared, 1)
            dve.wait_ge(mask_load, 48)
            dve.wait_ge(c_load, CONSTS)
            dve.tensor_tensor(lb[:, :, :], lb_raw[:, :, 1, :], lb_raw[:, :, 0, :], ALU.subtract).then_inc(lb_diff, 1)
            dve.wait_ge(lb_exp, 1)
            step(dve.tensor_scalar(lb[:, :, :], lb[:, :, :], BIG, 1.0, ALU.min, ALU.add))
            step(dve.reciprocal(lb[:, :, :], lb[:, :, :]))
            step(dve.tensor_scalar(lb_rest[:, :, :], lb[:, :, :], -1.0, 1.0, ALU.mult, ALU.add))
            step(dve.tensor_scalar(lb_neg[:, :, :], lb[:, :, :], 1.0, None, ALU.subtract))
            dve.tensor_scalar(qk_w[:, 0:1], qk_w[:, 0:1], -float(NA_DIM) ** -0.5, None, ALU.mult).then_inc(params, 1)
            dve.wait_ge(params, 1)
            for n in range(FIRST_QK, BEFORE - 2):
                qk_product(n)
                qk_lo(n)
            for s in range(-2, STEPS + 1):
                qk = BEFORE + s if -2 <= s <= 9 else None
                if 0 <= s < STEPS:
                    take_pT(s, 0)
                    take_pT(s, 1)
                if s - 1 >= -2 and s + 1 < STEPS:
                    normalise_probs(s + 1, 2)
                if -2 <= s - 1 <= 9:
                    qk_lo(BEFORE + s - 1)
                if qk is not None:
                    qk_product(qk)
                if s + 2 < STEPS:
                    build_bias(s + 2)
                if 0 <= s < STEPS:
                    take_pT(s, 2)
                    take_pT(s, 3)
                if s + 2 < STEPS:
                    for g in range(NG):
                        mask_scores(s + 2, g)
                    normalise_probs(s + 2, 0)
            hgrn_may_start(dve)
            for n in FIRST_HEAD:
                if UNITS[n][0] in ("ff", "fb"):
                    clamp_gate(n)
                    finish_gate(n)
            z_arguments(0, 0)
            z_arguments(0, 1)
            z_products(0, 0)
            last = []
            for h in range(HG_HEADS):
                for i in range(PIECES):
                    for n in last:
                        clamp_gate(n)
                    if i < NLEV and (h, i) != (0, 0):
                        take_level(h, i)
                    if after(h, i, 1)[0] < HG_HEADS:
                        z_products(*after(h, i, 1))
                    if (h, i) == (0, 0):
                        take_level(h, i)
                    if i == 7:
                        chain_states(h)
                    if after(h, i, 2)[0] < HG_HEADS:
                        z_arguments(*after(h, i, 2))
                    for n in last:
                        finish_gate(n)
                    if h and i == RESULT_AT[h - 1]:
                        head_result(h - 1)
                    last = HEAD_UNITS[h][i]
            for n in last:
                clamp_gate(n)
            mixer_lo(0)
            for n in last:
                finish_gate(n)
            head_result(HG_HEADS - 1)
            def add_bank(i, bank0):
                t, half = divmod(i, 2)
                r = resid[:, t, half * HALF:half * HALF + HALF]
                dve.tensor_tensor(r, r, out_bank(i, bank0)[:, :], ALU.add).then_inc(added, 1)

            for b in range(OUT_BLOCKS):
                for i in range(2 * TT):
                    if b == 0 and i % 2 == 0:
                        dve.wait_ge(resid_load[i // 2], 16)
                    if b + 1 < OUT_BLOCKS and i == 8:
                        mixer_lo(b + 1)
                    dve.wait_ge(down_done, 16 * b + i + 1)
                    if b:
                        dve.wait_ge(added, 16 * (b - 1) + i + 1)
                    add_bank(i, 0)
                    if b == OUT_BLOCKS - 1 and i >= 3 and i % 2 and i < 2 * TT - 1:
                        normalise_tokens(1, (i - 3) // 2)
                    if b == OUT_BLOCKS - 1 and i >= 11:
                        take_uT(1, i - 11)
            for n in range(5, KT):
                take_uT(1, n)
            for t in range(TT - 2, TT):
                normalise_tokens(1, t)

            def activations(r, j, spread=()):
                for i, (f, half) in enumerate(up_order(j)):
                    cols = slice(half * HALF, half * HALF + HALF)
                    relu, a = u_tok[:, i, 0:HALF], u_tok[:, i, HALF:D]
                    for n in (spread[i] if spread else ()):
                        take_uT(1, n)
                    dve.wait_ge(relu_done, count(r, 8, 4 * j + i + 1))
                    dve.tensor_tensor(a, relu, relu, ALU.mult).then_inc(sqr_done, 1)
                    dve.wait_ge(sqr_done, count(r, 8, 4 * j + i + 1))
                    dve.wait_ge(a_hi, count(r, 8, 4 * j + i + 1))
                    dve.tensor_tensor(acts[:, j % 2, 1, f, cols], a, acts[:, j % 2, 0, f, cols].bitcast(F32),
                                      ALU.subtract).then_inc(a_lo, 1)

            def add_block(r, j):
                for i in range(2 * TT):
                    dve.wait_ge(down_done, count(r, 32, 16 * (OUT_BLOCKS + j) + i + 1))
                    dve.wait_ge(added, count(r, 32, 16 * (OUT_BLOCKS + j - 1) + i + 1))
                    add_bank(i, 4)

            activations(None, 0, UT_TAKEN)
            with dve.Fori(0, MLP_TURNS, 1) as r:
                activations(r, 1)
                add_block(r, 0)
                activations(r, 2)
                add_block(r, 1)
            activations(None, LAST)
            add_block(None, LAST - 1)
            add_block(None, LAST)

        @block.tensor
        def _(pe):
            def product(dst, a, b, first=True, last=True, skip=False):
                pe.matmul(dst, a[0], b[0], start=first, stop=False, skip_group_check=skip)
                pe.matmul(dst, a[0], b[1], start=False, stop=False, skip_group_check=skip)
                return pe.matmul(dst, a[1], b[0], start=False, stop=last, skip_group_check=skip)

            ring = (w_hi, w_lo)
            uT = (uT_hi, uT_lo)

            def transpose_tokens(norm, n):
                k, half = n % KT, n // KT
                src = (x_tok, u_tok)[norm]
                b = uT_bank(n)
                if n >= 4:
                    pe.wait_ge(uT_dve, 16 * norm + n - 3)
                pe.wait_ge(u_ready, TT * norm + 4 * half + 4)
                for t in range(4):
                    ins = pe.transpose(b[:, P * t:P * t + P], src[:, 4 * half + t, P * k:P * k + P], ident)
                ins.then_inc(uT_done, 1)

            def projection(n, ks=range(KT)):
                kind, what, part = UNITS[n]
                if n >= 2 and ks[0] == 0:
                    pe.wait_ge(*freed(n - 2))
                b = bank[n % 2]
                done = 0
                if n:
                    k1, _, p1 = UNITS[n - 1]
                    done = 2 * (p1 == TT - 1) if k1 in ("v", "hv") else int(p1 == 1)
                if kind in ("v", "hv"):
                    tile = TILE_OF[("in", (C_V if kind == "v" else C_HV) + 256 * what)]
                    pe.wait_ge(w_split, 2 * (tile + 2))
                    pe.wait_ge(uT_dve, 8 if part < 4 else 16)
                    r = tile % RING
                    for k in ks:
                        a = [t[:, k, P * part:P * part + P] for t in uT]
                        w = [t[:, r:r + 2, P * k:P * k + P] for t in ring]
                        dst = b[:, 0:256]
                        first = pe.matmul(dst, a[0], w[0], start=k == 0, stop=False)
                        if k == 0 and done:
                            first.then_inc(w_used, done)
                        pe.matmul(dst, a[0], w[1], start=False, stop=False)
                        ins = pe.matmul(dst, a[1], w[0], start=False, stop=k == KT - 1)
                else:
                    tile = TILE_OF[("in", COL[kind] + P * what)]
                    pe.wait_ge(w_split, 2 * (tile + 1))
                    pe.wait_ge(uT_dve, 16)
                    r = tile % RING
                    for k in ks:
                        w = [t[:, r, P * k:P * k + P] for t in ring]
                        u = [t[:, k, part * HALF:part * HALF + HALF] for t in uT]
                        first = pe.matmul(b[:, :], w[0], u[0], start=k == 0, stop=False)
                        if k == 0 and done:
                            first.then_inc(w_used, done)
                        pe.matmul(b[:, :], w[0], u[1], start=False, stop=False)
                        ins = pe.matmul(b[:, :], w[1], u[0], start=False, stop=k == KT - 1)
                if ks[-1] == KT - 1:
                    ins.then_inc(proj_done, 1)

            def take_steps(steps):
                for n in sorted({n for n, _ in steps}):
                    projection(n, [k for m, k in steps if m == n])

            def qk_average(n):
                pe.wait_ge(qk_sq, n - FIRST_QK + 1)
                if n > FIRST_QK:
                    pe.wait_ge(unit_act, act_hands(n - 1) + 1)
                pe.matmul(bank[7][:, :], head_mean, qk_t[:, 0, :], start=True, stop=True).then_inc(qk_mean, 1)

            def score_tiles(s, groups):
                p, n = divmod(s, NB)
                if s >= STEPS:
                    return
                pe.wait_ge(qk_ready, qk_count(UNIT[("k", p, 1)]))
                for g in groups:
                    i = NG * s + g
                    if i >= 2:
                        pe.wait_ge(masked, i - 1)
                    rows = slice(KEY_ROW0[g], KEY_ROW0[g] + KEY_ROWS[g])
                    cols = slice(BAND_START[n], BAND_START[n] + BAND)
                    keys = [t[:, p % 2, :].rearrange("p (r c) -> p r c", c=GRID)[:, rows, cols] for t in (k_hi, k_lo)]
                    product(bank[2 + i % 2][:, 0:TILE_W[g]], [q_tiles[:, p % 2, i_, g, n, :] for i_ in range(2)],
                            keys).then_inc(score_done, 1)

            def transpose_probs(s, kg):
                i = NG * s + kg
                pe.wait_ge(prob_done, NG * s + KG_GROUPS[kg][-1] + 1)
                if i >= 2:
                    pe.wait_ge(pT_dve, i - 1)
                for j, g in enumerate(KG_GROUPS[kg]):
                    at = TILE_OFF[g] + P * (kg - KG0[g])
                    ins = pe.transpose(bank[4 + i % 2][:, P * j:P * j + P], probs[:, s % 2, at:at + P], ident)
                ins.then_inc(pT_done, 1)

            def times_values(s, kg):
                i = NG * s + kg
                g0, w = KG_GROUPS[kg][0], P * len(KG_GROUPS[kg])
                pe.wait_ge(pT_dve, i + 1)
                if kg == 0:
                    pe.wait_ge(v_load[s % 2], 16 * 8 * (s // 2 + 1))
                    if s:
                        pe.wait_ge(mix_done, 2 * s)
                product(bank[6][:, P * g0:P * g0 + w], [t[:, s % 2, kg, :] for t in (v_hi, v_lo)],
                        [t[:, i % 2, 0:w] for t in (pT_hi, pT_lo)], first=kg == 0, last=kg == NG - 1,
                        skip=True).then_inc(pv_done, 1)

            def chunk(t, c):
                return t[:, P * c:P * c + P]

            def level(h, i):
                t = z_turn(h, i)
                pe.wait_ge(z_ready, steps_to(PRODUCT_STEPS, h, i))
                for cg in range(2):
                    n = 2 * (NLEV * h + i) + cg
                    if n >= 2:
                        pe.wait_ge(lev_taken, n - 1)
                    else:
                        pe.wait_ge(masked, NG * STEPS)
                    for c in range(4 * cg, 4 * cg + 4):
                        q = h_q[:, h % 2, :] if i == 6 else zz[:, t, 1, :]
                        ins = pe.matmul(bank[2 + cg][:, P * (c % 4):P * (c % 4) + P], chunk(zz[:, t, 0, :], c),
                                        chunk(q, c), start=True, stop=True)
                    ins.then_inc(lev_done, 1)

            def chunk_products(h, share):
                t = z_turn(h, 7)
                pe.wait_ge(z_ready, steps_to(PRODUCT_STEPS, h, 7))
                for d in range(2):
                    if h:
                        pe.wait_ge(*((o_rs, 2 * h), (o_norm, 2 * h))[d])
                    elif d == 0:
                        pe.wait_ge(pT_dve, NG * STEPS)
                    else:
                        pe.wait_ge(mix_done, 2 * STEPS)
                        pe.wait_ge(unit_act, act_hands(UNIT[("hv", 0, 0)]))
                    for cg in range(2):
                        for c in range(4 * cg, 4 * cg + 4):
                            ins = pe.transpose(bank[4 + 2 * d + cg][:, P * (c % 4):P * (c % 4) + P],
                                               chunk(zz[:, t, d, :], c), ident)
                        ins.then_inc(kT_done, 1)
                for d in range(2):
                    share(2 * d)
                    pe.wait_ge(kT_act, 4 * h + 2 * d + 2)
                    for j in range(2):
                        for k, c in enumerate((((0, 1, 2, 3), (4, 5, 6)), ((7, 6, 5, 4), (3, 2, 1)))[d][j]):
                            ins = pe.matmul(bank[4 + 2 * d + j][:, P * k:P * k + P], chunk(k_tok, c),
                                            h_v[:, c, P * h:P * h + P], start=True, stop=True)
                        ins.then_inc(upd_done, 1)
                    share(2 * d + 1)

            def head_outputs(h):
                t = z_turn(h, 8)
                pe.wait_ge(z_ready, steps_to(PRODUCT_STEPS, h, 8))
                pe.wait_ge(st_done, 4 * (h + 1))
                pe.wait_ge(lev_taken, 2 * NLEV * (h + 1))
                for part in range(2):
                    for c in range(4 * part, 4 * part + 4):
                        dst = bank[6 + part][:, P * (c % 4):P * (c % 4) + P]
                        pe.matmul(dst, h_v[:, c, P * h:P * h + P], scores[:, c, :], start=True, stop=False)
                        if c >= 1:
                            ins = pe.matmul(dst, state[:, 0, c - 1, :], chunk(zz[:, t, 0, :], c), start=False, stop=c == 7)
                        if c <= 6:
                            ins = pe.matmul(dst, state[:, 1, c, :], chunk(zz[:, t, 1, :], c), start=False, stop=True)
                    ins.then_inc(o_done, 1)

            def head_means(h):
                for part in range(2):
                    pe.wait_ge(o_sq, 2 * h + part + 1)
                    pe.matmul(bank[4 + part][:, :], all_mean, tmp[:, part, :], start=True, stop=True).then_inc(o_mean, 1)

            pe.wait_ge(tab_load, 16)
            for n in range(KT):
                transpose_tokens(0, n)
            for n in range(FIRST_QK + 1):
                projection(n)
                for i in UT_AFTER.get(n, ()):
                    transpose_tokens(0, i)
            for n in range(FIRST_QK + 1, BEFORE - 1):
                projection(n, range(2))
                qk_average(n - 1)
                projection(n, range(2, KT))
            for s in range(-2, STEPS):
                def share(i):
                    if s in STEP_UNIT:
                        projection(STEP_UNIT[s], range(2 * i, 2 * i + 2))
                    for j in VALUE_UNITS.get(s, ())[i:i + 1]:
                        projection(UNIT[("hv", 0, 0)] + j)

                if s >= 0:
                    transpose_probs(s, 0)
                    transpose_probs(s, 1)
                share(0)
                if -2 <= s <= 9:
                    qk_average(BEFORE + s)
                if s >= 0:
                    times_values(s, 0)
                    transpose_probs(s, 2)
                share(1)
                if s >= 0:
                    times_values(s, 1)
                    transpose_probs(s, 3)
                score_tiles(s + 2, (0, 1))
                share(2)
                if s >= 0:
                    times_values(s, 2)
                score_tiles(s + 2, (2,))
                share(3)
                if s >= 0:
                    times_values(s, 3)
                score_tiles(s + 2, (3,))
            for n in FIRST_HEAD:
                projection(n)
            for h in range(HG_HEADS):
                for i in range(PIECES):
                    steps = UNIT_STEPS[h][i]
                    if (h, i) == (0, 0):
                        take_steps(steps)
                        level(h, i)
                    elif i < NLEV:
                        level(h, i)
                        if i == 0:
                            head_means(h - 1)
                        take_steps(steps)
                    elif i == 7:
                        chunk_products(h, lambda q: take_steps(steps[len(steps) * q // 4:len(steps) * (q + 1) // 4]))
                    else:
                        take_steps(steps)
                        head_outputs(h)

            def add_product(i, turn, place, bank0, finished, free):
                t, half = divmod(i, 2)
                pe.wait_ge(added, free)
                dst = out_bank(i, bank0)[:, :]
                for f in range(FBLK):
                    a = [acts[:, turn, x_, f, P * t:P * t + P] for x_ in range(2)]
                    w = [x_[:, place + f, half * HALF:half * HALF + HALF] for x_ in ring]
                    first = pe.matmul(dst, a[0], w[0], start=f == 0, stop=False)
                    if f == 0 and finished:
                        first.then_inc(w_used, finished)
                    pe.matmul(dst, a[0], w[1], start=False, stop=False)
                    ins = pe.matmul(dst, a[1], w[0], start=False, stop=f == FBLK - 1)
                ins.then_inc(down_done, 1)

            for b in range(OUT_BLOCKS):
                pe.wait_ge(w_split, 2 * (N_IN + FBLK * (b + 1)))
                pe.wait_ge(m_lo, FBLK * (b + 1))
                for i in range(2 * TT):
                    if b == 0 and i == 2:
                        pe.wait_ge(*freed(len(UNITS) - 1))
                    if b == 0 and i == 1:
                        head_means(HG_HEADS - 1)
                    add_product(i, b % 2, FBLK * b % RING, 0, (1 if b == 0 else FBLK) if i == 0 else 0,
                                max(16 * b + i - 3, 0))
                    if b == OUT_BLOCKS - 1 and i >= 10:
                        transpose_tokens(1, i - 10)
            transpose_tokens(1, 6)
            transpose_tokens(1, 7)

            def up(r, j, spread=None):
                place = 2 if j else 0
                for i, (f, half) in enumerate(up_order(j)):
                    if j:
                        pe.wait_ge(relu_done, count(r, 8, 4 * j))
                        pe.wait_ge(w_split, count(r, 16, 2 * (len(TILES) + 4 * j - 2 + f + 1)))
                    else:
                        pe.wait_ge(added, 16 * OUT_BLOCKS)
                        pe.wait_ge(w_split, 2 * (len(TILES) + f + 1))
                        pe.wait_ge(uT_dve, 16 + (8 if half == 0 else 16))
                    dst = bank[2 * f + half][:, :]
                    for k in range(KT):
                        w = [t[:, place + f, P * k:P * k + P] for t in ring]
                        u = [t[:, k, half * HALF:half * HALF + HALF] for t in uT]
                        first = pe.matmul(dst, w[0], u[0], start=k == 0, stop=False)
                        if k == 0 and i == 0:
                            first.then_inc(w_used, FBLK)
                        if k == 0 and j and (f, half) == (1, 0):
                            first.then_inc(w_used, 1)
                        pe.matmul(dst, w[0], u[1], start=False, stop=False)
                        ins = pe.matmul(dst, w[1], u[0], start=False, stop=k == KT - 1)
                        if not j:
                            for n in UT_SPREAD.get((i, k), ()):
                                transpose_tokens(1, n)
                    ins.then_inc(up_done, 1)

            def down(r, j):
                last = r is None and j == LAST
                pe.wait_ge(a_lo, count(r, 8, 4 * (j + 1)))
                pe.wait_ge(w_split, count(r, 16, 2 * (len(TILES) + 4 * j + (4 if last else 6))))
                for i in range(2 * TT):
                    add_product(i, j % 2, 2 if last else 0, 4, 1 if i == 0 else 0,
                                count(r, 32, 16 * (OUT_BLOCKS + j) + i - 3))

            up(None, 0)
            with pe.Fori(0, MLP_TURNS, 1) as r:
                up(r, 1)
                down(r, 0)
                up(r, 2)
                down(r, 1)
            up(None, LAST)
            down(None, LAST - 1)
            down(None, LAST)


_INS = ["x", "w_in", "w_out", "attn_norm_w", "mlp_norm_w", "q_norm_w", "k_norm_w", "rpb", "hg_norm_w",
        "lb_fwd", "lb_bwd", "w_up", "w_down"]


def kernel(**inputs):
    import numpy as _np
    import concourse.bacc as _bacc
    from concourse import mybir as _mybir
    from concourse.bass_utils import run_bass_kernel_spmd as _run

    nc = _bacc.Bacc("TRN2", target_bir_lowering=False, num_devices=1)
    data = {name: _np.ascontiguousarray(inputs[name]) for name in _INS}
    rpb = _np.zeros((NA_HEADS, 16, 15, RPB_PITCH), data["rpb"].dtype)
    for c in range(16):
        rpb[:, c, :, 1 + c:32 + c] = data["rpb"][0]
    data["rpb"] = rpb
    data["tables"], data["masks"] = shape_tables()
    arrays, args = {}, []
    for name, a in data.items():
        arrays[f"in_{name}"] = a
        args.append(nc.dram_tensor(f"in_{name}", a.shape, _mybir.dt.from_np(a.dtype), kind="ExternalInput").ap())
    out = nc.dram_tensor("out_0", (1, S, D), F32, kind="ExternalOutput").ap()
    hybrid_block(nc, *args, out)
    r = _run(nc, [arrays], core_ids=[0])
    return r.results[0]["out_0"]
```
